# Optimizing a Trainium2 kernel written in Bass

```python
import math
import jax
import jax.numpy as jnp
from jax import lax
import numpy as np
import jax, jax.numpy as jnp

D_MODEL = 1024
BATCH = 1
SEQ = 512
DEPTH = 1

D_MIX = D_MODEL
DA_HEADS = 4
DA_HEAD_DIM = 64
DA_VAL_DIM = 2 * DA_HEAD_DIM
DA_QK = DA_HEADS * 2 * DA_HEAD_DIM
DA_WIDTH = DA_HEADS * DA_VAL_DIM
ML_HEADS = 4
ML_HEAD_DIM = (D_MIX - DA_WIDTH) // ML_HEADS
ML_WIDTH = ML_HEADS * ML_HEAD_DIM
ML_CONV = 4
ML_CHUNK = 64
IN_SPLITS = (DA_QK, DA_QK, DA_WIDTH, ML_WIDTH, ML_WIDTH, ML_WIDTH, ML_WIDTH, ML_HEADS, ML_HEADS)
N_IN = sum(IN_SPLITS)
MEM_LEN = 256
X_HEADS = 4
X_HEAD_DIM = D_MODEL // X_HEADS
N_GROUPS = 4
EXPERTS_PER_GROUP = 8
N_EXPERTS = N_GROUPS * EXPERTS_PER_GROUP
TOP_K = 2
D_EXPERT = 512
MOE_BLOCK = 128
Q_BLOCK = 128
ROPE_THETA = 10000.0
EPS = 1e-6


def rms_norm(x, g):
    xf = x.astype(jnp.float32)
    y = xf * lax.rsqrt(jnp.mean(xf * xf, axis=-1, keepdims=True) + EPS)
    return (y * g.astype(jnp.float32)).astype(x.dtype)

def rotary(t, pos):
    d = t.shape[-1]
    inv_freq = ROPE_THETA ** (-jnp.arange(0, d, 2, dtype=jnp.float32) / d)
    ang = pos.astype(jnp.float32)[:, None] * inv_freq[None, :]
    cos = jnp.cos(ang).astype(t.dtype)
    sin = jnp.sin(ang).astype(t.dtype)
    t1, t2 = t[..., : d // 2], t[..., d // 2:]
    return jnp.concatenate([t1 * cos - t2 * sin, t2 * cos + t1 * sin], axis=-1)

def diff_attention(q, k, v, lam, subln_g, lam_init):
    bsz, seq = q.shape[0], q.shape[1]
    pos = jnp.arange(seq)
    q = rotary(q.transpose(0, 2, 3, 1, 4), pos) * (DA_HEAD_DIM ** -0.5)
    k = rotary(k.transpose(0, 2, 3, 1, 4), pos)
    v = v.transpose(0, 2, 1, 3)
    n_blk = seq // Q_BLOCK
    q_blocks = q.reshape(bsz, DA_HEADS, 2, n_blk, Q_BLOCK, DA_HEAD_DIM).transpose(3, 0, 1, 2, 4, 5)
    k_pos = jnp.arange(seq)

    def one_block(args):
        q_blk, start = args
        s = jnp.einsum('bhmqd,bhmkd->bhmqk', q_blk, k).astype(jnp.float32)
        q_pos = start + jnp.arange(Q_BLOCK)
        causal = k_pos[None, :] <= q_pos[:, None]
        p = jax.nn.softmax(jnp.where(causal, s, -jnp.inf), axis=-1)
        a = p[:, :, 0] - lam * p[:, :, 1]
        return jnp.einsum('bhqk,bhkd->bhqd', a.astype(v.dtype), v)

    o = lax.map(one_block, (q_blocks, jnp.arange(n_blk) * Q_BLOCK))
    o = o.transpose(1, 0, 3, 2, 4).reshape(bsz, seq, DA_HEADS, DA_VAL_DIM)
    o = rms_norm(o, subln_g) * (1.0 - lam_init)
    return o.reshape(bsz, seq, DA_WIDTH)

def causal_depthwise_conv(u, w, b):
    c = u.shape[-1]
    y = lax.conv_general_dilated(u, w.astype(u.dtype), window_strides=(1,),
                                 padding=[(ML_CONV - 1, 0)],
                                 dimension_numbers=('NWC', 'WIO', 'NWC'),
                                 feature_group_count=c)
    return y + b.astype(u.dtype)

def mlstm_chunkwise(q, k, v, o_pre, i_pre, f_pre, norm_g):
    f32 = jnp.float32
    bsz, seq = q.shape[0], q.shape[1]
    n_ch = seq // ML_CHUNK

    def heads(t):
        return t.astype(f32).reshape(bsz, n_ch, ML_CHUNK, ML_HEADS, ML_HEAD_DIM).transpose(1, 0, 3, 2, 4)

    def gates(t):
        return t.astype(f32).reshape(bsz, n_ch, ML_CHUNK, ML_HEADS).transpose(1, 0, 3, 2)

    qc, kc, vc = heads(q), heads(k) * (ML_HEAD_DIM ** -0.5), heads(v)
    ic = gates(i_pre)
    lfc = jax.nn.log_sigmoid(gates(f_pre))
    tri = jnp.tril(jnp.ones((ML_CHUNK, ML_CHUNK), dtype=bool))

    def step(carry, xs):
        c_mat, n_vec, m_prev = carry
        qj, ks, vs, ig, lf = xs
        a = jnp.cumsum(lf, axis=-1)
        log_d = jnp.where(tri, a[..., :, None] - a[..., None, :] + ig[..., None, :], -jnp.inf)
        log_inter = a + m_prev[..., None]
        m_row = jnp.maximum(log_inter, jnp.max(log_d, axis=-1))
        w_intra = jnp.exp(log_d - m_row[..., None])
        w_inter = jnp.exp(log_inter - m_row)
        s = jnp.einsum('bhjd,bhsd->bhjs', qj, ks) * w_intra
        num = (w_inter[..., None] * jnp.einsum('bhjd,bhde->bhje', qj, c_mat)
               + jnp.einsum('bhjs,bhse->bhje', s, vs))
        den = w_inter * jnp.einsum('bhjd,bhd->bhj', qj, n_vec) + jnp.sum(s, axis=-1)
        h = num / jnp.maximum(jnp.abs(den), jnp.exp(-m_row))[..., None]
        g = a[..., -1]
        log_w = g[..., None] - a + ig
        m_new = jnp.maximum(g + m_prev, jnp.max(log_w, axis=-1))
        w_state = jnp.exp(log_w - m_new[..., None])
        decay = jnp.exp(g + m_prev - m_new)
        c_new = decay[..., None, None] * c_mat + jnp.einsum('bhs,bhsd,bhse->bhde', w_state, ks, vs)
        n_new = decay[..., None] * n_vec + jnp.einsum('bhs,bhsd->bhd', w_state, ks)
        return (c_new, n_new, m_new), h

    init = (jnp.zeros((bsz, ML_HEADS, ML_HEAD_DIM, ML_HEAD_DIM), f32),
            jnp.zeros((bsz, ML_HEADS, ML_HEAD_DIM), f32),
            jnp.zeros((bsz, ML_HEADS), f32))
    _, h = lax.scan(step, init, (qc, kc, vc, ic, lfc))
    h = h.transpose(1, 0, 3, 2, 4).reshape(bsz, seq, ML_HEADS, ML_HEAD_DIM)
    mu = jnp.mean(h, axis=-1, keepdims=True)
    var = jnp.mean(jnp.square(h - mu), axis=-1, keepdims=True)
    hn = (h - mu) * lax.rsqrt(var + EPS) * norm_g.astype(f32).reshape(ML_HEADS, ML_HEAD_DIM)
    o = jax.nn.sigmoid(o_pre.astype(f32)).reshape(bsz, seq, ML_HEADS, ML_HEAD_DIM)
    return (o * hn).reshape(bsz, seq, ML_WIDTH).astype(q.dtype)

def hybrid_mixer(h, w_in, w_out, da_lambda, da_subln_g, lam_init, ml_conv_w, ml_conv_b, ml_gate_b, ml_norm_g):
    bsz, seq = h.shape[0], h.shape[1]
    proj = h @ w_in
    dq, dk, dv, mq, mk, mv, mo, mi, mf = jnp.split(proj, np.cumsum(IN_SPLITS)[:-1].tolist(), axis=-1)
    lv = da_lambda.astype(jnp.float32)
    lam = jnp.exp(jnp.sum(lv[0] * lv[1])) - jnp.exp(jnp.sum(lv[2] * lv[3])) + lam_init
    y_da = diff_attention(dq.reshape(bsz, seq, DA_HEADS, 2, DA_HEAD_DIM),
                          dk.reshape(bsz, seq, DA_HEADS, 2, DA_HEAD_DIM),
                          dv.reshape(bsz, seq, DA_HEADS, DA_VAL_DIM), lam, da_subln_g, lam_init)
    qk = jax.nn.silu(causal_depthwise_conv(jnp.concatenate([mq, mk], axis=-1), ml_conv_w, ml_conv_b))
    mq_c, mk_c = jnp.split(qk, 2, axis=-1)
    y_ml = mlstm_chunkwise(mq_c, mk_c, mv, mo,
                           mi + ml_gate_b[0].astype(mi.dtype), mf + ml_gate_b[1].astype(mf.dtype), ml_norm_g)
    return jnp.concatenate([y_da, y_ml], axis=-1) @ w_out

def cross_attention(h, mem_n, wq, wk, wv, wo):
    bsz, seq = h.shape[0], h.shape[1]
    m_len = mem_n.shape[1]
    q = (h @ wq).reshape(bsz, seq, X_HEADS, X_HEAD_DIM)
    k = (mem_n @ wk).reshape(bsz, m_len, X_HEADS, X_HEAD_DIM)
    v = (mem_n @ wv).reshape(bsz, m_len, X_HEADS, X_HEAD_DIM)
    s = jnp.einsum('bqhd,bkhd->bhqk', q, k).astype(jnp.float32) * (X_HEAD_DIM ** -0.5)
    p = jax.nn.softmax(s, axis=-1)
    o = jnp.einsum('bhqk,bkhd->bqhd', p.astype(v.dtype), v).reshape(bsz, seq, D_MODEL)
    return o @ wo

def hierarchical_moe(h, w_rg, b_rg, w_re, b_re, w1, w3, w2):
    f32 = jnp.float32
    bsz, seq, d = h.shape
    n_tok = bsz * seq
    xt = h.reshape(n_tok, d)
    g_prob = jax.nn.softmax((xt @ w_rg).astype(f32) + b_rg.astype(f32), axis=-1)
    g_idx = jnp.argmax(g_prob, axis=-1).astype(jnp.int32)
    g_w = jnp.take_along_axis(g_prob, g_idx[:, None], axis=-1)[:, 0]
    e_logits = ((xt @ w_re).astype(f32) + b_re.astype(f32)).reshape(n_tok, N_GROUPS, EXPERTS_PER_GROUP)
    e_logits = jnp.take_along_axis(e_logits, g_idx[:, None, None], axis=1)[:, 0]
    top_p, top_i = lax.top_k(jax.nn.softmax(e_logits, axis=-1), TOP_K)
    comb = g_w[:, None] * top_p / jnp.sum(top_p, axis=-1, keepdims=True)
    expert = g_idx[:, None] * EXPERTS_PER_GROUP + top_i.astype(jnp.int32)
    n_asg = n_tok * TOP_K
    flat_e = expert.reshape(-1)
    flat_tok = jnp.repeat(jnp.arange(n_tok, dtype=jnp.int32), TOP_K)
    flat_w = comb.reshape(-1)
    order = jnp.argsort(flat_e)
    sorted_e, sorted_tok, sorted_w = flat_e[order], flat_tok[order], flat_w[order]
    counts = jnp.bincount(flat_e, length=N_EXPERTS).astype(jnp.int32)
    padded = (counts + MOE_BLOCK - 1) // MOE_BLOCK * MOE_BLOCK
    starts = jnp.cumsum(counts) - counts
    pad_ends = jnp.cumsum(padded)
    pad_starts = pad_ends - padded
    dest = pad_starts[sorted_e] + jnp.arange(n_asg, dtype=jnp.int32) - starts[sorted_e]
    n_blocks = -(-n_asg // MOE_BLOCK) + N_EXPERTS
    n_rows = n_blocks * MOE_BLOCK
    buf_tok = jnp.full((n_rows,), n_tok, jnp.int32).at[dest].set(sorted_tok)
    buf_w = jnp.zeros((n_rows,), f32).at[dest].set(sorted_w)
    block_e = jnp.clip(jnp.searchsorted(pad_ends, jnp.arange(n_blocks, dtype=jnp.int32) * MOE_BLOCK, side='right'),
                       0, N_EXPERTS - 1).astype(jnp.int32)
    xpad = jnp.concatenate([xt, jnp.zeros((1, d), xt.dtype)], axis=0)
    xb = xpad[buf_tok].reshape(n_blocks, MOE_BLOCK, d)

    def run_block(args):
        x_blk, e = args
        return (jax.nn.silu(x_blk @ w1[e]) * (x_blk @ w3[e])) @ w2[e]

    yb = lax.map(run_block, (xb, block_e)).reshape(n_rows, d)
    yb = yb * buf_w[:, None].astype(yb.dtype)
    out = jnp.zeros((n_tok + 1, d), yb.dtype).at[buf_tok].add(yb)[:n_tok]
    return out.reshape(bsz, seq, d)

def first_inputs(seed: int = 0) -> dict:
    key = jax.random.key(seed)
    ks = jax.random.split(key, 32)
    f32 = jnp.float32
    L = DEPTH

    def nrm(k, shape, scale):
        return jax.random.normal(k, shape, f32) * scale

    def gain(k, shape):
        return 1.0 + 0.02 * jax.random.normal(k, shape, f32)

    f_bias = jnp.linspace(3.0, 6.0, ML_HEADS, dtype=f32)
    ml_gate_b = jnp.stack([nrm(ks[9], (L, ML_HEADS), 0.1),
                           f_bias[None, :] + nrm(ks[10], (L, ML_HEADS), 0.1)], axis=1)
    return {
        'x': nrm(ks[0], (BATCH, SEQ, D_MODEL), 1.0),
        'mem': nrm(ks[1], (BATCH, MEM_LEN, D_MODEL), 1.0),
        'norm_mix_g': gain(ks[2], (L, D_MODEL)),
        'w_in': nrm(ks[3], (L, D_MODEL, N_IN), D_MODEL ** -0.5),
        'w_out': nrm(ks[4], (L, D_MIX, D_MODEL), D_MIX ** -0.5),
        'da_lambda': nrm(ks[5], (L, 4, DA_HEAD_DIM), 0.1),
        'da_subln_g': gain(ks[6], (L, DA_VAL_DIM)),
        'ml_conv_w': nrm(ks[7], (L, ML_CONV, 1, 2 * ML_WIDTH), ML_CONV ** -0.5),
        'ml_conv_b': nrm(ks[8], (L, 2 * ML_WIDTH), 0.02),
        'ml_gate_b': ml_gate_b,
        'ml_norm_g': gain(ks[11], (L, ML_WIDTH)),
        'norm_x_g': gain(ks[12], (L, D_MODEL)),
        'norm_mem_g': gain(ks[13], (L, D_MODEL)),
        'w_xq': nrm(ks[14], (L, D_MODEL, D_MODEL), D_MODEL ** -0.5),
        'w_xk': nrm(ks[15], (L, D_MODEL, D_MODEL), D_MODEL ** -0.5),
        'w_xv': nrm(ks[16], (L, D_MODEL, D_MODEL), D_MODEL ** -0.5),
        'w_xo': nrm(ks[17], (L, D_MODEL, D_MODEL), D_MODEL ** -0.5),
        'norm_ffn_g': gain(ks[18], (L, D_MODEL)),
        'w_router_group': nrm(ks[19], (L, D_MODEL, N_GROUPS), D_MODEL ** -0.5),
        'b_router_group': nrm(ks[20], (L, N_GROUPS), 0.01),
        'w_router_expert': nrm(ks[21], (L, D_MODEL, N_EXPERTS), D_MODEL ** -0.5),
        'b_router_expert': nrm(ks[22], (L, N_EXPERTS), 0.01),
        'w1': nrm(ks[23], (L, N_EXPERTS, D_MODEL, D_EXPERT), D_MODEL ** -0.5),
        'w3': nrm(ks[24], (L, N_EXPERTS, D_MODEL, D_EXPERT), D_MODEL ** -0.5),
        'w2': nrm(ks[25], (L, N_EXPERTS, D_EXPERT, D_MODEL), D_EXPERT ** -0.5),
        'norm_final_g': gain(ks[26], (D_MODEL,)),
    }

def first_block(x, mem, norm_mix_g, w_in, w_out, da_lambda, da_subln_g, ml_conv_w, ml_conv_b, ml_gate_b,
              ml_norm_g, norm_x_g, norm_mem_g, w_xq, w_xk, w_xv, w_xo, norm_ffn_g, w_router_group,
              b_router_group, w_router_expert, b_router_expert, w1, w3, w2, norm_final_g):
    for l in range(DEPTH):
        lam_init = 0.8 - 0.6 * math.exp(-0.3 * l)
        x = x + hybrid_mixer(rms_norm(x, norm_mix_g[l]), w_in[l], w_out[l], da_lambda[l], da_subln_g[l],
                             lam_init, ml_conv_w[l], ml_conv_b[l], ml_gate_b[l], ml_norm_g[l])
        x = x + cross_attention(rms_norm(x, norm_x_g[l]), rms_norm(mem, norm_mem_g[l]),
                                w_xq[l], w_xk[l], w_xv[l], w_xo[l])
        x = x + hierarchical_moe(rms_norm(x, norm_ffn_g[l]), w_router_group[l], b_router_group[l],
                                 w_router_expert[l], b_router_expert[l], w1[l], w3[l], w2[l])
    return rms_norm(x, norm_final_g)


DEPTH_2 = 2

N_A = DEPTH_2 // 2
N_B = DEPTH_2 - N_A

CONV_CH = D_MODEL
CONV_W = 3

HEAD_DIM = 64
N_HEADS = D_MODEL // HEAD_DIM
N_KV_HEADS = 4
GROUP = N_HEADS // N_KV_HEADS
WINDOW = 128
BLOCK = 128
ROT_DIM = HEAD_DIM // 4
ROPE_THETA_2 = 500000.0
NEG_INF = -1e30


def rmsnorm(x, g):
    xf = x.astype(jnp.float32)
    y = xf * lax.rsqrt(jnp.mean(xf * xf, axis=-1, keepdims=True) + EPS)
    return (y * g.astype(jnp.float32)).astype(x.dtype)

def rope_tables(seq):
    pos = jnp.arange(seq, dtype=jnp.float32)
    inv = ROPE_THETA_2 ** (-jnp.arange(0, ROT_DIM, 2, dtype=jnp.float32) / ROT_DIM)
    ang = pos[:, None] * inv[None, :]
    return jnp.cos(ang), jnp.sin(ang)

def partial_rope(t, cos, sin):
    tf = t.astype(jnp.float32)
    rot, rest = tf[..., :ROT_DIM], tf[..., ROT_DIM:]
    r1, r2 = rot[..., : ROT_DIM // 2], rot[..., ROT_DIM // 2:]
    c = cos[None, :, None, :]
    s = sin[None, :, None, :]
    out = jnp.concatenate([r1 * c - r2 * s, r2 * c + r1 * s, rest], axis=-1)
    return out.astype(t.dtype)

def short_conv_mixer(x, ln_g, w_in, conv_w, w_out):
    h = rmsnorm(x, ln_g)
    b_gate, c_gate, u, z = jnp.split(h @ w_in, 4, axis=-1)
    v = c_gate * u
    conv = lax.conv_general_dilated(
        v, conv_w.astype(v.dtype), window_strides=(1,), padding=[(CONV_W - 1, 0)],
        dimension_numbers=("NWC", "WIO", "NWC"), feature_group_count=CONV_CH)
    y = b_gate * conv * jax.nn.silu(z)
    return y @ w_out

def shared_kv(x, ln_g, w_kv, k_norm_g, cos, sin):
    bsz, seq, _ = x.shape
    nb = seq // BLOCK
    h = rmsnorm(x, ln_g)
    k, v = jnp.split(h @ w_kv, 2, axis=-1)
    k = k.reshape(bsz, seq, N_KV_HEADS, HEAD_DIM)
    v = v.reshape(bsz, seq, N_KV_HEADS, HEAD_DIM)
    k = partial_rope(rmsnorm(k, k_norm_g), cos, sin)

    def band(t):
        tb = t.reshape(bsz, nb, BLOCK, N_KV_HEADS, HEAD_DIM)
        prev = jnp.concatenate([jnp.zeros_like(tb[:, :1]), tb[:, :-1]], axis=1)
        tb = jnp.concatenate([prev, tb], axis=2)
        return jnp.moveaxis(tb, 1, 0)

    return band(k), band(v)

def swa_sink_mixer(x, ln_g, w_in, q_norm_g, sinks, w_out, k_band, v_band, cos, sin):
    bsz, seq, _ = x.shape
    nb = seq // BLOCK
    h = rmsnorm(x, ln_g)
    q, z = jnp.split(h @ w_in, 2, axis=-1)
    q = q.reshape(bsz, seq, N_HEADS, HEAD_DIM)
    q = partial_rope(rmsnorm(q, q_norm_g), cos, sin)
    q = q.reshape(bsz, nb, BLOCK, N_KV_HEADS, GROUP, HEAD_DIM)
    q = jnp.moveaxis(q, 1, 0)

    scale = 1.0 / math.sqrt(HEAD_DIM)
    a_idx = jnp.arange(BLOCK)[:, None]
    c_idx = jnp.arange(2 * BLOCK)[None, :]
    rel_ok = (c_idx <= a_idx + BLOCK) & (c_idx > a_idx + BLOCK - WINDOW)
    sink = sinks.astype(jnp.float32).reshape(N_KV_HEADS, GROUP)[None, :, :, None, None]

    def block_attn(args):
        qb, kb, vb, blk = args
        s = jnp.einsum("bqkgd,bckd->bkgqc", qb.astype(jnp.float32),
                       kb.astype(jnp.float32)) * scale
        mask = rel_ok & ((blk > 0) | (c_idx >= BLOCK))
        s = jnp.where(mask[None, None, None], s, NEG_INF)
        m = jnp.maximum(jnp.max(s, axis=-1, keepdims=True), sink)
        p = jnp.exp(s - m)
        denom = jnp.sum(p, axis=-1, keepdims=True) + jnp.exp(sink - m)
        o = jnp.einsum("bkgqc,bckd->bqkgd", p / denom, vb.astype(jnp.float32))
        return o.astype(x.dtype)

    o = lax.map(block_attn, (q, k_band, v_band, jnp.arange(nb)))
    o = jnp.moveaxis(o, 0, 1).reshape(bsz, seq, N_HEADS * HEAD_DIM)
    return (o * jax.nn.silu(z)) @ w_out

def second_inputs(seed: int = 0) -> dict:
    key = jax.random.key(seed)
    ks = jax.random.split(key, 16)
    f32 = jnp.float32
    D, W, H, KV, HD = D_MODEL, CONV_CH, N_HEADS, N_KV_HEADS, HEAD_DIM
    nrm = lambda k, shape, fan: jax.random.normal(k, shape, f32) * (fan ** -0.5)
    return {
        "x": jax.random.normal(ks[0], (BATCH, SEQ, D), f32),
        "ln_a": 1.0 + 0.02 * jax.random.normal(ks[1], (N_A, D), f32),
        "w_in_a": nrm(ks[2], (N_A, D, 4 * W), D),
        "conv_a": nrm(ks[3], (N_A, CONV_W, 1, W), CONV_W),
        "w_out_a": nrm(ks[4], (N_A, W, D), W),
        "ln_kv": 1.0 + 0.02 * jax.random.normal(ks[5], (D,), f32),
        "w_kv": nrm(ks[6], (D, 2 * KV * HD), D),
        "k_norm": 1.0 + 0.02 * jax.random.normal(ks[7], (HD,), f32),
        "ln_b": 1.0 + 0.02 * jax.random.normal(ks[8], (N_B, D), f32),
        "w_in_b": nrm(ks[9], (N_B, D, 2 * H * HD), D),
        "q_norm": 1.0 + 0.02 * jax.random.normal(ks[10], (N_B, HD), f32),
        "sinks": 0.5 * jax.random.normal(ks[11], (N_B, H), f32),
        "w_out_b": nrm(ks[12], (N_B, H * HD, D), H * HD),
    }

def second_block(x, ln_a, w_in_a, conv_a, w_out_a, ln_kv, w_kv, k_norm,
              ln_b, w_in_b, q_norm, sinks, w_out_b):
    seq = x.shape[1]
    cos, sin = rope_tables(seq)
    k_band = v_band = None
    for layer in range(DEPTH_2):
        if layer < N_A:
            i = layer
            x = x + short_conv_mixer(x, ln_a[i], w_in_a[i], conv_a[i], w_out_a[i])
        else:
            i = layer - N_A
            if i == 0:
                k_band, v_band = shared_kv(x, ln_kv, w_kv, k_norm, cos, sin)
            x = x + swa_sink_mixer(x, ln_b[i], w_in_b[i], q_norm[i], sinks[i], w_out_b[i],
                                   k_band, v_band, cos, sin)
    return x


def setup_inputs(seed=0):
    out = dict(first_inputs(seed))
    for name, value in second_inputs(seed + 1).items():
        if name != "x":
            out[name + "_2"] = value
    return out


def reference(
    x, mem, norm_mix_g, w_in, w_out, da_lambda, da_subln_g, ml_conv_w, ml_conv_b, ml_gate_b,
    ml_norm_g, norm_x_g, norm_mem_g, w_xq, w_xk, w_xv, w_xo, norm_ffn_g, w_router_group,
    b_router_group, w_router_expert, b_router_expert, w1, w3, w2, norm_final_g, ln_a_2,
    w_in_a_2, conv_a_2, w_out_a_2, ln_kv_2, w_kv_2, k_norm_2, ln_b_2, w_in_b_2, q_norm_2,
    sinks_2, w_out_b_2,
):
    x = first_block(
        x, mem, norm_mix_g, w_in, w_out, da_lambda, da_subln_g, ml_conv_w, ml_conv_b, ml_gate_b,
        ml_norm_g, norm_x_g, norm_mem_g, w_xq, w_xk, w_xv, w_xo, norm_ffn_g, w_router_group,
        b_router_group, w_router_expert, b_router_expert, w1, w3, w2, norm_final_g,
    )
    return second_block(
        x, ln_a_2, w_in_a_2, conv_a_2, w_out_a_2, ln_kv_2, w_kv_2, k_norm_2, ln_b_2, w_in_b_2,
        q_norm_2, sinks_2, w_out_b_2,
    )


_drawn_inputs = setup_inputs


def setup_inputs(seed=0):
    import zlib

    import numpy as np

    out = dict(_drawn_inputs(seed))
    spreads = {}
    factors = {'ml_conv_b': 2.809,
     'ml_norm_g': 2.915,
     'norm_x_g': 4.585,
     'norm_mem_g': 5.724,
     'b_router_group': 3.744,
     'b_router_expert': 4.88,
     'ln_a_2': 2.677,
     'ln_kv_2': 8.0,
     'k_norm_2': 8.0,
     'ln_b_2': 8.0,
     'q_norm_2': 8.0,
     'sinks_2': 64.0}
    for name, (base, spread) in spreads.items():
        noise = np.random.default_rng([zlib.crc32(name.encode()), seed]).standard_normal(out[name].shape)
        drawn = base * np.exp(spread * noise) if base else spread * noise
        out[name] = jnp.asarray(drawn.astype(out[name].dtype))
    for name, factor in factors.items():
        out[name] = (out[name] * factor).astype(out[name].dtype)
    return out
```

```python
import math
from contextlib import ExitStack

import numpy as np

import concourse.bass as bass
from concourse import mybir

F32 = mybir.dt.float32
I32 = mybir.dt.int32
U32 = mybir.dt.uint32
ALU = mybir.AluOpType
ACT = mybir.ActivationFunctionType
AX = mybir.AxisListType

P = 128
D = 1024
SEQ = 512
NT = SEQ // P
KD = D // P
MEM = 256
MT = MEM // P
HEADS = 4
DA_DIM = 64
LAM_INIT = 0.8 - 0.6 * math.exp(-0.0)
EPS = 1e-6
NEG = -1e30
CONV1 = 4
CONV2 = 3
GROUPS = 4
EXPERTS = 32
PER_GROUP = EXPERTS // GROUPS
FF = 512
SLOTS = 64
TILES = SEQ // SLOTS
OVER = 2 * SEQ // SLOTS - 1
ITEMS = EXPERTS + OVER
NOWHERE = 4096.0
WH = 16
WKV = 4
WD = 64
ROT = 16
CHUNK = 4096
RING = 5

CONST_COLS = [("ident", P), ("mask_qk", P), ("mask_kq", P), ("rot", P), ("before", P), ("ones", P),
              ("slot_row", P), ("item_row", ITEMS), ("tok_col", NT), ("band", 2 * P),
              ("cos2", NT * ROT // 2), ("sin2", NT * ROT // 2), ("half_col", 1)]
CONST_AT = {}
_n = 0
for _name, _c in CONST_COLS:
    CONST_AT[_name] = (_n, _c)
    _n += _c
CONST_N = _n


def shape_constants():
    c = np.zeros((P, CONST_N), np.float32)

    def put(name, a):
        at, n = CONST_AT[name]
        c[:, at:at + n] = np.asarray(a, np.float32).reshape(P, n)

    i = np.arange(P)
    put("ident", np.eye(P))
    put("mask_qk", np.where(i[None, :] <= i[:, None], 0.0, NEG))
    put("mask_kq", np.where(i[:, None] <= i[None, :], 0.0, NEG))
    rot = np.zeros((P, P))
    for base in (0, DA_DIM):
        for j in range(DA_DIM // 2):
            rot[base + DA_DIM // 2 + j, base + j] = -1.0
            rot[base + j, base + DA_DIM // 2 + j] = 1.0
    put("rot", rot)
    put("before", i[:, None] < i[None, :])
    put("ones", np.ones((P, P)))
    put("slot_row", np.broadcast_to(i % SLOTS, (P, P)))
    put("item_row", np.broadcast_to(np.arange(ITEMS), (P, ITEMS)))
    put("tok_col", i[:, None] + P * np.arange(NT)[None, :])
    q, k = i[:, None], np.arange(2 * P)[None, :]
    put("band", np.where((k <= q + P) & (k > q), 0.0, NEG))
    pos = np.arange(SEQ, dtype=np.float32)
    inv = np.float32(500000.0) ** (-np.arange(0, ROT, 2, dtype=np.float32) / np.float32(ROT))
    ang = (pos[:, None] * inv[None, :]).astype(np.float32)
    rows = lambda a: a.reshape(NT, P, ROT // 2).transpose(1, 0, 2).reshape(P, -1)
    put("cos2", rows(np.cos(ang)))
    put("sin2", rows(np.sin(ang)))
    put("half_col", (i >= SLOTS) * 2.0 * SEQ)
    inv = np.float32(10000.0) ** (-np.arange(0, DA_DIM, 2, dtype=np.float32) / np.float32(DA_DIM))
    ang = (pos[:, None] * inv[None, :]).astype(np.float32).T
    rope = np.concatenate([np.tile(np.cos(ang), (4, 1)), np.tile(np.sin(ang), (4, 1))], axis=1)
    pick = np.zeros((HEADS, HEADS, P), np.float32)
    for h in range(HEADS):
        pick[h, h, :] = -1.0
    return {"consts": c, "rope": rope.astype(np.float32), "pick": pick.reshape(HEADS, HEADS * P)}


def first_plan():
    plan = [(("x_t", k), "act" if k % 2 == 0 else "dve") for k in range(KD)]
    plan += [(("gate", "i"), "dve"), (("gate", "f"), "dve")]
    for j in range(2 * HEADS):
        plan.append((("qk", j), "act"))
        if j >= 1:
            plan.append((("qk_rot", j - 1), "dve"))
    plan.append((("dv", 0), "act"))
    plan.append((("qk_rot", 2 * HEADS - 1), "dve"))
    plan += [(("dv", t), "act") for t in range(1, NT)]
    for i in range(16 + 2):
        if i < 16:
            plan += [(("ds", i, 0), "act"), (("ds", i, 1), "act")]
            plan.append((("proj", i), "dve" if 8 <= i < 12 else "act"))
        if 1 <= i <= 16:
            plan.append((("da_t", i - 1), "dve"))
        if i >= 2:
            plan.append((("do", i - 2), "act"))
    plan.append((("gates_t",), "dve"))
    for h in range(HEADS):
        plan.append((("m_row", h), "act"))
        for kb in range(NT):
            plan.append((("ms", h, kb), "dve"))
        for qb in range(NT):
            plan.append((("mh", h, qb), "dve"))
    plan += [(("y_t", m), "dve") for m in range(8)]
    plan += [(("wo", n, t), "dve") for n in range(2) for t in range(NT)]
    plan += [(("mem_t", k), "dve") for k in range(KD // 2)]
    plan += [(("xk", m), "act") for m in range(8)]
    plan += [(("xv", n, t), "act") for n in range(2) for t in range(MT)]
    plan += [(("x1_t", k), "act" if k % 2 == 0 else "dve") for k in range(KD)]
    plan += [(("xq", m), "act") for m in range(8)]
    for i in range(16 + 2):
        if i < 16:
            plan.append((("xs", i), "act"))
        if i >= 2:
            plan.append((("xp", i - 2), "dve"))
            if (i - 2) % NT == NT - 1:
                plan += [(("xo", (i - 2) // NT, d), "act") for d in range(2)]
    plan += [(("xw", n, t), "dve") for n in range(2) for t in range(NT)]
    plan += [(("x2_t", k), "act" if k % 2 == 0 else "dve") for k in range(KD)]
    plan += [(("route", t), "dve") for t in range(NT)]
    plan += [(("rank", t), "dve") for t in range(NT)] + [(("count",), "dve")]
    plan += [(("table",), "dve")]
    return plan


def second_plan():
    plan = [(("x4_t", k), "act" if k % 2 == 0 else "dve") for k in range(KD)]
    for j in range(KD):
        plan += [(("c", j), "act"), (("u", j), "dve"), (("z", j), "act"), (("b", j), "dve")]
    plan += [(("wa", n, t), "dve") for n in range(2) for t in range(NT)]
    plan += [(("x5_t", k), "dve") for k in range(KD)]
    plan += [(("kv", t), "act") for t in range(NT)]
    plan += [(("q", n, t), "act") for n in range(2) for t in range(NT)]
    plan += [(("zz", m), "act") for m in range(8)]
    plan += [(("k_t", g), "dve") for g in range(WKV)]
    plan += [(("q_t", p), "act") for p in range(8)]
    for i in range(16 + 2):
        if i < 16:
            plan += [(("ws", i, 0), "dve"), (("ws", i, 1), "dve")]
        if i >= 2:
            plan += [(("wp", i - 2, kt), "act") for kt in window_tiles(i - 2)]
            plan.append((("wv", i - 2), "dve"))
    plan += [(("wb", n, t), "dve") for n in range(2) for t in range(NT)]
    return plan


def window_tiles(i):
    return [0, 1] if i // WKV > 0 else [1]


class Use:

    def __init__(self, n, what, by, filled, after, of_engine):
        self.what, self.bank, self.by = what, n % 8, by
        self.filled = filled
        self.after = after
        self.emptied = of_engine


def number(plan, base, act0, dve0):
    uses, order, count = {}, [], {"act": act0, "dve": dve0}
    for n, (what, by) in enumerate(plan):
        count[by] += 1
        after = (order[n - 8].by, order[n - 8].emptied) if n >= 8 else None
        u = Use(n, what, by, base + n + 1, after, count[by])
        order.append(u)
        uses[what] = u
    return uses, count["act"], count["dve"]


N_MORE = 3 + 2 + CONV1 + 1 + CONV2 + 5

INS = ["x", "mem", "norm_mix_g", "w_in", "w_out", "da_lambda", "da_subln_g", "ml_conv_w", "ml_conv_b",
       "ml_gate_b", "ml_norm_g", "norm_x_g", "norm_mem_g", "w_xq", "w_xk", "w_xv", "w_xo", "norm_ffn_g",
       "w_router_group", "b_router_group", "w_router_expert", "b_router_expert", "w1", "w3", "w2",
       "norm_final_g", "ln_a_2", "w_in_a_2", "conv_a_2", "w_out_a_2", "ln_kv_2", "w_kv_2", "k_norm_2",
       "ln_b_2", "w_in_b_2", "q_norm_2", "sinks_2", "w_out_b_2"]


def build(nc, a, out):
    U, act1, dve1 = number(first_plan(), 0, 0, 0)
    n1 = len(first_plan())
    V, act2, dve2 = number(second_plan(), n1, act1, dve1)

    ctx = ExitStack()
    with ctx:
        def sb(name, cols, dt=F32, parts=P):
            return ctx.enter_context(nc.sbuf_tensor(name, [parts, cols], dt))

        sems = {}

        def sem(name):
            if name not in sems:
                sems[name] = ctx.enter_context(nc.semaphore(name))
            return sems[name]

        ring = [sb(f"ring{i}", CHUNK) for i in range(RING)]
        X = sb("X", NT * D)
        XN = sb("XN", NT * D)
        HT = sb("HT", KD * SEQ)
        A0 = sb("A0", KD * SEQ)
        A1 = sb("A1", KD * (SEQ + CONV1 - 1))
        B0 = sb("B0", NT * SEQ)
        B1 = sb("B1", NT * HEADS * (P + 1))
        B2 = sb("B2", NT * SEQ)
        E = sb("E", NT * SEQ)
        cst = sb("cst", CONST_N)
        pick = sb("pick", HEADS * P, parts=HEADS)
        small = sb("small", 1472)
        ints = sb("ints", 2 * ITEMS + 8, dt=I32)

        bank = [ctx.enter_context(nc.psum_tensor(f"bank{i}", [P, 512], F32)) for i in range(8)]

        xn_dram = nc.dram_tensor("xn_dram", (2 * SEQ, 512), F32).ap()
        y_dram = nc.dram_tensor("y_dram", (4 * SEQ, 512), F32).ap()

        def const(name, rows=P):
            at, n = CONST_AT[name]
            return cst[0:rows, at:at + n]

        ident = const("ident")
        taken = [0]

        def col(n):
            at = taken[0]
            taken[0] += n
            assert taken[0] <= 1472
            return small[:, at:at + n]

        g_mix, g_x, g_mem, g_ffn, g_a, g_kv, g_b = (col(KD) for _ in range(7))
        g_xh = col(KD)
        g_sub, g_ml, conv_w, conv_b = col(1), col(HEADS), col(KD * CONV1), col(KD)
        gate_b = col(2)
        conv_w2 = col(KD * CONV2)
        lam_in, lam_c = col(4 * DA_DIM), col(8)
        router_b = col(GROUPS + EXPERTS)
        k_gain, q_gain, sink = col(WD), col(WD), col(WH)
        ss, ms, root, rstd = col(80), col(80), col(80), col(80)
        stat = col(96)
        mx, neg, zsum, rz = (col(16) for _ in range(4))
        bmT, em = col(32), col(16)
        bT, mT = bmT[:, 0:16], bmT[:, 16:32]
        lam_s, neg_lam, g_sub_s = lam_c[:, 0:4], lam_c[:, 4:5], lam_c[:, 5:6]

        def f3(t, shape, at=0):
            n = int(np.prod(shape))
            v = t[:, at:at + n]
            if len(shape) == 2:
                return v.rearrange("p (a b) -> p a b", a=shape[0])
            return v.rearrange("p (a b c) -> p a b c", a=shape[0], b=shape[1])

        x_rows, xn, hT = f3(X, (NT, D)), f3(XN, (NT, D)), f3(HT, (KD, SEQ))
        w_gates = E[:, 1024:1024 + 8 * KD].rearrange("p (k n) -> p k n", k=KD)
        cosT, sinT = E[:, 0:SEQ], E[:, SEQ:2 * SEQ]
        qkT = f3(A0, (KD, SEQ))
        convT = f3(A1, (KD, SEQ + CONV1 - 1))
        mqkT = convT[:, :, CONV1 - 1:]
        dv_rows = f3(B0, (NT, SEQ))
        mv_rows = f3(B1, (NT, HEADS, P + 1))
        moT = f3(B2, (HEADS, SEQ))
        e_buf = f3(E, (2, 2, SEQ))
        yT = xn_cols = f3(XN, (KD, SEQ))
        rope_tmp = X[:, 0:SEQ]
        conv_tmp = f3(X, (2, SEQ), 0)
        daT = f3(X, (2, NT, P), 2 * SEQ)
        o_rows = f3(X, (NT, HEADS, P), 4 * SEQ)
        gw = [f3(XN, (1, SEQ), SEQ * i)[0:HEADS, 0, :] for i in range(8)]
        g_i, g_f, g_min, g_l, g_a_sum, g_bb, g_M, g_ex = gw
        d_buf = f3(A0, (2, SEQ), 0)
        arg_diag = f3(A0, (2, SEQ), 2 * SEQ)
        hm_rows = f3(A0, (NT, HEADS, P), 4 * SEQ)
        sdT = f3(HT, (2, NT, SEQ))
        mem_rows = f3(A1, (MT, D))
        memT = f3(A0, (KD, MEM))
        xqT, xkT, xv_rows = f3(A0, (KD, SEQ)), f3(B2, (KD, MEM)), f3(B0, (MT, D))
        xe = f3(E, (4, MEM))
        pT = f3(B1, (2, MT, SEQ))
        w_slot = [[ring[0], ring[1], ring[2]], [ring[3], ring[4], A1]]
        over_slot = [HT, A0, XN]
        xg = [E[:, 0:512], E[:, 512:1024], B0[:, 1536:2048], B2[:, 1024:1536]]
        y_sb = [E[:, 1024:1536], E[:, 1536:2048]]
        xgT = [f3(B0, (4, 2, SLOTS), 512 * b) for b in range(2)]
        gT = [f3(B0, (4, SLOTS), 1024 + 256 * b) for b in range(2)]
        sil = [B1[:, 0:512], B1[:, 512:1024]]
        gg = [B1[:, 1024:1536], B1[:, 1536:2048]]
        tab = B2[:, 0:3 * ITEMS]
        tab_w = B2[:, 2 * ITEMS:3 * ITEMS]
        router_w = f3(B2, (KD, GROUPS + EXPERTS), 256)
        sel1h = f3(B2, (2, NT, EXPERTS), 600)
        selb = f3(B2, (NT, EXPERTS), 860)
        rw = B2[:, 1000:2048]
        tab_g, tab_s = ints[:, 0:ITEMS], ints[:, ITEMS:2 * ITEMS]
        idx_g = [ints[:, 2 * ITEMS + q:2 * ITEMS + q + 1] for q in range(4)]
        idx_s = [ints[:, 2 * ITEMS + 4 + b:2 * ITEMS + 5 + b] for b in range(2)]
        over_n = ints[0:1, 2 * ITEMS + 6:2 * ITEMS + 7]
        over_e = sb("over_e", OVER + 1, dt=I32, parts=1)

        act_n, dve_n, pool_n = [0], [0], [0]
        act_step, dve_step, pool_step = sem("act_step"), sem("dve_step"), sem("pool_step")
        bank_filled = sem("bank_filled")
        emptied = {"act": sem("emptied_by_act"), "dve": sem("emptied_by_dve")}

        def wait_emptied(eng, use):
            eng.wait_ge(emptied[use.by], use.emptied)

        def then_own(eng, ins, step, n):
            n[0] += 1
            ins.then_inc(step, 1)
            eng.wait_ge(step, n[0])

        def w_cols(w, c0, n=512):
            return w.rearrange("(p k) n -> p k n", k=KD)[:, :, c0:c0 + n]

        def w_nat(w, c0, n=512):
            return w.rearrange("(k p) n -> p k n", p=P)[:, :, c0:c0 + n]

        lg = f3(rw, (NT, 40), 0)
        top = f3(rw, (NT, 16), 160)
        el = f3(rw, (NT, 8), 224)
        dif = f3(rw, (NT, 16), 256)
        pexp = f3(rw, (NT, 16), 320)
        rk, ovb, ea, slot, item, comb, tokg, toks = (rw[:, 384 + 8 * n:392 + 8 * n] for n in range(8))
        r4a, r4b, r4c, zg, gf, half5 = (rw[:, 448 + 4 * n:452 + 4 * n] for n in range(6))
        ohg = rw[:, 472:476]
        oh_slot = [rw[:, 480 + P * n:608 + P * n] for n in range(2)]
        oh_item = [rw[:, 736 + 3 * ITEMS * n:736 + 3 * ITEMS * (n + 1)] for n in range(2)]
        cnt, nov, ovend, ovbase, zero32, junk32 = (E[:, 1024 + EXPERTS * n:1024 + EXPERTS * (n + 1)] for n in range(6))
        over_cmp = E[0:1, 1280:1280 + (OVER + 1) * EXPERTS]
        over_row = E[0:1, 1900:1900 + OVER + 1]
        top_i = sb("top_i", NT * 16, dt=U32)
        gate_ready_cols = stat[:, 44:48]
        y_back = [f3(XN if t < 2 else A0, (2, D), 2048 * (t % 2)) for t in range(NT)]
        g_fin = B0[:, 0:D]

        cbuf, zbuf = f3(B2, (2, SEQ)), f3(B2, (2, SEQ), 2 * SEQ)
        vbuf = f3(B1, (2, SEQ + CONV2 - 1))
        cacc = f3(E, (2, SEQ))
        hkvT = f3(A0, (KD, SEQ))
        k_rows, v_rows2 = f3(B0, (NT * WKV, WD)), f3(B0, (NT, WKV * WD), NT * WKV * WD)
        q_rows = f3(XN, (NT, D))
        sq_buf = f3(E, (4, SEQ))
        k_dup, k2T = f3(B2, (NT, 2 * WKV * WD)), f3(B1, (WKV, SEQ))
        q2T, zT = f3(A0, (KD, SEQ)), f3(A1, (KD, SEQ))
        wS = f3(HT, (3, 4, 2 * P))
        wpT = f3(E, (2, 2, 4 * P))
        yT2 = f3(XN, (KD, SEQ))

        w_in = a["w_in"][0]
        chunks1 = [(w_cols(w_in, 0), ("qk", 3)), (w_cols(w_in, 512), ("qk", 7)), (w_cols(w_in, 1024), ("dv", 3)),
                   (w_cols(w_in, 1536), ("proj", 3)), (w_cols(w_in, 2048), ("proj", 7)),
                   (w_cols(w_in, 2560), ("proj", 11)), (w_cols(w_in, 3072), ("proj", 15))]
        chunks1 += [(w_nat(a["w_out"][0], 512 * n), ("wo", n, 3)) for n in range(2)]
        chunks1 += [(w_cols(a["w_xk"][0], 512 * n), ("xk", 4 * n + 3)) for n in range(2)]
        chunks1 += [(w_cols(a["w_xv"][0], 512 * n), ("xv", n, MT - 1)) for n in range(2)]
        chunks1 += [(w_cols(a["w_xq"][0], 512 * n), ("xq", 4 * n + 3)) for n in range(2)]
        chunks1 += [(w_nat(a["w_xo"][0], 512 * n), ("xw", n, 3)) for n in range(2)]
        ch1 = {}
        for c, name in enumerate(["dq", "dk", "dv", "mq", "mk", "mv", "mo", "wo0", "wo1", "xk0", "xk1",
                                  "xv0", "xv1", "xq0", "xq1", "xw0", "xw1"]):
            ch1[name] = c
        w_in_a = a["w_in_a_2"][0].rearrange("(p k) (f n) -> p k f n", k=KD, f=4)
        chunks2 = [(w_in_a[:, :, :, P * j:P * j + P], ("b", j)) for j in range(KD)]
        chunks2 += [(w_nat(a["w_out_a_2"][0], 512 * n), ("wa", n, 3)) for n in range(2)]
        chunks2 += [(w_cols(a["w_kv_2"], 0), ("kv", 3))]
        chunks2 += [(w_cols(a["w_in_b_2"][0], 512 * n), ("q", n, 3)) for n in range(2)]
        chunks2 += [(w_cols(a["w_in_b_2"][0], 1024 + 512 * n), ("zz", 4 * n + 3)) for n in range(2)]
        chunks2 += [(w_nat(a["w_out_b_2"][0], 512 * n), ("wb", n, 3)) for n in range(2)]
        ch2 = {}
        for c, name in enumerate([f"a{j}" for j in range(KD)] + ["wa0", "wa1", "kv", "q0", "q1", "z0", "z1",
                                                                "wb0", "wb1"]):
            ch2[name] = c
        w1_loaded = [sem(f"w1_loaded{i}") for i in range(RING)]
        w2_loaded = [sem(f"w2_loaded{i}") for i in range(RING)]
        we_loaded = [[sem(f"we_loaded{b}{j}") for j in range(3)] for b in range(2)]

        def w_at(n, c):
            return f3(ring[c % RING], (KD, 512))

        def expert_weights(e):
            one = lambda w: w[0, bass.ds(e, 1)]
            return [one(a["w1"]).rearrange("o (h p k) n -> p (o h) (k n)", h=2, p=P),
                    one(a["w3"]).rearrange("o (h p k) n -> p (o h) (k n)", h=2, p=P),
                    one(a["w2"]).rearrange("o (p k) n -> p (o k n)", p=P)]

        def as_expert(t, j):
            return f3(t, (2, 2048)) if j < 2 else t[:, 0:CHUNK]

        def w_slot_as(b, j):
            return as_expert(w_slot[b][j], j)

        block = ctx.enter_context(nc.Block())

        @block.sync
        def _(sp):
            consts_loaded, x_loaded = sem("consts_loaded"), sem("x_loaded")
            for t in range(NT):
                sp.dma_start(x_rows[:, t, :], a["x"][0, P * t:P * t + P, :]).then_inc(sem(f"x_loaded{t}"), 16)
            sp.dma_start(cst[:, :], a["consts"]).then_inc(consts_loaded, 16)
            sp.dma_start(g_mix, a["norm_mix_g"][0].rearrange("(p k) -> p k", k=KD)).then_inc(consts_loaded, 16)
            sp.dma_start(w_gates, w_cols(w_in, 3584, 8)).then_inc(consts_loaded, 16)
            sp.dma_start(gate_b[0:HEADS, :], a["ml_gate_b"][0].rearrange("g h -> h g"),
                         allow_slow_non_contiguous=True).then_inc(consts_loaded, 16)

            for c, (src, last) in enumerate(chunks1):
                if c >= RING:
                    sp.wait_ge(bank_filled, U[chunks1[c - RING][1]].filled)
                sp.dma_start(w_at(1, c), src).then_inc(w1_loaded[c % RING], 16)
                if c == 1:
                    for dst, name, k in ((g_x, "norm_x_g", KD), (g_mem, "norm_mem_g", KD), (g_ffn, "norm_ffn_g", KD),
                                         (g_a, "ln_a_2", KD), (g_b, "ln_b_2", KD)):
                        sp.dma_start(dst, a[name][0].rearrange("(p k) -> p k", k=k)).then_inc(sem("more_loaded"), 16)
                    sp.dma_start(g_kv, a["ln_kv_2"].rearrange("(p k) -> p k", k=KD)).then_inc(sem("more_loaded"), 16)
                    for hf in range(2):
                        sp.dma_start(g_xh[:, 4 * hf:4 * hf + 4],
                                     a["norm_ffn_g"][0, 512 * hf:512 * hf + 512].rearrange("(p k) -> p k", k=4))\
                          .then_inc(sem("more_loaded"), 16)

            def second_weights(c):
                src = chunks2[c][0]
                if c < KD:
                    dst = f3(ring[c % RING], (KD, 4 * P))
                    for f in range(4):
                        sp.dma_start(dst[:, :, P * f:P * f + P], src[:, :, f, :]).then_inc(w2_loaded[c % RING], 16)
                else:
                    sp.dma_start(w_at(2, c), src).then_inc(w2_loaded[c % RING], 16)

            for b in range(2):
                for j, src in enumerate(expert_weights(b)):
                    slot = 3 * b + j
                    if slot < RING:
                        c = max(c for c in range(len(chunks1)) if c % RING == slot)
                        sp.wait_ge(bank_filled, U[chunks1[c][1]].filled)
                    else:
                        sp.wait_ge(bank_filled, U["mem_t", KD // 2 - 1].filled)
                    sp.dma_start(w_slot_as(b, j), src).then_inc(we_loaded[b][j], 16)
            h_done, y_done = sem("h_done"), sem("y_done")
            with sp.Fori(1, EXPERTS // 2) as i:
                for b in range(2):
                    for j, src in enumerate(expert_weights(2 * i + b)):
                        sp.wait_ge(h_done if j < 2 else y_done, 2 * i + b - 1)
                        sp.wait_ge(we_loaded[1][2], 16)
                        sp.dma_start(w_slot_as(b, j), src).then_inc(we_loaded[b][j], 16)

            sp.wait_ge(h_done, EXPERTS - 1)
            for c in range(2):
                second_weights(c)
            sp.wait_ge(y_done, EXPERTS - 1)
            second_weights(2)

            wait_emptied(sp, U["table",])
            n = sp.value_load(over_n, min_val=0, max_val=OVER)
            with sp.If(n > 0):
                with sp.Fori(0, OVER) as k:
                    sp.wait_ge(sem("y_ready"), k + EXPERTS)
                    e = sp.value_load(over_e[0:1, bass.ds(k, 1)], min_val=0, max_val=EXPERTS - 1)
                    for j, src in enumerate(expert_weights(e)):
                        sp.dma_start(as_expert(over_slot[j], j), src).then_inc(sem("ov_w_loaded"), 16)

            for t in range(NT):
                sp.wait_ge(sem(f"y_back{t}"), 64)
            for c in range(3, len(chunks2)):
                if c >= RING:
                    sp.wait_ge(bank_filled, V[chunks2[c - RING][1]].filled)
                second_weights(c)
            for n in range(2):
                for t in range(NT):
                    wait_emptied(sp, V["wb", n, t])
                    sp.dma_start(out[0, P * t:P * t + P, 512 * n:512 * n + 512],
                                 x_rows[:, t, 512 * n:512 * n + 512]).then_inc(sem("out_stored"), 16)
            sp.wait_ge(sem("out_stored"), 16 * 2 * NT)

        def w2_value(c):
            return sum(16 * (4 if d < KD else 1) for d in range(c % RING, c + 1, RING))

        @block.gpsimd
        def _(pool):
            more = sem("more_loaded2")
            pool.memset(convT[:, :, 0:CONV1 - 1], 0.0).then_inc(sem("pads_zero"), 1)
            pool.memset(mv_rows[:, :, :, P:P + 1], 1.0).then_inc(sem("pads_zero"), 1)
            loads = [(rope_dst, a["rope"]) for rope_dst in (E[:, 0:2 * SEQ],)]
            loads += [(pick[:, :], a["pick"])]
            loads += [(lam_in, a["da_lambda"][0].rearrange("f n -> (f n)").partition_broadcast(P))]
            loads += [(g_sub, a["da_subln_g"][0].rearrange("(p k) -> p k", k=1))]
            loads += [(g_ml, a["ml_norm_g"][0].rearrange("(h p) -> p h", p=P))]
            loads += [(conv_w.rearrange("p (t m) -> p t m", m=KD)[:, t, :],
                       a["ml_conv_w"][0, t, 0].rearrange("(m p) -> p m", p=P)) for t in range(CONV1)]
            loads += [(conv_b, a["ml_conv_b"][0].rearrange("(m p) -> p m", p=P))]
            loads += [(conv_w2.rearrange("p (t m) -> p t m", m=KD)[:, t, :],
                       a["conv_a_2"][0, t, 0].rearrange("(m p) -> p m", p=P)) for t in range(CONV2)]
            loads += [(router_b[:, 0:GROUPS], a["b_router_group"][0].partition_broadcast(P)),
                      (router_b[:, GROUPS:], a["b_router_expert"][0].partition_broadcast(P)),
                      (k_gain, a["k_norm_2"].partition_broadcast(P)), (q_gain, a["q_norm_2"][0].partition_broadcast(P)),
                      (sink, a["sinks_2"][0].partition_broadcast(P))]
            for dst, src in loads:
                pool.dma_start(dst, src, allow_slow_non_contiguous=True).then_inc(more, 16)
            assert len(loads) == N_MORE

            pool.wait_ge(bank_filled, U["ms", HEADS - 1, NT - 1].filled)
            pool.dma_start(mem_rows, a["mem"][0].rearrange("(t p) d -> p t d", p=P)).then_inc(sem("mem_loaded"), 16)
            pool.wait_ge(bank_filled, U["y_t", 3].filled)
            for t in range(NT):
                pool.dma_start(x_rows[:, t, :], a["x"][0, P * t:P * t + P, :]).then_inc(sem("x_again"), 16)
            pool.wait_ge(bank_filled, U["xs", 15].filled)
            rg = a["w_router_group"][0].rearrange("(p k) n -> p k n", k=KD)
            re = a["w_router_expert"][0].rearrange("(p k) n -> p k n", k=KD)
            pool.dma_start(router_w[:, :, 0:GROUPS], rg).then_inc(sem("router_loaded"), 16)
            pool.dma_start(router_w[:, :, GROUPS:], re).then_inc(sem("router_loaded"), 16)
            for t in range(NT):
                pool.wait_ge(sem("x2n_ready"), t + 1)
                for hf in range(2):
                    pool.dma_start(xn_dram[512 * hf + P * t:512 * hf + P * t + P, :],
                                   xn[:, t, 512 * hf:512 * hf + 512]).then_inc(sem("xn_stored"), 16)
            pool.wait_ge(bank_filled, U["xo", HEADS - 1, 1].filled)
            for b in range(3):
                then_own(pool, pool.memset(xg[b], 0.0), pool_step, pool_n)
            pool.wait_ge(sem("xn_stored"), 16 * 2 * NT)
            wait_emptied(pool, U["table",])
            then_own(pool, pool.memset(xg[3], 0.0), pool_step, pool_n)

            xg_turned, y_ready = sem("xg_turned"), sem("y_ready")
            first_idx, gather_idx, scatter_idx = sem("first_idx"), sem("gather_idx"), sem("scatter_idx")

            def index(dst, src, written, value):
                pool.tensor_copy(dst, src).then_inc(written, 1)
                pool.wait_ge(sem("xn_stored"), 16 * 2 * NT)
                pool.wait_ge(written, value)

            def gather_rows(q, s="xg_loaded"):
                pool.indirect_dma_start(xg[q], None, xn_dram,
                                        bass.IndirectOffsetOnAxis(ap=idx_g[q].bitcast(U32), axis=0),
                                        bounds_check=2 * SEQ - 1, oob_is_err=False).then_inc(sem(f"{s}{q}"), 16)

            def scatter_rows(b, s="y_stored"):
                pool.indirect_dma_start(y_dram, bass.IndirectOffsetOnAxis(ap=idx_s[b].bitcast(U32), axis=0),
                                        y_sb[b], None, bounds_check=4 * SEQ - 1, oob_is_err=False)\
                    .then_inc(sem(f"{s}{b}"), 16)

            for q in range(4):
                index(idx_g[q], tab_g[:, q:q + 1], first_idx, q + 1)
                gather_rows(q)

            def four(i, last):
                for q in range(4):
                    e = 4 * i + q
                    b = q % 2
                    if not last:
                        pool.wait_ge(xg_turned, e + 1)
                        index(idx_g[q], tab_g[:, bass.ds(e + 4, 1)], gather_idx, e + 1)
                        gather_rows(q)
                    pool.wait_ge(y_ready, e + 1)
                    index(idx_s[b], tab_s[:, bass.ds(e, 1)], scatter_idx, e + 1)
                    scatter_rows(b)

            with pool.Fori(0, EXPERTS // 4 - 1) as i:
                four(i, False)
            four(EXPERTS // 4 - 1, True)
            for b in range(2):
                pool.wait_ge(sem(f"y_stored{b}"), 16 * EXPERTS // 2)

            n = pool.value_load(over_n, min_val=0, max_val=OVER)
            with pool.If(n > 0):
                with pool.Fori(1, OVER + 1) as k:
                    index(idx_g[0], tab_g[:, bass.ds(k + (EXPERTS - 1), 1)], sem("ov_gather_idx"), k)
                    gather_rows(0, "ov_xg_loaded")
                    pool.wait_ge(y_ready, k + EXPERTS)
                    index(idx_s[0], tab_s[:, bass.ds(k + (EXPERTS - 1), 1)], sem("ov_scatter_idx"), k)
                    pool.indirect_dma_start(y_dram, bass.IndirectOffsetOnAxis(ap=idx_s[0].bitcast(U32), axis=0),
                                            y_sb[0], None, bounds_check=4 * SEQ - 1, oob_is_err=False)\
                        .then_inc(sem("ov_stored"), 16)
                    pool.wait_ge(sem("ov_stored"), 16 * k)
            pool.wait_ge(sem("pe_left_experts"), 1)
            for t in range(NT):
                for c in range(2):
                    for hf in range(2):
                        r = 1024 * hf + 512 * c + P * t
                        dst = y_back[t][:, c, 512 * hf:512 * hf + 512]
                        pool.dma_start(dst, y_dram[r:r + P, :]).then_inc(sem(f"y_back{t}"), 16)
            pool.dma_start(g_fin, a["norm_final_g"].partition_broadcast(P)).then_inc(sem("g_fin_loaded"), 16)

        @block.tensor
        def _(pe):
            done = [0]

            def fill(us, *what):
                u = us[what]
                base = 0 if us is U else n1
                assert u.filled == base + done[0] + 1, what
                done[0] += 1
                if u.after:
                    pe.wait_ge(emptied[u.after[0]], u.after[1])
                return bank[u.bank]

            def gemm(o, lhs, rhs, n=KD):
                for k in range(n):
                    last = pe.matmul(o, lhs(k), rhs(k), start=(k == 0), stop=(k == n - 1))
                return last.then_inc(bank_filled, 1)

            def turn(us, name, src, ready, base, n=NT):
                for k in range(KD):
                    o = fill(us, name, k)
                    for t in range(n):
                        if k == 0:
                            pe.wait_ge(ready, base + t + 1)
                        last = pe.transpose(o[:, P * t:P * t + P], src[:, t, k:D:KD], ident)
                    last.then_inc(bank_filled, 1)

            def chunk(c):
                pe.wait_ge(w1_loaded[c % RING], 16 * (c // RING + 1))
                return w_at(1, c)

            pe.wait_ge(sem("consts_loaded"), 16 * 4)
            turn(U, "x_t", xn, sem("x0n_ready"), 0)
            wait_emptied(pe, U["x_t", 6])
            wait_emptied(pe, U["x_t", 7])
            for g in range(2):
                gemm(fill(U, "gate", "if"[g])[0:HEADS, :], lambda k: w_gates[:, k, 4 * g:4 * g + 4],
                     lambda k: hT[:, k, :])

            def rotate(j):
                o = fill(U, "qk_rot", j)
                wait_emptied(pe, U["qk", j])
                pe.matmul(o[:, :], const("rot"), qkT[:, j, :], start=True, stop=True).then_inc(bank_filled, 1)

            for j in range(2 * HEADS):
                w = chunk(ch1["dq"] + j // HEADS)
                m = j % HEADS
                gemm(fill(U, "qk", j)[:, :], lambda k: w[:, k, P * m:P * m + P], lambda k: hT[:, k, :])
                if j >= 1:
                    rotate(j - 1)
            w = chunk(ch1["dv"])
            for t in range(NT):
                gemm(fill(U, "dv", t)[:, :], lambda k: hT[:, k, P * t:P * t + P], lambda k: w[:, k, :])
                if t == 0:
                    rotate(2 * HEADS - 1)

            for i in range(16 + 2):
                if i < 16:
                    h, qb = divmod(i, NT)
                    n = P * (qb + 1)
                    for m in range(2):
                        o = fill(U, "ds", i, m)
                        pe.wait_ge(sem("qk_rotated"), 5 + h)
                        r = slice(64 * m, 64 * m + 64)
                        pe.matmul(o[:, 0:n], qkT[r, h, P * qb:P * qb + P], qkT[r, HEADS + h, 0:n],
                                  start=True, stop=True).then_inc(bank_filled, 1)
                    w = chunk(ch1["mq"] + i // 4)
                    m = i % 4
                    o = fill(U, "proj", i)
                    if 8 <= i < 12:
                        gemm(o[:, :], lambda k: hT[:, k, P * m:P * m + P], lambda k: w[:, k, :])
                    else:
                        gemm(o[:, :], lambda k: w[:, k, P * m:P * m + P], lambda k: hT[:, k, :])
                if 1 <= i <= 16:
                    j = i - 1
                    o = fill(U, "da_t", j)
                    pe.wait_ge(sem("da_ready"), j + 1)
                    for kb in range(j % NT + 1):
                        last = pe.transpose(o[:, P * kb:P * kb + P], e_buf[:, j % 2, 0, P * kb:P * kb + P], ident)
                    last.then_inc(bank_filled, 1)
                if i >= 2:
                    j = i - 2
                    h, qb = divmod(j, NT)
                    o = fill(U, "do", j)
                    wait_emptied(pe, U["da_t", j])
                    wait_emptied(pe, U["dv", NT - 1])
                    gemm(o[:, 0:P], lambda k: daT[:, j % 2, k, :], lambda k: dv_rows[:, k, P * h:P * h + P], qb + 1)

            o = fill(U, "gates_t")
            pe.wait_ge(sem("gates_ready"), 1)
            for v, src in enumerate((g_bb, g_ex)):
                for t in range(NT):
                    last = pe.transpose(o[:, 16 * v + 4 * t:16 * v + 4 * t + 4], src[:, P * t:P * t + P],
                                        ident[0:HEADS, 0:HEADS])
            last.then_inc(bank_filled, 1)
            for h in range(HEADS):
                pe.wait_ge(sem("more_loaded2"), 16 * N_MORE)
                pe.matmul(fill(U, "m_row", h)[:, :], pick[:, P * h:P * h + P], g_M, start=True, stop=True)\
                  .then_inc(bank_filled, 1)
                pe.wait_ge(sem("silu_ready"), 8)
                for kb in range(NT):
                    o = fill(U, "ms", h, kb)
                    pe.matmul(o[:, P * kb:SEQ], mqkT[:, HEADS + h, P * kb:P * kb + P], mqkT[:, h, P * kb:SEQ],
                              start=True, stop=True).then_inc(bank_filled, 1)
                wait_emptied(pe, U["proj", 11])
                pe.wait_ge(sem("pads_zero"), 2)
                for qb in range(NT):
                    o = fill(U, "mh", h, qb)
                    wait_emptied(pe, U["ms", h, qb])
                    gemm(o[:, 0:P + 1], lambda k: sdT[:, h % 2, k, P * qb:P * qb + P],
                         lambda k: mv_rows[:, k, h, :], qb + 1)
            for m in range(8):
                o = fill(U, "y_t", m)
                pe.wait_ge(sem("y_rows_ready"), m + 1)
                for t in range(NT):
                    src = o_rows[:, t, m, :] if m < 4 else hm_rows[:, t, m - 4, :]
                    last = pe.transpose(o[:, P * t:P * t + P], src, ident)
                last.then_inc(bank_filled, 1)
            wait_emptied(pe, U["y_t", 7])
            for n in range(2):
                w = chunk(ch1[f"wo{n}"])
                for t in range(NT):
                    gemm(fill(U, "wo", n, t)[:, :], lambda k: yT[:, k, P * t:P * t + P], lambda k: w[:, k, :])

            for k in range(KD // 2):
                o = fill(U, "mem_t", k)
                pe.wait_ge(sem("memn_ready"), MT)
                for kk in range(2):
                    for t in range(MT):
                        last = pe.transpose(o[:, MEM * kk + P * t:MEM * kk + P * t + P],
                                            mem_rows[:, t, 2 * k + kk:D:KD], ident)
                last.then_inc(bank_filled, 1)
            wait_emptied(pe, U["mem_t", KD // 2 - 1])
            for m in range(8):
                w = chunk(ch1["xk0"] + m // 4)
                gemm(fill(U, "xk", m)[:, 0:MEM], lambda k: w[:, k, P * (m % 4):P * (m % 4) + P],
                     lambda k: memT[:, k, :])
            for n in range(2):
                w = chunk(ch1["xv0"] + n)
                for t in range(MT):
                    gemm(fill(U, "xv", n, t)[:, :], lambda k: memT[:, k, P * t:P * t + P], lambda k: w[:, k, :])
            turn(U, "x1_t", xn, sem("x1n_ready"), 0)
            wait_emptied(pe, U["x1_t", 6])
            wait_emptied(pe, U["x1_t", 7])
            for m in range(8):
                w = chunk(ch1["xq0"] + m // 4)
                gemm(fill(U, "xq", m)[:, :], lambda k: w[:, k, P * (m % 4):P * (m % 4) + P], lambda k: hT[:, k, :])
            wait_emptied(pe, U["xv", 1, MT - 1])
            for i in range(16 + 2):
                if i < 16:
                    h, t = divmod(i, NT)
                    o = fill(U, "xs", i)
                    wait_emptied(pe, U["xq", 2 * h + 1])
                    gemm(o[:, 0:MEM], lambda k: xqT[:, 2 * h + k, P * t:P * t + P], lambda k: xkT[:, 2 * h + k, :], 2)
                if i >= 2:
                    j = i - 2
                    h, t = divmod(j, NT)
                    o = fill(U, "xp", j)
                    pe.wait_ge(sem("xp_ready"), j + 1)
                    for kt in range(MT):
                        last = pe.transpose(o[:, P * kt:P * kt + P], xe[:, j % 4, P * kt:P * kt + P], ident)
                    last.then_inc(bank_filled, 1)
                    if t == NT - 1:
                        wait_emptied(pe, U["xp", j])
                        for d in range(2):
                            c0 = MEM * h + P * d
                            gemm(fill(U, "xo", h, d)[:, :], lambda k: xv_rows[:, k, c0:c0 + P],
                                 lambda k: pT[:, h % 2, k, :], MT)
            wait_emptied(pe, U["xo", HEADS - 1, 1])
            for n in range(2):
                w = chunk(ch1["xw0"] + n)
                for t in range(NT):
                    gemm(fill(U, "xw", n, t)[:, :], lambda k: yT[:, k, P * t:P * t + P], lambda k: w[:, k, :])

            turn(U, "x2_t", xn, sem("x2n_ready"), 0)
            wait_emptied(pe, U["x2_t", 6])
            wait_emptied(pe, U["x2_t", 7])
            pe.wait_ge(sem("router_loaded"), 32)
            for t in range(NT):
                gemm(fill(U, "route", t)[:, 0:GROUPS + EXPERTS], lambda k: hT[:, k, P * t:P * t + P],
                     lambda k: router_w[:, k, :])
            pe.wait_ge(sem("chosen_ready"), NT)
            for t in range(NT):
                o = fill(U, "rank", t)
                for s in range(t + 1):
                    last = pe.matmul(o[:, 0:EXPERTS], const("ones") if s < t else const("before"), selb[:, s, :],
                                     start=(s == 0), stop=(s == t))
                last.then_inc(bank_filled, 1)
            gemm(fill(U, "count")[:, 0:EXPERTS], lambda k: const("ones"), lambda k: selb[:, k, :], NT)
            o = fill(U, "table")
            for s in range(2 * NT):
                pe.wait_ge(sem("onehots_ready"), s + 1)
                last = pe.matmul(o[:, 0:3 * ITEMS], oh_slot[s % 2], oh_item[s % 2], start=(s == 0),
                                 stop=(s == 2 * NT - 1))
                if s == 2 * NT - 1:
                    last.then_inc(bank_filled, 1)
                else:
                    last.then_inc(sem("onehots_used"), 1)
            pe.wait_ge(emptied["act"], act1)
            pe.wait_ge(emptied["dve"], dve1)

            h_done, y_done, xg_turned, g_turned = sem("h_done"), sem("y_done"), sem("xg_turned"), sem("g_turned")

            def turn_rows(q):
                for k in range(4):
                    last = pe.transpose(bank[q % 2][:, P * k:P * k + P], xg[q][:, k:512:4], ident)
                return last

            def hidden(b, slot):
                for n, (hf, k) in enumerate((hf, k) for hf in range(2) for k in range(4)):
                    for j in range(2):
                        w = as_expert(slot[j], j)[:, hf, 512 * k:512 * k + 512]
                        last = pe.matmul(bank[2 + b][64 * j:64 * j + 64, :], xgT[b][:, k, hf, :], w,
                                         start=(n == 0), stop=(n == 7), skip_group_check=True)
                return last

            def turn_gated(b):
                for k in range(4):
                    last = pe.transpose(bank[4 + b][:, SLOTS * k:SLOTS * k + SLOTS], gg[b][0:SLOTS, k:512:4],
                                        ident[0:SLOTS, 0:SLOTS])
                return last

            def down(b, slot):
                w = as_expert(slot[2], 2).rearrange("p (k n) -> p k n", k=4)
                for k in range(4):
                    for hf in range(2):
                        last = pe.matmul(bank[6 + b][64 * hf:64 * hf + 64, :], gT[b][:, k, :],
                                         w[:, k, 512 * hf:512 * hf + 512], start=(k == 0), stop=(k == 3),
                                         skip_group_check=True)
                return last

            def step_turn(i, q):
                pe.wait_ge(sem(f"xg_loaded{q}"), 16 * i + 16)
                turn_rows(q).then_inc(xg_turned, 1)

            def step_hidden(i, b):
                e = 2 * i + b
                pe.wait_ge(sem("xgT_ready"), e + 1)
                for j in range(2):
                    pe.wait_ge(we_loaded[b][j], 16 * i + 16)
                hidden(b, w_slot[b]).then_inc(h_done, 1)

            def step_down(i, b, first=False):
                e = 2 * i + b
                pe.wait_ge(sem("gT_ready"), e + 1)
                pe.wait_ge(we_loaded[b][2], 16 * i + 16)
                if not first:
                    pe.wait_ge(sem("y_ready"), e - 1)
                down(b, w_slot[b]).then_inc(y_done, 1)

            def step_gated(i, b):
                pe.wait_ge(sem("consts_loaded"), 64)
                pe.wait_ge(sem("g_ready"), 2 * i + b + 1)
                turn_gated(b).then_inc(g_turned, 1)

            def pair(j, half, first=False, last=False, second=False):
                i = 2 * j + half
                step_hidden(i, 0)
                step_turn(j, 2 * half + 1)
                if not first:
                    step_down(i - 1, 1, first=second)
                step_gated(i, 0)
                step_hidden(i, 1)
                if not last:
                    step_turn(j + half, 2 - 2 * half)
                step_down(i, 0, first=first)
                step_gated(i, 1)

            step_turn(0, 0)
            pair(0, 0, first=True)
            pair(0, 1, second=True)
            with pe.Fori(1, EXPERTS // 4 - 1) as j:
                pair(j, 0)
                pair(j, 1)
            pair(EXPERTS // 4 - 1, 0)
            pair(EXPERTS // 4 - 1, 1, last=True)
            step_down(EXPERTS // 2 - 1, 1)
            pe.wait_ge(sem("y_ready"), EXPERTS)

            wait_emptied(pe, U["table",])
            n = pe.value_load(over_n, min_val=0, max_val=OVER)
            with pe.If(n > 0):
                with pe.Fori(0, OVER) as k:
                    pe.wait_ge(sem("ov_xg_loaded0"), 16 * k + 16)
                    turn_rows(0).then_inc(sem("ov_xg_turned"), 1)
                    pe.wait_ge(sem("ov_xgT_ready"), k + 1)
                    pe.wait_ge(sem("ov_w_loaded"), 48 * k + 48)
                    hidden(0, over_slot).then_inc(sem("ov_h_done"), 1)
                    pe.wait_ge(sem("consts_loaded"), 64)
                    pe.wait_ge(sem("ov_g_ready"), k + 1)
                    turn_gated(0).then_inc(sem("ov_g_turned"), 1)
                    pe.wait_ge(sem("ov_gT_ready"), k + 1)
                    down(0, over_slot).then_inc(sem("ov_y_done"), 1)
                    pe.wait_ge(sem("ov_stored"), 16 * k + 16)
            pe.nop().then_inc(sem("pe_left_experts"), 1)

            done[0] = 0

            def chunk_b(c):
                pe.wait_ge(w2_loaded[c % RING], w2_value(c))
                return w_at(2, c)

            turn(V, "x4_t", xn, sem("x4n_ready"), 0)
            wait_emptied(pe, V["x4_t", 6])
            wait_emptied(pe, V["x4_t", 7])
            for j in range(KD):
                w = chunk_b(ch2["a0"] + j)
                for f, name in ((1, "c"), (2, "u"), (3, "z"), (0, "b")):
                    gemm(fill(V, name, j)[:, :], lambda k: w[:, k, P * f:P * f + P], lambda k: hT[:, k, :])
            wait_emptied(pe, V["b", KD - 1])
            for n in range(2):
                w = chunk_b(ch2["wa0"] + n)
                for t in range(NT):
                    gemm(fill(V, "wa", n, t)[:, :], lambda k: yT[:, k, P * t:P * t + P], lambda k: w[:, k, :])
            turn(V, "x5_t", xn, sem("x5n_ready"), 0)
            wait_emptied(pe, V["x5_t", KD - 1])
            w = chunk_b(ch2["kv"])
            for t in range(NT):
                gemm(fill(V, "kv", t)[:, :], lambda k: hkvT[:, k, P * t:P * t + P], lambda k: w[:, k, :])
            for n in range(2):
                w = chunk_b(ch2["q0"] + n)
                for t in range(NT):
                    gemm(fill(V, "q", n, t)[:, :], lambda k: hT[:, k, P * t:P * t + P], lambda k: w[:, k, :])
            for m in range(8):
                w = chunk_b(ch2["z0"] + m // 4)
                gemm(fill(V, "zz", m)[:, :], lambda k: w[:, k, P * (m % 4):P * (m % 4) + P], lambda k: hT[:, k, :])
            pe.wait_ge(sem("k2_ready"), 1)
            for g in range(WKV):
                o = fill(V, "k_t", g)
                for t in range(NT):
                    last = pe.transpose(o[:, P * t:P * t + P], k_dup[:, t, P * g:P * g + P], ident)
                last.then_inc(bank_filled, 1)
            pe.wait_ge(sem("q2_ready"), 1)
            for p in range(8):
                o = fill(V, "q_t", p)
                for t in range(NT):
                    last = pe.transpose(o[:, P * t:P * t + P], q_rows[:, t, P * p:P * p + P], ident)
                last.then_inc(bank_filled, 1)
            wait_emptied(pe, V["k_t", WKV - 1])
            wait_emptied(pe, V["q_t", 7])
            for i in range(16 + 2):
                if i < 16:
                    nb, g = divmod(i, WKV)
                    k0, n = (P * (nb - 1), 2 * P) if nb else (0, P)
                    for hh in range(2):
                        o = fill(V, "ws", i, hh)
                        r = slice(64 * hh, 64 * hh + 64)
                        for pr in range(2):
                            last = pe.matmul(o[:, 256 * pr:256 * pr + n], q2T[r, 2 * g + pr, P * nb:P * nb + P],
                                             k2T[r, g, k0:k0 + n], start=True, stop=True)
                        last.then_inc(bank_filled, 1)
                if i >= 2:
                    j = i - 2
                    nb, g = divmod(j, WKV)
                    pe.wait_ge(sem("wp_ready"), j + 1)
                    for kt in window_tiles(j):
                        o = fill(V, "wp", j, kt)
                        for q in range(4):
                            c0 = P * (kt - (nb == 0))
                            last = pe.transpose(o[:, P * q:P * q + P], wS[:, j % 3, q, c0:c0 + P], ident)
                        last.then_inc(bank_filled, 1)
                    o = fill(V, "wv", j)
                    kts = window_tiles(j)
                    wait_emptied(pe, V["wp", j, 1])
                    for n, kt in enumerate(kts):
                        for hh in range(2):
                            last = pe.matmul(o[64 * hh:64 * hh + 64, 0:256],
                                             v_rows2[:, nb - 1 + kt, WD * g:WD * g + WD],
                                             wpT[:, j % 2, kt, 256 * hh:256 * hh + 256], start=(n == 0),
                                             stop=(n == len(kts) - 1), skip_group_check=True)
                    last.then_inc(bank_filled, 1)
            wait_emptied(pe, V["wv", 15])
            for n in range(2):
                w = chunk_b(ch2["wb0"] + n)
                for t in range(NT):
                    gemm(fill(V, "wb", n, t)[:, :], lambda k: yT2[:, k, P * t:P * t + P], lambda k: w[:, k, :])


        @block.scalar
        def _(act):
            done = emptied["act"]

            def filled(u):
                act.wait_ge(bank_filled, u.filled)
                return bank[u.bank]

            summed = [0]

            def sums(src, t, c, out_=None):
                n = summed[0]
                summed[0] += 1
                if out_ is None:
                    act.wait_ge(sem("ss_ready"), n - 1)
                    out_ = E[:, D * (n % 2):D * (n % 2) + D]
                act.activation(out_, src[:, t, :], ACT.Square, accum_out=ss[:, c:c + 1]).then_inc(sem("ss_ready"), 1)

            def roots(n, c0, c1):
                act.wait_ge(sem("ms_ready"), n)
                act.activation(root[:, c0:c1], ms[:, c0:c1], ACT.Sqrt).then_inc(sem("root_ready"), 1)

            def to_cols(us, name, gain):
                for k in range(0, KD, 2):
                    o = filled(us[name, k])
                    act.activation(hT[:, k, :], o[:, :], ACT.Copy, scale=gain[:, k:k + 1]).then_inc(done, 1)

            for t in range(NT):
                act.wait_ge(sem(f"x_loaded{t}"), 16)
                sums(x_rows, t, t, xn[:, t, :])
            roots(1, 0, NT)
            act.wait_ge(sem("consts_loaded"), 64)
            to_cols(U, "x_t", g_mix)

            act.wait_ge(sem("gate_abs_ready"), 1)
            act.activation(g_ex, g_l, ACT.Exp).then_inc(act_step, 1)
            act.wait_ge(act_step, 1)
            act.activation(g_l, g_ex, ACT.Ln, bias=1.0).then_inc(sem("gate_log_ready"), 1)
            act.wait_ge(sem("lam_sum_ready"), 1)
            act.activation(lam_s[:, 2:4], lam_s[:, 0:2], ACT.Exp).then_inc(sem("lam_exp_ready"), 1)

            for j in range(2 * HEADS):
                o = filled(U["qk", j])
                act.activation(qkT[:, j, :], o[:, :], ACT.Copy).then_inc(done, 1)
            for t in range(NT):
                o = filled(U["dv", t])
                act.activation(dv_rows[:, t, :], o[:, :], ACT.Copy).then_inc(done, 1)
            act.wait_ge(sem("qk_rotated"), 2 * HEADS)
            for i in range(16 + 2):
                if i < 16:
                    h, qb = divmod(i, NT)
                    n = P * (qb + 1)
                    act.wait_ge(sem("da_max_ready"), i + 1)
                    if i >= 2:
                        act.wait_ge(bank_filled, U["da_t", i - 2].filled)
                    for m in range(2):
                        c = 2 * (i % 2) + m
                        o = filled(U["ds", i, m])
                        act.activation(e_buf[:, i % 2, m, 0:n], o[:, 0:n], ACT.Exp, bias=neg[:, c:c + 1],
                                       scale=DA_DIM ** -0.5, accum_out=zsum[:, c:c + 1]).then_inc(done, 1)
                    if i < 8:
                        o = filled(U["proj", i])
                        act.activation(mqkT[:, i, :], o[:, :], ACT.Copy).then_inc(done, 1)
                    elif i >= 12:
                        o = filled(U["proj", i])
                        act.activation(moT[:, i - 12, :], o[:, :], ACT.Copy).then_inc(done, 1)
                if i >= 2:
                    j = i - 2
                    h, qb = divmod(j, NT)
                    o = filled(U["do", j])
                    act.activation(o_rows[:, qb, h, :], o[:, 0:P], ACT.Copy).then_inc(act_step, 1)
                    act.wait_ge(act_step, 2 + j)
                    act.activation(o[:, 0:P], o[:, 0:P], ACT.Square, accum_out=ss[:, 32 + j:33 + j]).then_inc(done, 1)
                if i == 11:
                    act.wait_ge(sem("conv_done"), 8)
                    for m in range(8):
                        act.activation(mqkT[:, m, :], mqkT[:, m, :], ACT.Silu).then_inc(sem("silu_ready"), 1)

            wait_emptied(act, U["gates_t",])
            act.activation(em, mT, ACT.Exp, scale=-1.0).then_inc(sem("em_ready"), 1)
            for h in range(HEADS):
                o = filled(U["m_row", h])
                act.wait_ge(sem("diag_ready"), h + 1)
                for kb in range(NT):
                    n = NT * h + kb
                    if n >= 2:
                        wait_emptied(act, U[("ms",) + divmod(n - 2, NT)])
                    bias = bT[:, 4 * kb + h:4 * kb + h + 1]
                    if kb < NT - 1:
                        rest = act.activation(d_buf[:, n % 2, P:SEQ - P * kb], o[:, P * kb + P:SEQ], ACT.Exp, bias=bias)
                        if kb == NT - 2:
                            rest.then_inc(done, 1)
                    act.activation(d_buf[:, n % 2, 0:P], arg_diag[:, h % 2, P * kb:P * kb + P], ACT.Exp,
                                   bias=bias).then_inc(sem("d_ready"), 1)
            wait_emptied(act, U["proj", 15])
            for m in range(HEADS):
                act.activation(moT[:, m, :], moT[:, m, :], ACT.Sigmoid).then_inc(sem("sig_ready"), 1)
            roots(2, 32, 64)

            act.wait_ge(sem("mem_loaded"), 16)
            for t in range(MT):
                sums(mem_rows, t, NT + t)
            roots(3, NT, NT + MT)
            for t in range(NT):
                wait_emptied(act, U["wo", 1, t])
                sums(x_rows, t, 8 + t)
            roots(4, 8, 8 + NT)
            for m in range(8):
                o = filled(U["xk", m])
                act.activation(xkT[:, m, :], o[:, 0:MEM], ACT.Copy).then_inc(done, 1)
            for n in range(2):
                for t in range(MT):
                    o = filled(U["xv", n, t])
                    act.activation(xv_rows[:, t, 512 * n:512 * n + 512], o[:, :], ACT.Copy).then_inc(done, 1)
            act.wait_ge(sem("more_loaded"), 16 * 8)
            to_cols(U, "x1_t", g_x)
            for m in range(8):
                o = filled(U["xq", m])
                act.activation(xqT[:, m, :], o[:, :], ACT.Copy).then_inc(done, 1)
            for i in range(16 + 2):
                if i < 16:
                    o = filled(U["xs", i])
                    act.wait_ge(sem("xmax_ready"), i + 1)
                    if i >= 4:
                        act.wait_ge(bank_filled, U["xp", i - 4].filled)
                    c = i % 8
                    act.activation(xe[:, i % 4, :], o[:, 0:MEM], ACT.Exp, bias=neg[:, c:c + 1], scale=1.0 / 16,
                                   accum_out=zsum[:, c:c + 1]).then_inc(done, 1)
                if i >= 2 and (i - 2) % NT == NT - 1:
                    for d in range(2):
                        o = filled(U["xo", (i - 2) // NT, d])
                        act.activation(yT[:, 2 * ((i - 2) // NT) + d, :], o[:, :], ACT.Copy).then_inc(done, 1)
            for t in range(NT):
                wait_emptied(act, U["xw", 1, t])
                sums(x_rows, t, 12 + t)
            roots(5, 12, 12 + NT)
            to_cols(U, "x2_t", g_ffn)
            act.wait_ge(sem("dif_ready"), 1)
            act.activation(pexp, dif, ACT.Exp).then_inc(sem("pexp_ready"), 1)

            h_done, g_turned = sem("h_done"), sem("g_turned")

            def silu(b):
                return act.activation(sil[b][SLOTS:P, :], bank[2 + b][0:SLOTS, :], ACT.Silu)

            def gated_cols(b):
                return act.activation(gT[b], bank[4 + b][:, 0:4 * SLOTS].rearrange("p (k s) -> p k s", k=4), ACT.Copy)

            def pair(i, first=False):
                for b in range(2):
                    e = 2 * i + b
                    act.wait_ge(h_done, e + 1)
                    if not first:
                        act.wait_ge(sem("g_ready"), e - 1)
                    silu(b).then_inc(sem("silu_e_ready"), 1)
                    act.wait_ge(g_turned, e + 1)
                    if not first:
                        act.wait_ge(sem("y_done"), e - 1)
                    gated_cols(b).then_inc(sem("gT_ready"), 1)

            pair(0, True)
            with act.Fori(1, EXPERTS // 2) as i:
                pair(i)
            act.wait_ge(sem("y_done"), EXPERTS)
            wait_emptied(act, U["table",])
            n = act.value_load(over_n, min_val=0, max_val=OVER)
            with act.If(n > 0):
                with act.Fori(0, OVER) as k:
                    act.wait_ge(sem("ov_h_done"), k + 1)
                    silu(0).then_inc(sem("ov_silu_ready"), 1)
                    act.wait_ge(sem("ov_g_turned"), k + 1)
                    gated_cols(0).then_inc(sem("ov_gT_ready"), 1)
                    act.wait_ge(sem("ov_stored"), 16 * k + 16)

            for t in range(NT):
                act.wait_ge(sem("x3_ready"), t + 1)
                sums(x_rows, t, 16 + t)
            roots(6, 16, 16 + NT)
            for t in range(NT):
                act.wait_ge(sem("x4_ready"), t + 1)
                sums(x_rows, t, 20 + t)
            roots(7, 20, 20 + NT)
            to_cols(V, "x4_t", g_a)
            for j in range(KD):
                o = filled(V["c", j])
                if j >= 2:
                    wait_emptied(act, V["u", j - 2])
                act.activation(cbuf[:, j % 2, :], o[:, :], ACT.Copy).then_inc(done, 1)
                o = filled(V["z", j])
                if j >= 2:
                    wait_emptied(act, V["b", j - 2])
                act.activation(zbuf[:, j % 2, :], o[:, :], ACT.Silu).then_inc(done, 1)
            for t in range(NT):
                wait_emptied(act, V["wa", 1, t])
                sums(x_rows, t, 24 + t)
            roots(8, 24, 24 + NT)
            for t in range(NT):
                o = filled(V["kv", t])
                act.activation(k_rows[:, WKV * t:WKV * t + WKV, :], o[:, 0:256].rearrange("p (g d) -> p g d", g=WKV),
                               ACT.Copy)
                act.activation(v_rows2[:, t, :], o[:, 256:512], ACT.Copy)
                act.activation(sq_buf[:, t, 0:256], o[:, 0:256], ACT.Square).then_inc(done, 1)
            for n in range(2):
                for t in range(NT):
                    o = filled(V["q", n, t])
                    act.wait_ge(sem("sq_used"), NT * n + t + 1)
                    act.activation(q_rows[:, t, 512 * n:512 * n + 512], o[:, :], ACT.Copy)
                    act.activation(sq_buf[:, t, :], o[:, :], ACT.Square).then_inc(done, 1)
            roots(9, 0, 80)
            for m in range(8):
                o = filled(V["zz", m])
                act.activation(zT[:, m, :], o[:, :], ACT.Silu).then_inc(done, 1)
            for p in range(8):
                o = filled(V["q_t", p])
                act.activation(q2T[:, p, :], o[:, :], ACT.Copy).then_inc(done, 1)
            for i in range(16 + 2):
                if i < 16:
                    n = 2 * P if i // WKV else P
                    act.wait_ge(sem("w_max_ready"), i + 1)
                    for q in range(4):
                        c = 8 * (i % 2) + q
                        act.activation(wS[:, i % 3, q, 0:n], wS[:, i % 3, q, 0:n], ACT.Exp, bias=neg[:, c:c + 1],
                                       accum_out=zsum[:, c:c + 1])
                    c = 4 * (i % 2)
                    act.activation(stat[:, 16 + c:20 + c], stat[:, c:c + 4], ACT.Exp).then_inc(sem("w_exp_ready"), 1)
                if i >= 2:
                    j = i - 2
                    if j >= 2:
                        act.wait_ge(bank_filled, V["wv", j - 2].filled)
                    for kt in window_tiles(j):
                        o = filled(V["wp", j, kt])
                        act.activation(wpT[:, j % 2, kt, :], o[:, :], ACT.Copy).then_inc(done, 1)

        @block.vector
        def _(dve):
            done = emptied["dve"]

            def filled(u):
                dve.wait_ge(bank_filled, u.filled)
                return bank[u.bank]

            def own(ins):
                then_own(dve, ins, dve_step, dve_n)

            ss_total, ms_total = [0], [0]

            def rstds(n_sums, spans):
                ss_total[0] += n_sums
                ms_total[0] += 1
                if n_sums:
                    dve.wait_ge(sem("ss_ready"), ss_total[0])
                for c0, c1, width in spans:
                    last = dve.tensor_scalar(ms[:, c0:c1], ss[:, c0:c1], 1.0 / width, EPS, ALU.mult, ALU.add)
                last.then_inc(sem("ms_ready"), 1)
                dve.wait_ge(sem("root_ready"), ms_total[0])
                own(dve.reciprocal(rstd[:, spans[0][0]:spans[-1][1]], root[:, spans[0][0]:spans[-1][1]]))

            def normalise(c0, ready):
                for t in range(NT):
                    dve.tensor_scalar(xn[:, t, :], x_rows[:, t, :], rstd[:, c0 + t:c0 + t + 1], None, ALU.mult)\
                       .then_inc(ready, 1)

            def to_cols(us, name, gain):
                for k in range(1, KD, 2):
                    o = filled(us[name, k])
                    dve.tensor_scalar(hT[:, k, :], o[:, :], gain[:, k:k + 1], None, ALU.mult).then_inc(done, 1)

            rstds(NT, [(0, NT, D)])
            normalise(0, sem("x0n_ready"))
            dve.wait_ge(sem("consts_loaded"), 64)
            to_cols(U, "x_t", g_mix)

            for g, dst in enumerate((g_i, g_f)):
                o = filled(U["gate", "if"[g]])
                dve.tensor_scalar(dst, o[0:HEADS, :], gate_b[0:HEADS, g:g + 1], None, ALU.add).then_inc(done, 1)
            wait_emptied(dve, U["gate", "f"])
            dve.tensor_scalar(g_min, g_f, 0.0, None, ALU.min)
            dve.scalar_tensor_tensor(g_l, g_f, -1.0, g_f, ALU.mult, ALU.min).then_inc(sem("gate_abs_ready"), 1)
            dve.wait_ge(sem("more_loaded2"), 16 * N_MORE)
            for m in range(2):
                last = dve.tensor_tensor_reduce(rw[:, 64 * m:64 * m + 64], lam_in[:, P * m:P * m + DA_DIM],
                                                lam_in[:, P * m + DA_DIM:P * m + P], 1.0, 0.0, ALU.mult, ALU.add,
                                                lam_s[:, m:m + 1])
            last.then_inc(sem("lam_sum_ready"), 1)
            dve.tensor_scalar(g_sub_s, g_sub, 1.0 - LAM_INIT, None, ALU.mult)
            dve.wait_ge(sem("gate_log_ready"), 1)
            own(dve.tensor_tensor(g_f, g_min, g_l, ALU.subtract))
            own(dve.memset(g_min, 0.0))
            own(dve.tensor_tensor_scan(g_a_sum, g_f, g_min, 0.0, ALU.add, ALU.add))
            own(dve.tensor_tensor(g_bb, g_i, g_a_sum, ALU.subtract))
            own(dve.tensor_tensor_scan(g_M, g_min, g_bb, 0.0, ALU.add, ALU.max))
            dve.tensor_tensor(g_ex, g_M, g_a_sum, ALU.add).then_inc(sem("gates_ready"), 1)
            dve.wait_ge(sem("lam_exp_ready"), 1)
            own(dve.tensor_tensor(neg_lam, lam_s[:, 3:4], lam_s[:, 2:3], ALU.subtract))
            own(dve.tensor_scalar(neg_lam, neg_lam, -LAM_INIT, None, ALU.add))

            for j in range(2 * HEADS):
                o = filled(U["qk_rot", j])
                dve.tensor_tensor(rope_tmp, o[:, :], sinT, ALU.mult).then_inc(done, 1)
                own(dve.tensor_tensor(qkT[:, j, :], qkT[:, j, :], cosT, ALU.mult))
                dve.tensor_tensor(qkT[:, j, :], qkT[:, j, :], rope_tmp, ALU.add).then_inc(sem("qk_rotated"), 1)
                dve.wait_ge(sem("qk_rotated"), j + 1)

            def conv(j):
                wait_emptied(dve, U["proj", j])
                w = lambda tap: conv_w[:, KD * tap + j:KD * tap + j + 1]
                acc = conv_tmp[:, j % 2, :]
                own(dve.tensor_scalar(acc, convT[:, j, 0:SEQ], w(0), conv_b[:, j:j + 1], ALU.mult, ALU.add))
                for tap in range(1, CONV1 - 1):
                    own(dve.scalar_tensor_tensor(acc, convT[:, j, tap:tap + SEQ], w(tap), acc, ALU.mult, ALU.add))
                dve.scalar_tensor_tensor(mqkT[:, j, :], mqkT[:, j, :], w(CONV1 - 1), acc, ALU.mult, ALU.add)\
                   .then_inc(sem("conv_done"), 1)

            dve.wait_ge(sem("pads_zero"), 2)
            for i in range(16 + 2):
                if i < 16:
                    h, qb = divmod(i, NT)
                    n = P * (qb + 1)
                    c = 2 * (i % 2)
                    for m in range(2):
                        o = filled(U["ds", i, m])
                        last = dve.tensor_tensor(o[:, n - P:n], o[:, n - P:n], const("mask_qk"), ALU.add)
                    own(last)
                    for m in range(2):
                        last = dve.tensor_reduce(mx[:, c + m:c + m + 1], bank[U["ds", i, m].bank][:, 0:n], AX.X, ALU.max)
                    own(last)
                    dve.tensor_scalar(neg[:, c:c + 2], mx[:, c:c + 2], -(DA_DIM ** -0.5), None, ALU.mult)\
                       .then_inc(sem("da_max_ready"), 1)
                    if 8 <= i < 12:
                        o = filled(U["proj", i])
                        dve.tensor_copy(mv_rows[:, i - 8, :, 0:P], o[:, :].rearrange("p (h d) -> p h d", h=HEADS))\
                           .then_inc(done, 1)
                if 1 <= i <= 16:
                    j = i - 1
                    h, qb = divmod(j, NT)
                    n, c = P * (qb + 1), 2 * (j % 2)
                    wait_emptied(dve, U["ds", j, 1])
                    own(dve.reciprocal(rz[:, c:c + 2], zsum[:, c:c + 2]))
                    own(dve.tensor_tensor(rz[:, c + 1:c + 2], rz[:, c + 1:c + 2], neg_lam, ALU.mult))
                    e0, e1 = e_buf[:, j % 2, 0, 0:n], e_buf[:, j % 2, 1, 0:n]
                    own(dve.tensor_scalar(e0, e0, rz[:, c:c + 1], None, ALU.mult))
                    dve.scalar_tensor_tensor(e0, e1, rz[:, c + 1:c + 2], e0, ALU.mult, ALU.add)\
                       .then_inc(sem("da_ready"), 1)
                    if j < 8:
                        conv(j)
                    o = filled(U["da_t", j])
                    if j >= 2:
                        dve.wait_ge(bank_filled, U["do", j - 2].filled)
                    dve.tensor_copy(daT[:, j % 2, 0:qb + 1, :], o[:, 0:n].rearrange("p (k q) -> p k q", q=P))\
                       .then_inc(done, 1)

            o = filled(U["gates_t",])
            dve.tensor_copy(bmT, o[:, 0:32]).then_inc(done, 1)
            dve.wait_ge(sem("em_ready"), 1)
            bn, mv, t2 = stat[:, 32:38], stat[:, 0:32], stat[:, 40:44]
            for h in range(HEADS):
                o = filled(U["m_row", h])
                dve.tensor_tensor(arg_diag[:, h % 2, :].rearrange("p (k q) -> p k q", k=NT),
                                  o[:, :].rearrange("p (k q) -> p k q", k=NT),
                                  const("mask_kq").unsqueeze(1).to_broadcast([P, NT, P]), ALU.add)\
                   .then_inc(sem("diag_ready"), 1)
                for kb in range(NT):
                    o = filled(U["ms", h, kb])
                    dve.wait_ge(sem("d_ready"), NT * h + kb + 1)
                    n = SEQ - P * kb
                    dve.scalar_tensor_tensor(sdT[:, h % 2, kb, P * kb:SEQ], o[:, P * kb:SEQ], float(P) ** -0.5,
                                             d_buf[:, (NT * h + kb) % 2, 0:n], ALU.mult, ALU.mult).then_inc(done, 1)
                for qb in range(NT):
                    o = filled(U["mh", h, qb])
                    c = NT * h + qb
                    own(dve.tensor_copy(t2[:, 3:4], o[:, P:P + 1]))
                    own(dve.scalar_tensor_tensor(t2[:, 0:1], t2[:, 3:4], -1.0, t2[:, 3:4], ALU.mult, ALU.max))
                    own(dve.tensor_scalar(t2[:, 1:2], t2[:, 0:1], em[:, 4 * qb + h:4 * qb + h + 1], None, ALU.max))
                    own(dve.reciprocal(t2[:, 2:3], t2[:, 1:2]))
                    dve.tensor_scalar(hm_rows[:, qb, h, :], o[:, 0:P], t2[:, 2:3], None, ALU.mult).then_inc(done, 1)
                    wait_emptied(dve, U["mh", h, qb])
                    own(dve.bn_stats(bn, hm_rows[:, qb, h, :]))
                    own(dve.bn_aggr(mv[:, 2 * c:2 * c + 2], bn))

            wait_emptied(dve, U["do", 15])
            own(dve.tensor_scalar(ss[:, 48:64], mv[:, 1:32:2], float(P), None, ALU.mult))
            rstds(0, [(32, 64, P)])
            for m in range(4):
                v = o_rows[:, :, m, :]
                r = rstd[:, 32 + 4 * m:36 + 4 * m].unsqueeze(2).to_broadcast([P, NT, P])
                dve.tensor_tensor(v, v, r, ALU.mult).then_inc(sem("y_rows_ready"), 1)
            for h in range(HEADS):
                for t in range(NT):
                    c = NT * h + t
                    last = dve.tensor_scalar(hm_rows[:, t, h, :], hm_rows[:, t, h, :], mv[:, 2 * c:2 * c + 1],
                                             rstd[:, 48 + c:49 + c], ALU.subtract, ALU.mult)
                last.then_inc(sem("y_rows_ready"), 1)
            for m in range(8):
                o = filled(U["y_t", m])
                if m < 4:
                    dve.tensor_scalar(yT[:, m, :], o[:, :], g_sub_s, None, ALU.mult).then_inc(done, 1)
                else:
                    dve.wait_ge(sem("sig_ready"), m - 3)
                    dve.scalar_tensor_tensor(yT[:, m, :], o[:, :], g_ml[:, m - 4:m - 3], moT[:, m - 4, :],
                                             ALU.mult, ALU.mult).then_inc(done, 1)

            rstds(MT, [(NT, NT + MT, D)])
            for t in range(MT):
                dve.tensor_scalar(mem_rows[:, t, :], mem_rows[:, t, :], rstd[:, NT + t:NT + t + 1], None, ALU.mult)\
                   .then_inc(sem("memn_ready"), 1)

            def add_rows(us, name):
                for n in range(2):
                    for t in range(NT):
                        o = filled(us[name, n, t])
                        v = x_rows[:, t, 512 * n:512 * n + 512]
                        dve.tensor_tensor(v, o[:, :], v, ALU.add).then_inc(done, 1)

            dve.wait_ge(sem("x_again"), 16 * NT)
            add_rows(U, "wo")
            dve.wait_ge(sem("more_loaded"), 16 * 8)
            for k in range(KD // 2):
                o = filled(U["mem_t", k])
                g = g_mem[:, 2 * k:2 * k + 2].unsqueeze(2).to_broadcast([P, 2, MEM])
                dve.tensor_tensor(memT[:, 2 * k:2 * k + 2, :], o[:, :].rearrange("p (k t) -> p k t", k=2), g, ALU.mult)\
                   .then_inc(done, 1)
            rstds(NT, [(8, 8 + NT, D)])
            normalise(8, sem("x1n_ready"))
            to_cols(U, "x1_t", g_x)

            for i in range(16 + 2):
                if i < 16:
                    o = filled(U["xs", i])
                    c = i % 8
                    own(dve.tensor_reduce(mx[:, c:c + 1], o[:, 0:MEM], AX.X, ALU.max))
                    dve.tensor_scalar(neg[:, c:c + 1], mx[:, c:c + 1], -1.0 / 16, None, ALU.mult)\
                       .then_inc(sem("xmax_ready"), 1)
                if 1 <= i <= 16:
                    j = i - 1
                    c = j % 8
                    wait_emptied(dve, U["xs", j])
                    own(dve.reciprocal(rz[:, c:c + 1], zsum[:, c:c + 1]))
                    dve.tensor_scalar(xe[:, j % 4, :], xe[:, j % 4, :], rz[:, c:c + 1], None, ALU.mult)\
                       .then_inc(sem("xp_ready"), 1)
                if i >= 2:
                    j = i - 2
                    h, t = divmod(j, NT)
                    o = filled(U["xp", j])
                    if h >= 2 and t == 0:
                        dve.wait_ge(bank_filled, U["xo", h - 2, 1].filled)
                    dve.tensor_copy(pT[:, h % 2, :, P * t:P * t + P], o[:, 0:MEM].rearrange("p (k q) -> p k q", q=P))\
                       .then_inc(done, 1)
            add_rows(U, "xw")
            rstds(NT, [(12, 12 + NT, D)])
            normalise(12, sem("x2n_ready"))
            to_cols(U, "x2_t", g_ffn)

            for t in range(NT):
                own(dve.memset(lg[:, t, GROUPS:8], NEG))
            for t in range(NT):
                o = filled(U["route", t])
                own(dve.tensor_tensor(lg[:, t, 0:GROUPS], o[:, 0:GROUPS], router_b[:, 0:GROUPS], ALU.add))
                dve.tensor_tensor(lg[:, t, 8:40], o[:, GROUPS:GROUPS + EXPERTS], router_b[:, GROUPS:], ALU.add)\
                   .then_inc(done, 1)
                wait_emptied(dve, U["route", t])
                own(dve.max(top[:, t, 0:8], lg[:, t, 0:8]))
                own(dve.max_index(top_i[:, 16 * t:16 * t + 8], top[:, t, 0:8], lg[:, t, 0:8]))
                own(dve.tensor_copy(gf[:, t:t + 1], top_i[:, 16 * t:16 * t + 1]))
                own(dve.tensor_scalar(ohg, const("item_row")[:, 0:GROUPS], gf[:, t:t + 1], None, ALU.is_equal))
                own(dve.tensor_scalar(el[:, t, :], lg[:, t, 8:16], ohg[:, 0:1], None, ALU.mult))
                for g in range(1, GROUPS):
                    own(dve.scalar_tensor_tensor(el[:, t, :], lg[:, t, 8 + 8 * g:16 + 8 * g], ohg[:, g:g + 1],
                                                 el[:, t, :], ALU.mult, ALU.add))
                own(dve.max(top[:, t, 8:16], el[:, t, :]))
                own(dve.max_index(top_i[:, 16 * t + 8:16 * t + 16], top[:, t, 8:16], el[:, t, :]))
                own(dve.tensor_copy(ea[:, t:8:NT], top_i[:, 16 * t + 8:16 * t + 10]))
                own(dve.scalar_tensor_tensor(ea[:, t:8:NT], gf[:, t:t + 1].to_broadcast([P, 2]), float(PER_GROUP),
                                             ea[:, t:8:NT], ALU.mult, ALU.add))
                for c in range(2):
                    last = dve.tensor_scalar(sel1h[:, c, t, :], const("item_row")[:, 0:EXPERTS],
                                             ea[:, NT * c + t:NT * c + t + 1], None, ALU.is_equal)
                own(last)
                dve.tensor_tensor(selb[:, t, :], sel1h[:, 0, t, :], sel1h[:, 1, t, :], ALU.add)\
                   .then_inc(sem("chosen_ready"), 1)
                for c in range(2):
                    last = dve.tensor_scalar(dif[:, t, 8 * c:8 * c + 8], top[:, t, 8 * c:8 * c + 8],
                                             top[:, t, 8 * c:8 * c + 1], None, ALU.subtract)
            last.then_inc(sem("dif_ready"), 1)
            dve.wait_ge(sem("pexp_ready"), 1)
            own(dve.tensor_reduce(zg, pexp[:, :, 0:8], AX.X, ALU.add))
            own(dve.tensor_tensor(r4a, pexp[:, :, 8], pexp[:, :, 9], ALU.add))
            own(dve.tensor_tensor(r4b, r4a, zg, ALU.mult))
            own(dve.reciprocal(r4c, r4b))
            for c in range(2):
                last = dve.tensor_tensor(comb[:, NT * c:NT * c + NT], pexp[:, :, 8 + c], r4c, ALU.mult)
            own(last)
            for c in range(2):
                last = dve.tensor_scalar(toks[:, NT * c:NT * c + NT], const("tok_col"), SEQ * c - NOWHERE, None, ALU.add)
            own(last)
            for c in range(2):
                last = dve.tensor_scalar(tokg[:, NT * c:NT * c + NT], const("tok_col"), -NOWHERE, None, ALU.add)
            own(last)
            own(dve.tensor_scalar(half5[:, 0:1], const("half_col"), 0.5, None, ALU.mult))
            for t in range(NT):
                o = filled(U["rank", t])
                for c in range(2):
                    last = dve.tensor_tensor_reduce(junk32, o[:, 0:EXPERTS], sel1h[:, c, t, :], 1.0, 0.0, ALU.mult, ALU.add,
                                                    rk[:, NT * c + t:NT * c + t + 1])
                    if c == 0:
                        own(last)
                last.then_inc(done, 1)
                wait_emptied(dve, U["rank", t])
            o = filled(U["count",])
            dve.tensor_copy(cnt, o[:, 0:EXPERTS]).then_inc(done, 1)
            wait_emptied(dve, U["count",])
            own(dve.memset(zero32, 0.0))
            own(dve.tensor_scalar(nov, cnt, float(SLOTS), None, ALU.is_gt))
            for j in range(2, TILES):
                own(dve.scalar_tensor_tensor(nov, cnt, float(SLOTS * j), nov, ALU.is_gt, ALU.add))
            own(dve.tensor_tensor_scan(ovend, nov, zero32, 0.0, ALU.add, ALU.add))
            own(dve.tensor_tensor(ovbase, ovend, nov, ALU.subtract))
            own(dve.tensor_copy(over_n, ovend[0:1, EXPERTS - 1:EXPERTS]))
            own(dve.tensor_tensor(over_cmp.rearrange("p (k e) -> p k e", e=EXPERTS),
                                  const("item_row", 1)[:, 0:OVER + 1].unsqueeze(2).to_broadcast([1, OVER + 1, EXPERTS]),
                                  ovend[0:1, :].unsqueeze(1).to_broadcast([1, OVER + 1, EXPERTS]), ALU.is_ge))
            own(dve.tensor_reduce(over_row, over_cmp.rearrange("p (k e) -> p k e", e=EXPERTS), AX.X, ALU.add))
            own(dve.tensor_scalar(over_e[:, :], over_row, EXPERTS - 1.0, None, ALU.min))
            for c in range(2 * NT):
                own(dve.tensor_tensor_reduce(junk32, ovbase, sel1h[:, c // NT, c % NT, :], 1.0, 0.0, ALU.mult, ALU.add,
                                             ovb[:, c:c + 1]))
            jt = slot
            own(dve.tensor_scalar(jt, rk, float(SLOTS), None, ALU.is_ge))
            for j in range(2, TILES):
                own(dve.scalar_tensor_tensor(jt, rk, float(SLOTS * j), jt, ALU.is_ge, ALU.add))
            own(dve.tensor_tensor(item, jt, ovb, ALU.add))
            own(dve.scalar_tensor_tensor(item, item, EXPERTS - 1.0, ea, ALU.add, ALU.subtract))
            own(dve.tensor_scalar(ovb, jt, 1.0, None, ALU.min))
            own(dve.tensor_tensor(item, item, ovb, ALU.mult))
            own(dve.tensor_tensor(item, item, ea, ALU.add))
            own(dve.scalar_tensor_tensor(slot, jt, -float(SLOTS), rk, ALU.mult, ALU.add))
            for s in range(2 * NT):
                if s >= 2:
                    dve.wait_ge(sem("onehots_used"), s - 1)
                dve.tensor_scalar(oh_slot[s % 2], const("slot_row"), slot[:, s:s + 1], None, ALU.is_equal)
                for n, v in enumerate((tokg, toks, comb)):
                    last = dve.tensor_scalar(oh_item[s % 2][:, ITEMS * n:ITEMS * (n + 1)], const("item_row"),
                                             item[:, s:s + 1], v[:, s:s + 1], ALU.is_equal, ALU.mult)
                last.then_inc(sem("onehots_ready"), 1)
            o = filled(U["table",])
            dve.tensor_scalar(tab_g, o[:, 0:ITEMS], half5[:, 0:1], NOWHERE, ALU.add, ALU.add)
            dve.tensor_scalar(tab_s, o[:, ITEMS:2 * ITEMS], const("half_col"), NOWHERE, ALU.add, ALU.add)
            dve.tensor_copy(tab_w, o[:, 2 * ITEMS:3 * ITEMS]).then_inc(done, 1)
            wait_emptied(dve, U["table",])

            def rows_cols(b):
                g = g_xh.rearrange("p (h k) -> p k h", h=2).unsqueeze(3).to_broadcast([P, 4, 2, SLOTS])
                return dve.tensor_tensor(xgT[b], bank[b][:, :].rearrange("p (k h s) -> p k h s", k=4, h=2), g, ALU.mult)

            def gate_up(b):
                return dve.tensor_tensor(gg[b][0:SLOTS, :], sil[b][SLOTS:P, :], bank[2 + b][SLOTS:P, :], ALU.mult)

            def weigh(b, e):
                return dve.tensor_scalar(y_sb[b], bank[6 + b][:, :], tab_w[:, bass.ds(e, 1)], None, ALU.mult)

            def step_cols(i, b, first=False):
                e = 2 * i + b
                dve.wait_ge(sem("xg_turned"), e + 1)
                if not first:
                    dve.wait_ge(sem("h_done"), e - 1)
                rows_cols(b).then_inc(sem("xgT_ready"), 1)

            def step_gate(i, b, first=False):
                e = 2 * i + b
                dve.wait_ge(sem("silu_e_ready"), e + 1)
                if not first:
                    dve.wait_ge(sem("g_turned"), e - 1)
                gate_up(b).then_inc(sem("g_ready"), 1)

            def step_weigh(i, b, first=False):
                e = 2 * i + b
                dve.wait_ge(sem("y_done"), e + 1)
                if not first:
                    dve.wait_ge(sem(f"y_stored{b}"), 16 * i)
                weigh(b, e).then_inc(sem("y_ready"), 1)

            def pair(i, first, last, second=False):
                step_cols(i, 1, first)
                step_gate(i, 0, first)
                if not first:
                    step_weigh(i - 1, 1, second)
                if not last:
                    step_cols(i + 1, 0)
                step_gate(i, 1, first)
                step_weigh(i, 0, first)

            step_cols(0, 0, True)
            pair(0, True, False)
            pair(1, False, False, True)
            with dve.Fori(2, EXPERTS // 2 - 1) as i:
                pair(i, False, False)
            pair(EXPERTS // 2 - 1, False, True)
            step_weigh(EXPERTS // 2 - 1, 1)
            n = dve.value_load(over_n, min_val=0, max_val=OVER)
            with dve.If(n > 0):
                with dve.Fori(0, OVER) as k:
                    dve.wait_ge(sem("ov_xg_turned"), k + 1)
                    rows_cols(0).then_inc(sem("ov_xgT_ready"), 1)
                    dve.wait_ge(sem("ov_silu_ready"), k + 1)
                    gate_up(0).then_inc(sem("ov_g_ready"), 1)
                    dve.wait_ge(sem("ov_y_done"), k + 1)
                    weigh(0, k + EXPERTS).then_inc(sem("y_ready"), 1)
                    dve.wait_ge(sem("ov_stored"), 16 * k + 16)

            dve.wait_ge(sem("g_fin_loaded"), 16)
            for t in range(NT):
                dve.wait_ge(sem(f"y_back{t}"), 64)
                own(dve.tensor_tensor(x_rows[:, t, :], x_rows[:, t, :], y_back[t][:, 0, :], ALU.add))
                dve.tensor_tensor(x_rows[:, t, :], x_rows[:, t, :], y_back[t][:, 1, :], ALU.add)\
                   .then_inc(sem("x3_ready"), 1)
            rstds(NT, [(16, 16 + NT, D)])
            for t in range(NT):
                dve.scalar_tensor_tensor(x_rows[:, t, :], x_rows[:, t, :], rstd[:, 16 + t:17 + t], g_fin, ALU.mult,
                                         ALU.mult).then_inc(sem("x4_ready"), 1)
            rstds(NT, [(20, 20 + NT, D)])
            normalise(20, sem("x4n_ready"))
            for n in range(2):
                own(dve.memset(vbuf[:, n, 0:CONV2 - 1], 0.0))
            to_cols(V, "x4_t", g_a)
            for j in range(KD):
                v, acc = vbuf[:, j % 2, :], cacc[:, j % 2, :]
                w = lambda tap: conv_w2[:, KD * tap + j:KD * tap + j + 1]
                o = filled(V["u", j])
                wait_emptied(dve, V["c", j])
                dve.tensor_tensor(v[:, CONV2 - 1:], o[:, :], cbuf[:, j % 2, :], ALU.mult).then_inc(done, 1)
                wait_emptied(dve, V["u", j])
                own(dve.tensor_scalar(acc, v[:, 0:SEQ], w(0), None, ALU.mult))
                for tap in range(1, CONV2):
                    own(dve.scalar_tensor_tensor(acc, v[:, tap:tap + SEQ], w(tap), acc, ALU.mult, ALU.add))
                wait_emptied(dve, V["z", j])
                own(dve.tensor_tensor(acc, acc, zbuf[:, j % 2, :], ALU.mult))
                o = filled(V["b", j])
                dve.tensor_tensor(yT[:, j, :], o[:, :], acc, ALU.mult).then_inc(done, 1)
            add_rows(V, "wa")
            rstds(NT, [(24, 24 + NT, D)])
            normalise(24, sem("x5n_ready"))
            for k in range(KD):
                o = filled(V["x5_t", k])
                dve.tensor_scalar(hkvT[:, k, :], o[:, :], g_kv[:, k:k + 1], None, ALU.mult)
                dve.tensor_scalar(hT[:, k, :], o[:, :], g_b[:, k:k + 1], None, ALU.mult).then_inc(done, 1)
            for t in range(NT):
                wait_emptied(dve, V["kv", t])
                dve.tensor_reduce(ss[:, WKV * t:WKV * t + WKV], sq_buf[:, t, 0:256].rearrange("p (g d) -> p g d", d=WD),
                                  AX.X, ALU.add).then_inc(sem("sq_used"), 1)
            for n in range(2):
                for t in range(NT):
                    wait_emptied(dve, V["q", n, t])
                    c = 16 + WH * t + 8 * n
                    dve.tensor_reduce(ss[:, c:c + 8], sq_buf[:, t, :].rearrange("p (h d) -> p h d", d=WD), AX.X, ALU.add)\
                       .then_inc(sem("sq_used"), 1)
            dve.wait_ge(sem("sq_used"), 3 * NT)
            rstds(0, [(0, 80, WD)])

            def unit(v, c0, gain, n):
                own(dve.tensor_tensor(v, v, rstd[:, c0:c0 + n].unsqueeze(2).to_broadcast([P, n, WD]), ALU.mult))
                own(dve.tensor_tensor(v, v, gain.unsqueeze(1).to_broadcast([P, n, WD]), ALU.mult))

            def rope(v, n):
                for t in range(NT):
                    hd = v[:, n * t:n * t + n, :]
                    r1, r2 = hd[:, :, 0:ROT // 2], hd[:, :, ROT // 2:ROT]
                    cs = [const(x)[:, 8 * t:8 * t + 8].unsqueeze(1).to_broadcast([P, n, ROT // 2]) for x in ("cos2", "sin2")]
                    tmp = [f3(E, (n, ROT // 2), SEQ * s + 128 * (t % 4)) for s in range(4)]
                    dve.tensor_tensor(tmp[0], r1, cs[0], ALU.mult)
                    dve.tensor_tensor(tmp[1], r2, cs[1], ALU.mult)
                    dve.tensor_tensor(tmp[2], r2, cs[0], ALU.mult)
                    own(dve.tensor_tensor(tmp[3], r1, cs[1], ALU.mult))
                    dve.tensor_tensor(r1, tmp[0], tmp[1], ALU.subtract)
                    own(dve.tensor_tensor(r2, tmp[2], tmp[3], ALU.add))

            unit(k_rows, 0, k_gain, NT * WKV)
            rope(k_rows, WKV)
            dup = f3(B2, (NT * WKV, 2, WD))
            for c in range(2):
                last = dve.tensor_copy(dup[:, :, c, :], k_rows)
            last.then_inc(sem("k2_ready"), 1)
            qh = f3(XN, (NT * WH, WD))
            for t in range(NT):
                unit(qh[:, WH * t:WH * t + WH, :], 16 + WH * t, q_gain, WH)
            rope(qh, WH)
            dve.nop().then_inc(sem("q2_ready"), 1)
            for g in range(WKV):
                o = filled(V["k_t", g])
                dve.tensor_copy(k2T[:, g, :], o[:, :]).then_inc(done, 1)

            for i in range(16 + 3):
                if i < 16:
                    nb, g = divmod(i, WKV)
                    n = 2 * P if nb else P
                    S = wS[:, i % 3, :, 0:n]
                    band = const("band")[:, 2 * P - n:].unsqueeze(1).to_broadcast([P, 2, n])
                    if i >= 3:
                        dve.wait_ge(bank_filled, V["wp", i - 3, 1].filled)
                    for hh in range(2):
                        o = filled(V["ws", i, hh])
                        dve.scalar_tensor_tensor(S[:, 2 * hh:2 * hh + 2, :],
                                                 o[:, :].rearrange("p (r k) -> p r k", r=2)[:, :, 0:n], WD ** -0.5, band,
                                                 ALU.mult, ALU.add).then_inc(done, 1)
                    wait_emptied(dve, V["ws", i, 1])
                    c = 8 * (i % 2)
                    m4, n4 = mx[:, c:c + 4], neg[:, c:c + 4]
                    own(dve.tensor_reduce(m4, S, AX.X, ALU.max))
                    sk = sink[:, 4 * g:4 * g + 4].rearrange("p (r h) -> p h r", h=2)
                    own(dve.tensor_tensor(m4.rearrange("p (h r) -> p h r", h=2), m4.rearrange("p (h r) -> p h r", h=2), sk,
                                          ALU.max))
                    own(dve.tensor_scalar(n4, m4, -1.0, None, ALU.mult))
                    s4 = stat[:, 4 * (i % 2):4 * (i % 2) + 4]
                    dve.tensor_tensor(s4.rearrange("p (h r) -> p h r", h=2), n4.rearrange("p (h r) -> p h r", h=2), sk,
                                      ALU.add).then_inc(sem("w_max_ready"), 1)
                if 1 <= i <= 16:
                    j = i - 1
                    n = 2 * P if j // WKV else P
                    c = 8 * (j % 2)
                    dve.wait_ge(sem("w_exp_ready"), j + 1)
                    own(dve.tensor_tensor(rz[:, c:c + 4], zsum[:, c:c + 4], stat[:, 16 + 4 * (j % 2):20 + 4 * (j % 2)],
                                          ALU.add))
                    own(dve.reciprocal(rz[:, c + 4:c + 8], rz[:, c:c + 4]))
                    S = wS[:, j % 3, :, 0:n]
                    dve.tensor_tensor(S, S, rz[:, c + 4:c + 8].unsqueeze(2).to_broadcast([P, 4, n]), ALU.mult)\
                       .then_inc(sem("wp_ready"), 1)
                if 2 <= i <= 17:
                    j = i - 2
                    nb, g = divmod(j, WKV)
                    o = filled(V["wv", j])
                    wait_emptied(dve, V["zz", 7])
                    dve.tensor_tensor(yT2[:, 2 * g:2 * g + 2, P * nb:P * nb + P],
                                      o[:, 0:256].rearrange("p (r q) -> p r q", r=2),
                                      zT[:, 2 * g:2 * g + 2, P * nb:P * nb + P], ALU.mult).then_inc(done, 1)
            add_rows(V, "wb")


def kernel(**inputs):
    import concourse.bacc as bacc
    from concourse.bass_utils import run_bass_kernel_spmd

    nc = bacc.Bacc("TRN2", target_bir_lowering=False, num_devices=1)
    arrays, a = {}, {}
    given = {name: np.ascontiguousarray(inputs[name]) for name in INS}
    given.update(shape_constants())
    for name, v in given.items():
        arrays[f"in_{name}"] = v
        a[name] = nc.dram_tensor(f"in_{name}", v.shape, mybir.dt.from_np(v.dtype), kind="ExternalInput").ap()
    out = nc.dram_tensor("out_0", (1, SEQ, D), F32, kind="ExternalOutput").ap()
    build(nc, a, out)
    r = run_bass_kernel_spmd(nc, [arrays], core_ids=[0])
    return r.results[0]["out_0"]
```

```python
import math
from contextlib import ExitStack

import numpy as np

import concourse.bass as bass
from concourse import mybir

F32 = mybir.dt.float32
F32R = mybir.dt.float32r
I32 = mybir.dt.int32
U32 = mybir.dt.uint32
ALU = mybir.AluOpType
ACT = mybir.ActivationFunctionType
AX = mybir.AxisListType

P = 128
D = 1024
SEQ = 512
NT = SEQ // P
KD = D // P
MEM = 256
MT = MEM // P
HEADS = 4
DA_DIM = 64
LAM_INIT = 0.8 - 0.6 * math.exp(-0.0)
EPS = 1e-6
NEG = -1e30
CONV1 = 4
CONV2 = 3
GROUPS = 4
EXPERTS = 32
PER_GROUP = EXPERTS // GROUPS
FF = 512
SLOTS = 64
TILES = SEQ // SLOTS
OVER = 2 * SEQ // SLOTS - 1
ITEMS = EXPERTS + OVER
NOWHERE = 4096.0
WH = 16
WKV = 4
WD = 64
ROT = 16
CHUNK = 4096
HALF = CHUNK // 2
GATE_M = 36

CONST_COLS = [("ident", P), ("mask_qk", P), ("mask_kq", P), ("rot", P), ("before", P), ("ones", P),
              ("slot_row", P), ("item_row", ITEMS), ("tok_col", NT), ("band", 2 * P),
              ("cos2", NT * ROT // 2), ("sin2", NT * ROT // 2), ("half_col", 1)]
CONST_AT = {}
_n = 0
for _name, _c in CONST_COLS:
    CONST_AT[_name] = (_n, _c)
    _n += _c
CONST_N = _n


def shape_constants():
    c = np.zeros((P, CONST_N), np.float32)

    def put(name, a):
        at, n = CONST_AT[name]
        c[:, at:at + n] = np.asarray(a, np.float32).reshape(P, n)

    i = np.arange(P)
    put("ident", np.eye(P))
    put("mask_qk", np.where(i[None, :] <= i[:, None], 0.0, NEG))
    put("mask_kq", np.where(i[:, None] <= i[None, :], 0.0, NEG))
    rot = np.zeros((P, P))
    for base in (0, DA_DIM):
        for j in range(DA_DIM // 2):
            rot[base + DA_DIM // 2 + j, base + j] = -1.0
            rot[base + j, base + DA_DIM // 2 + j] = 1.0
    put("rot", rot)
    put("before", i[:, None] < i[None, :])
    put("ones", np.ones((P, P)))
    put("slot_row", np.broadcast_to(i % SLOTS, (P, P)))
    put("item_row", np.broadcast_to(np.arange(ITEMS), (P, ITEMS)))
    put("tok_col", i[:, None] + P * np.arange(NT)[None, :])
    q, k = i[:, None], np.arange(2 * P)[None, :]
    put("band", np.where((k <= q + P) & (k > q), 0.0, NEG))
    pos = np.arange(SEQ, dtype=np.float32)
    inv = np.float32(500000.0) ** (-np.arange(0, ROT, 2, dtype=np.float32) / np.float32(ROT))
    ang = (pos[:, None] * inv[None, :]).astype(np.float32)
    rows = lambda a: a.reshape(NT, P, ROT // 2).transpose(1, 0, 2).reshape(P, -1)
    put("cos2", rows(np.cos(ang)))
    put("sin2", rows(np.sin(ang)))
    put("half_col", (i >= SLOTS) * 2.0 * SEQ)
    inv = np.float32(10000.0) ** (-np.arange(0, DA_DIM, 2, dtype=np.float32) / np.float32(DA_DIM))
    ang = (pos[:, None] * inv[None, :]).astype(np.float32).T
    rope = np.concatenate([np.tile(np.cos(ang), (4, 1)), np.tile(np.sin(ang), (4, 1))], axis=1)
    pick = np.zeros((HEADS, HEADS, P), np.float32)
    for h in range(HEADS):
        pick[h, h, :] = -1.0
    return {"consts": c, "rope": rope.astype(np.float32), "pick": pick.reshape(HEADS, HEADS * P)}


def first_plan():
    plan = [(("x_t", k), "dve") for k in range(KD)]
    plan += [(("gate",), "dve")]
    for j in range(2 * HEADS):
        plan.append((("qk", j), "act"))
        if j >= 1:
            plan.append((("qk_rot", j - 1), "dve"))
    plan.append((("dv", 0), "act"))
    plan.append((("qk_rot", 2 * HEADS - 1), "dve"))
    plan += [(("dv", t), "act") for t in range(1, NT)]
    for i in range(16 + 2):
        if i < 16:
            plan += [(("ds", i, 0), "act"), (("ds", i, 1), "act")]
            plan.append((("proj", i), "dve" if 8 <= i < 12 else "act"))
        if 1 <= i <= 16:
            plan.append((("da_t", i - 1), "dve"))
        if i >= 2:
            plan.append((("do", i - 2), "act"))
    plan.append((("gates_t",), "dve"))
    for h in range(HEADS):
        plan.append((("m_row", h), "act"))
        for kb in range(NT):
            plan.append((("ms", h, kb), "dve"))
        for qb in range(NT):
            plan.append((("mh", h, qb), "dve"))
    plan += [(("y_t", m), "dve") for m in range(8)]
    plan += [(("wo", n, t), "dve") for n in range(2) for t in range(NT)]
    plan += [(("mem_t", k), "dve") for k in range(KD // 2)]
    plan += [(("xk", m), "act") for m in range(8)]
    plan += [(("xv", n, t), "act") for n in range(2) for t in range(MT)]
    plan += [(("x1_t", k), "dve") for k in range(KD)]
    plan += [(("xq", m), "act") for m in range(8)]
    for i in range(16 + 2):
        if i < 16:
            plan.append((("xs", i), "act"))
        if i >= 2:
            plan.append((("xp", i - 2), "dve"))
            if (i - 2) % NT == NT - 1:
                plan += [(("xo", (i - 2) // NT, d), "dve") for d in range(2)]
    plan += [(("xw", n, t), "dve") for n in range(2) for t in range(NT)]
    plan += [(("x2_t", k), "act" if k % 2 == 0 else "dve") for k in range(KD)]
    plan += [(("route", t), "dve") for t in range(NT)]
    plan += [(("rank", t), "dve") for t in range(NT)] + [(("count",), "dve")]
    plan += [(("table",), "dve")]
    return plan


def second_plan():
    plan = [(("x4_t", k), "dve") for k in range(KD)]
    for half in range(2):
        for name, by in (("c", "act"), ("u", "dve"), ("z", "act"), ("b", "dve")):
            plan += [((name, j), by) for j in range(4 * half, 4 * half + 4)]
    plan += [(("wa", n, t), "dve") for n in range(2) for t in range(NT)]
    plan += [(("x5_t", k), "dve") for k in range(KD)]
    plan += [(("kv", t), "act") for t in range(NT)]
    plan += [(("q", n, t), "act") for n in range(2) for t in range(NT)]
    plan += [(("zz", m), "act") for m in range(8)]
    plan += [(("k_t", g), "dve") for g in range(WKV)]
    plan += [(("q_t", p), "act") for p in range(8)]
    for i in range(16 + 2):
        if i < 16:
            plan += [(("ws", i, 0), "dve"), (("ws", i, 1), "dve")]
        if i >= 2:
            plan += [(("wp", i - 2, kt), "act") for kt in window_tiles(i - 2)]
            plan.append((("wv", i - 2), "dve"))
    plan += [(("wb", n, t), "dve") for n in range(2) for t in range(NT)]
    return plan


def window_tiles(i):
    return [0, 1] if i // WKV > 0 else [1]


class Use:

    def __init__(self, n, what, by, filled, after, of_engine):
        self.what, self.bank, self.by = what, n % 8, by
        self.filled = filled
        self.after = after
        self.emptied = of_engine


def number(plan, base, act0, dve0):
    uses, order, count = {}, [], {"act": act0, "dve": dve0}
    for n, (what, by) in enumerate(plan):
        count[by] += 1
        after = (order[n - 8].by, order[n - 8].emptied) if n >= 8 else None
        u = Use(n, what, by, base + n + 1, after, count[by])
        order.append(u)
        uses[what] = u
    return uses, count["act"], count["dve"]


N_MORE = 3 + 2 + CONV1 + 1 + CONV2 + 5

INS = ["x", "mem", "norm_mix_g", "w_in", "w_out", "da_lambda", "da_subln_g", "ml_conv_w", "ml_conv_b",
       "ml_gate_b", "ml_norm_g", "norm_x_g", "norm_mem_g", "w_xq", "w_xk", "w_xv", "w_xo", "norm_ffn_g",
       "w_router_group", "b_router_group", "w_router_expert", "b_router_expert", "w1", "w3", "w2",
       "norm_final_g", "ln_a_2", "w_in_a_2", "conv_a_2", "w_out_a_2", "ln_kv_2", "w_kv_2", "k_norm_2",
       "ln_b_2", "w_in_b_2", "q_norm_2", "sinks_2", "w_out_b_2"]


def build(nc, a, out):
    U, act1, dve1 = number(first_plan(), 0, 0, 0)
    n1 = len(first_plan())
    V, act2, dve2 = number(second_plan(), n1, act1, dve1)

    ctx = ExitStack()
    with ctx:
        def sb(name, cols, dt=F32, parts=P):
            return ctx.enter_context(nc.sbuf_tensor(name, [parts, cols], dt))

        sems = {}

        def sem(name):
            if name not in sems:
                sems[name] = ctx.enter_context(nc.semaphore(name))
            return sems[name]

        rounded = {}

        def region(name, cols):
            with ExitStack() as place:
                plain = place.enter_context(nc.sbuf_tensor(name, [P, cols], F32))
            rounded[name] = ctx.enter_context(nc.sbuf_tensor(f"{name}_rounded", [P, cols], F32R))
            return plain

        ring = [region(f"ring{i}", CHUNK) for i in range(5)]
        X = sb("X", NT * D)
        XN = region("XN", NT * D)
        HT = region("HT", KD * SEQ)
        A0 = region("A0", KD * SEQ)
        A1 = region("A1", KD * (SEQ + CONV1 - 1))
        B0 = sb("B0", NT * SEQ)
        B1 = sb("B1", NT * HEADS * (P + 1))
        B2 = sb("B2", NT * SEQ)
        E = region("E", NT * SEQ)
        cst = sb("cst", CONST_N)
        pick = sb("pick", HEADS * P, parts=HEADS)
        small = sb("small", 1472)
        ints = sb("ints", 2 * ITEMS + 8, dt=I32)

        bank = [ctx.enter_context(nc.psum_tensor(f"bank{i}", [P, 512], F32)) for i in range(8)]

        xn_dram = nc.dram_tensor("xn_dram", (2 * SEQ, 512), F32).ap()
        y_dram = nc.dram_tensor("y_dram", (4 * SEQ, 512), F32).ap()

        def const(name, rows=P):
            at, n = CONST_AT[name]
            return cst[0:rows, at:at + n]

        ident = const("ident")
        taken = [0]

        def col(n):
            at = taken[0]
            taken[0] += n
            assert taken[0] <= 1472
            return small[:, at:at + n]

        g_mix, g_x, g_mem, g_ffn, g_a, g_kv, g_b = (col(KD) for _ in range(7))
        g_xh = col(KD)
        g_sub, g_ml, conv_w, conv_b = col(1), col(HEADS), col(KD * CONV1), col(KD)
        gate_b = col(2)
        conv_w2 = col(KD * CONV2)
        lam_in, lam_c = col(4 * DA_DIM), col(8)
        router_b = col(GROUPS + EXPERTS)
        k_gain, q_gain, sink = col(WD), col(WD), col(WH)
        ss, ms, root, rstd = col(80), col(80), col(80), col(80)
        stat = col(96)
        mx, neg, zsum, rz = (col(16) for _ in range(4))
        bmT, em = col(32), col(16)
        bT, mT = bmT[:, 0:16], bmT[:, 16:32]
        lam_s, neg_lam, g_sub_s = lam_c[:, 0:4], lam_c[:, 4:5], lam_c[:, 5:6]

        def f3(t, shape, at=0):
            n = int(np.prod(shape))
            v = t[:, at:at + n]
            if len(shape) == 2:
                return v.rearrange("p (a b) -> p a b", a=shape[0])
            return v.rearrange("p (a b c) -> p a b c", a=shape[0], b=shape[1])

        x_rows, xn, hT = f3(X, (NT, D)), f3(XN, (NT, D)), f3(HT, (KD, SEQ))
        w_gates = E[:, 1024:1024 + 8 * KD].rearrange("p (k n) -> p k n", k=KD)
        w_gates_split = [f3(E, (KD, GATE_M), 1152 + KD * GATE_M * s) for s in range(2)]
        cosT, sinT = E[:, 0:SEQ], E[:, SEQ:2 * SEQ]
        qkT = f3(A0, (KD, SEQ))
        convT = f3(A1, (KD, SEQ + CONV1 - 1))
        mqkT = convT[:, :, CONV1 - 1:]
        dv_rows = f3(B0, (NT, SEQ))
        mv_rows = f3(B1, (NT, HEADS, P + 1))
        moT = f3(B2, (HEADS, SEQ))
        e_buf = f3(E, (2, 2, SEQ))
        yT = xn_cols = f3(XN, (KD, SEQ))
        rope_tmp = X[:, 0:SEQ]
        conv_tmp = f3(X, (2, SEQ), 0)
        daT = f3(X, (2, NT, P), 2 * SEQ)
        o_rows = f3(X, (NT, HEADS, P), 4 * SEQ)
        gw = [f3(XN, (1, SEQ), SEQ * i)[0:HEADS, 0, :] for i in range(8)]
        g_i, g_f, g_min, g_l, g_a_sum, g_bb, g_M, g_ex = gw
        d_buf = f3(A0, (2, SEQ), 0)
        arg_diag = f3(A0, (2, SEQ), 2 * SEQ)
        hm_rows = f3(A0, (NT, HEADS, P), 4 * SEQ)
        sdT = f3(HT, (2, NT, SEQ))
        mem_rows = f3(A1, (MT, D))
        memT, mem_lo = f3(A0, (KD, MEM)), f3(A0, (KD, MEM), KD * MEM)
        lowT = f3(ring[4], (KD, SEQ))
        hkv_lo, y2_lo = f3(A1, (KD, SEQ)), f3(A0, (KD, SEQ))
        xqT, xkT, xv_rows = f3(A0, (KD, SEQ)), f3(B2, (KD, MEM)), f3(B0, (MT, D))
        xe = f3(E, (4, MEM))
        pT = f3(B1, (2, MT, SEQ))
        w_slot = [[ring[1], ring[3], A1], [ring[0], ring[2], ring[4]]]
        over_slot = [HT, A0, XN]
        xg = [E[:, 0:512], E[:, 512:1024], B0[:, 1536:2048], B2[:, 1024:1536]]
        y_sb = [E[:, 1024:1536], E[:, 1536:2048]]
        xgT = [f3(B0, (4, 2, SLOTS), 512 * b) for b in range(2)]
        gT = [f3(B0, (4, SLOTS), 1024 + 256 * b) for b in range(2)]
        sil = [B1[:, 0:512], B1[:, 512:1024]]
        gg = [B1[:, 1024:1536], B1[:, 1536:2048]]
        tab = B2[:, 0:3 * ITEMS]
        tab_w = B2[:, 2 * ITEMS:3 * ITEMS]
        router_w = f3(B2, (KD, GROUPS + EXPERTS), 256)
        sel1h = f3(B2, (2, NT, EXPERTS), 600)
        selb = f3(B2, (NT, EXPERTS), 860)
        rw = B2[:, 1000:2048]
        tab_g, tab_s = ints[:, 0:ITEMS], ints[:, ITEMS:2 * ITEMS]
        idx_g = [ints[:, 2 * ITEMS + q:2 * ITEMS + q + 1] for q in range(4)]
        idx_s = [ints[:, 2 * ITEMS + 4 + b:2 * ITEMS + 5 + b] for b in range(2)]
        over_n = ints[0:1, 2 * ITEMS + 6:2 * ITEMS + 7]
        over_e = sb("over_e", OVER + 1, dt=I32, parts=1)

        act_n, dve_n, pool_n = [0], [0], [0]
        act_step, dve_step, pool_step = sem("act_step"), sem("dve_step"), sem("pool_step")
        bank_filled = sem("bank_filled")
        emptied = {"act": sem("emptied_by_act"), "dve": sem("emptied_by_dve")}

        def wait_emptied(eng, use):
            eng.wait_ge(emptied[use.by], use.emptied)

        def then_own(eng, ins, step, n):
            n[0] += 1
            ins.then_inc(step, 1)
            eng.wait_ge(step, n[0])

        def w_cols(w, c0, n=512):
            return w.rearrange("(p k) n -> p k n", k=KD)[:, :, c0:c0 + n]

        def w_nat(w, c0, n=512):
            return w.rearrange("(k p) n -> p k n", p=P)[:, :, c0:c0 + n]

        lg = f3(rw, (NT, 40), 0)
        top = f3(rw, (NT, 16), 160)
        el = f3(rw, (NT, 8), 224)
        dif = f3(rw, (NT, 16), 256)
        pexp = f3(rw, (NT, 16), 320)
        rk, ovb, ea, slot, item, comb, tokg, toks = (rw[:, 384 + 8 * n:392 + 8 * n] for n in range(8))
        r4a, r4b, r4c, zg, gf, half5 = (rw[:, 448 + 4 * n:452 + 4 * n] for n in range(6))
        ohg = rw[:, 472:476]
        oh_slot = [rw[:, 480 + P * n:608 + P * n] for n in range(2)]
        oh_item = [rw[:, 736 + 3 * ITEMS * n:736 + 3 * ITEMS * (n + 1)] for n in range(2)]
        cnt, nov, ovend, ovbase, zero32, junk32 = (E[:, 1024 + EXPERTS * n:1024 + EXPERTS * (n + 1)] for n in range(6))
        over_cmp = E[0:1, 1280:1280 + (OVER + 1) * EXPERTS]
        over_row = E[0:1, 1900:1900 + OVER + 1]
        top_i = sb("top_i", NT * 16, dt=U32)
        gate_ready_cols = stat[:, 44:48]
        y_back = [f3(XN if t < 2 else A0, (2, D), 2048 * (t % 2)) for t in range(NT)]
        g_fin = B0[:, 0:D]

        cbuf, zbuf = f3(B2, (4, SEQ)), f3(B0, (4, SEQ))
        vbuf = f3(B1, (4, SEQ + CONV2 - 1))
        cacc = f3(E, (4, SEQ))
        hkvT = f3(A0, (KD, SEQ))
        k_rows, v_rows2 = f3(B0, (NT * WKV, WD)), f3(B0, (NT, WKV * WD), NT * WKV * WD)
        q_rows = f3(XN, (NT, D))
        sq_buf = f3(E, (4, SEQ))
        k_dup, k2T = f3(B2, (NT, 2 * WKV * WD)), f3(B1, (WKV, SEQ))
        q2T, zT = f3(A0, (KD, SEQ)), f3(A1, (KD, SEQ))
        wS = f3(HT, (3, 4, 2 * P))
        wpT = f3(E, (2, 2, 4 * P))
        yT2 = f3(XN, (KD, SEQ))

        w_in = a["w_in"][0]
        w_a, w_b = a["w_in_a_2"][0], a["w_in_b_2"][0]
        chunk_list, chunk_no = [], {}

        def add_chunk(name, src, us, last, by_half=True):
            chunk_no[name] = len(chunk_list)
            chunk_list.append((src, us[last].filled, by_half))

        add_chunk("dq", w_cols(w_in, 0), U, ("qk", 3), False)
        add_chunk("dk", w_cols(w_in, 512), U, ("qk", 7), False)
        add_chunk("dv", w_cols(w_in, 1024), U, ("dv", 3), False)
        for n, name in enumerate(("mq", "mk", "mv", "mo")):
            add_chunk(name, w_cols(w_in, 1536 + 512 * n), U, ("proj", 4 * n + 3), False)
        for n in range(2):
            add_chunk(f"wo{n}", w_nat(a["w_out"][0], 512 * n), U, ("wo", n, 3))
        for n in range(2):
            add_chunk(f"xk{n}", w_cols(a["w_xk"][0], 512 * n), U, ("xk", 4 * n + 3))
        for n in range(2):
            add_chunk(f"xv{n}", w_cols(a["w_xv"][0], 512 * n), U, ("xv", n, MT - 1))
        for n in range(2):
            add_chunk(f"xq{n}", w_cols(a["w_xq"][0], 512 * n), U, ("xq", 4 * n + 3))
        for n in range(2):
            add_chunk(f"xw{n}", w_nat(a["w_xo"][0], 512 * n), U, ("xw", n, 3))
        first_chunks = len(chunk_list)
        for n in range(2):
            for f, name in ((1, "c"), (2, "u"), (3, "z"), (0, "b")):
                add_chunk(f"{name}{n}", w_cols(w_a, D * f + 512 * n), V, (name, 4 * n + 3))
        for n in range(2):
            add_chunk(f"wa{n}", w_nat(a["w_out_a_2"][0], 512 * n), V, ("wa", n, 3))
        add_chunk("kv", w_cols(a["w_kv_2"], 0), V, ("kv", 3))
        for n in range(2):
            add_chunk(f"q{n}", w_cols(w_b, 512 * n), V, ("q", n, 3))
        for n in range(2):
            add_chunk(f"zz{n}", w_cols(w_b, D + 512 * n), V, ("zz", 4 * n + 3))
        for n in range(2):
            add_chunk(f"wb{n}", w_nat(a["w_out_b_2"][0], 512 * n), V, ("wb", n, 3))

        w_loaded = [sem(f"w_loaded{q}") for q in range(4)]
        w_high_ready, w_split = sem("w_high_ready"), sem("w_split")
        first_half_read = sem("first_half_read")

        def quarter(g, high):
            at = HALF * (g % 2)
            return f3(ring[(2 if high else 0) + g // 2 % 2], (4, 512), at)

        def wait_half_read(eng, g):
            _, filled, by_half = chunk_list[g // 2]
            if g % 2 == 0 and by_half:
                eng.wait_ge(first_half_read, sum(c[2] for c in chunk_list[:g // 2 + 1]))
            else:
                eng.wait_ge(bank_filled, filled)

        def r32(v):
            return bass.AP(tensor=rounded[v.tensor.name], offset=v.offset, ap=v.ap)

        def r32_read(v):
            return r32(v).bitcast(F32)

        we_loaded = [[sem(f"we_loaded{b}{j}") for j in range(3)] for b in range(2)]

        def expert_weights(e):
            one = lambda w: w[0, bass.ds(e, 1)]
            return [one(a["w1"]).rearrange("o (h p k) n -> p (o h) (k n)", h=2, p=P),
                    one(a["w3"]).rearrange("o (h p k) n -> p (o h) (k n)", h=2, p=P),
                    one(a["w2"]).rearrange("o (p k) n -> p (o k n)", p=P)]

        def as_expert(t, j):
            return f3(t, (2, 2048)) if j < 2 else t[:, 0:CHUNK]

        def w_slot_as(b, j):
            return as_expert(w_slot[b][j], j)

        block = ctx.enter_context(nc.Block())

        @block.sync
        def _(sp):
            consts_loaded, x_loaded = sem("consts_loaded"), sem("x_loaded")
            for t in range(NT):
                sp.dma_start(x_rows[:, t, :], a["x"][0, P * t:P * t + P, :]).then_inc(sem(f"x_loaded{t}"), 16)
            sp.dma_start(cst[:, :], a["consts"]).then_inc(consts_loaded, 16)
            sp.dma_start(g_mix, a["norm_mix_g"][0].rearrange("(p k) -> p k", k=KD)).then_inc(consts_loaded, 16)
            sp.dma_start(w_gates, w_cols(w_in, 3584, 8)).then_inc(consts_loaded, 16)
            for g in range(2):
                sp.dma_start(gate_b[32 * g:32 * g + HEADS, g:g + 1], a["ml_gate_b"][0, g].rearrange("(h o) -> h o", o=1),
                             allow_slow_non_contiguous=True).then_inc(consts_loaded, 16)

            def load_half(g):
                c, h = g // 2, g % 2
                sp.dma_start(quarter(g, False), chunk_list[c][0][:, 4 * h:4 * h + 4, :]).then_inc(w_loaded[g % 4], 16)

            for c in range(first_chunks):
                for g in (2 * c, 2 * c + 1):
                    if g >= 4:
                        wait_half_read(sp, g - 4)
                    load_half(g)
                if c == 1:
                    for dst, name, k in ((g_x, "norm_x_g", KD), (g_mem, "norm_mem_g", KD), (g_ffn, "norm_ffn_g", KD),
                                         (g_a, "ln_a_2", KD), (g_b, "ln_b_2", KD)):
                        sp.dma_start(dst, a[name][0].rearrange("(p k) -> p k", k=k)).then_inc(sem("more_loaded"), 16)
                    sp.dma_start(g_kv, a["ln_kv_2"].rearrange("(p k) -> p k", k=KD)).then_inc(sem("more_loaded"), 16)
                    for hf in range(2):
                        sp.dma_start(g_xh[:, 4 * hf:4 * hf + 4],
                                     a["norm_ffn_g"][0, 512 * hf:512 * hf + 512].rearrange("(p k) -> p k", k=4))\
                          .then_inc(sem("more_loaded"), 16)

            for b in range(2):
                for j, src in enumerate(expert_weights(b)):
                    if b == 0 and j == 2:
                        sp.wait_ge(bank_filled, U["mem_t", KD // 2 - 1].filled)
                    elif b == 0:
                        wait_half_read(sp, 2 * chunk_no["xw0"] + 1)
                    else:
                        wait_half_read(sp, 2 * chunk_no["xw1"] + 1)
                    sp.dma_start(w_slot_as(b, j), src).then_inc(we_loaded[b][j], 16)
            h_done, y_done = sem("h_done"), sem("y_done")
            with sp.Fori(1, EXPERTS // 2) as i:
                for b in range(2):
                    for j, src in enumerate(expert_weights(2 * i + b)):
                        sp.wait_ge(h_done if j < 2 else y_done, 2 * i + b - 1)
                        sp.wait_ge(we_loaded[1][2], 16)
                        sp.dma_start(w_slot_as(b, j), src).then_inc(we_loaded[b][j], 16)

            for n, c in enumerate(("c0", "u0")):
                sp.wait_ge(h_done, EXPERTS - 1 + n)
                for h in range(2):
                    load_half(2 * chunk_no[c] + h)

            wait_emptied(sp, U["table",])
            n = sp.value_load(over_n, min_val=0, max_val=OVER)
            with sp.If(n > 0):
                with sp.Fori(0, OVER) as k:
                    sp.wait_ge(sem("y_ready"), k + EXPERTS)
                    e = sp.value_load(over_e[0:1, bass.ds(k, 1)], min_val=0, max_val=EXPERTS - 1)
                    for j, src in enumerate(expert_weights(e)):
                        sp.dma_start(as_expert(over_slot[j], j), src).then_inc(sem("ov_w_loaded"), 16)

            for c in range(chunk_no["z0"], len(chunk_list)):
                for g in (2 * c, 2 * c + 1):
                    wait_half_read(sp, g - 4)
                    load_half(g)
            for n in range(2):
                for t in range(NT):
                    wait_emptied(sp, V["wb", n, t])
                    sp.dma_start(out[0, P * t:P * t + P, 512 * n:512 * n + 512],
                                 x_rows[:, t, 512 * n:512 * n + 512]).then_inc(sem("out_stored"), 16)
            sp.wait_ge(sem("out_stored"), 16 * 2 * NT)

        @block.gpsimd
        def _(pool):
            more = sem("more_loaded2")
            pool.memset(convT[:, :, 0:CONV1 - 1], 0.0).then_inc(sem("pads_zero"), 1)
            pool.memset(mv_rows[:, :, :, P:P + 1], 1.0).then_inc(sem("pads_zero"), 1)
            loads = [(rope_dst, a["rope"]) for rope_dst in (E[:, 0:2 * SEQ],)]
            loads += [(pick[:, :], a["pick"])]
            loads += [(lam_in, a["da_lambda"][0].rearrange("f n -> (f n)").partition_broadcast(P))]
            loads += [(g_sub, a["da_subln_g"][0].rearrange("(p k) -> p k", k=1))]
            loads += [(g_ml, a["ml_norm_g"][0].rearrange("(h p) -> p h", p=P))]
            loads += [(conv_w.rearrange("p (t m) -> p t m", m=KD)[:, t, :],
                       a["ml_conv_w"][0, t, 0].rearrange("(m p) -> p m", p=P)) for t in range(CONV1)]
            loads += [(conv_b, a["ml_conv_b"][0].rearrange("(m p) -> p m", p=P))]
            loads += [(conv_w2.rearrange("p (t m) -> p t m", m=KD)[:, t, :],
                       a["conv_a_2"][0, t, 0].rearrange("(m p) -> p m", p=P)) for t in range(CONV2)]
            loads += [(router_b[:, 0:GROUPS], a["b_router_group"][0].partition_broadcast(P)),
                      (router_b[:, GROUPS:], a["b_router_expert"][0].partition_broadcast(P)),
                      (k_gain, a["k_norm_2"].partition_broadcast(P)), (q_gain, a["q_norm_2"][0].partition_broadcast(P)),
                      (sink, a["sinks_2"][0].partition_broadcast(P))]
            for dst, src in loads:
                pool.dma_start(dst, src, allow_slow_non_contiguous=True).then_inc(more, 16)
            assert len(loads) == N_MORE

            def low_parts(c0, c1):
                for c in range(c0, c1):
                    for g in (2 * c, 2 * c + 1):
                        pool.wait_ge(w_high_ready, g + 1)
                        lo = quarter(g, False)
                        pool.tensor_tensor(r32(lo), lo, r32_read(quarter(g, True)), ALU.subtract).then_inc(w_split, 1)

            low_parts(0, chunk_no["xk0"])
            pool.wait_ge(bank_filled, U["ms", HEADS - 1, NT - 1].filled)
            pool.dma_start(mem_rows, a["mem"][0].rearrange("(t p) d -> p t d", p=P)).then_inc(sem("mem_loaded"), 16)
            pool.wait_ge(bank_filled, U["y_t", 3].filled)
            for t in range(NT):
                pool.dma_start(x_rows[:, t, :], a["x"][0, P * t:P * t + P, :]).then_inc(sem("x_again"), 16)
            low_parts(chunk_no["xk0"], first_chunks)
            pool.wait_ge(bank_filled, U["xs", 15].filled)
            rg = a["w_router_group"][0].rearrange("(p k) n -> p k n", k=KD)
            re = a["w_router_expert"][0].rearrange("(p k) n -> p k n", k=KD)
            pool.dma_start(router_w[:, :, 0:GROUPS], rg).then_inc(sem("router_loaded"), 16)
            pool.dma_start(router_w[:, :, GROUPS:], re).then_inc(sem("router_loaded"), 16)
            for t in range(NT):
                pool.wait_ge(sem("x2n_ready"), t + 1)
                for hf in range(2):
                    pool.dma_start(xn_dram[512 * hf + P * t:512 * hf + P * t + P, :],
                                   xn[:, t, 512 * hf:512 * hf + 512]).then_inc(sem("xn_stored"), 16)
            pool.wait_ge(bank_filled, U["xo", HEADS - 1, 1].filled)
            for b in range(3):
                then_own(pool, pool.memset(xg[b], 0.0), pool_step, pool_n)
            pool.wait_ge(sem("xn_stored"), 16 * 2 * NT)
            wait_emptied(pool, U["table",])
            then_own(pool, pool.memset(xg[3], 0.0), pool_step, pool_n)

            xg_turned, y_ready = sem("xg_turned"), sem("y_ready")
            first_idx, gather_idx, scatter_idx = sem("first_idx"), sem("gather_idx"), sem("scatter_idx")

            def index(dst, src, written, value):
                pool.tensor_copy(dst, src).then_inc(written, 1)
                pool.wait_ge(sem("xn_stored"), 16 * 2 * NT)
                pool.wait_ge(written, value)

            def gather_rows(q, s="xg_loaded"):
                pool.indirect_dma_start(xg[q], None, xn_dram,
                                        bass.IndirectOffsetOnAxis(ap=idx_g[q].bitcast(U32), axis=0),
                                        bounds_check=2 * SEQ - 1, oob_is_err=False).then_inc(sem(f"{s}{q}"), 16)

            def scatter_rows(b, s="y_stored"):
                pool.indirect_dma_start(y_dram, bass.IndirectOffsetOnAxis(ap=idx_s[b].bitcast(U32), axis=0),
                                        y_sb[b], None, bounds_check=4 * SEQ - 1, oob_is_err=False)\
                    .then_inc(sem(f"{s}{b}"), 16)

            for q in range(4):
                index(idx_g[q], tab_g[:, q:q + 1], first_idx, q + 1)
                gather_rows(q)

            def four(i, last):
                for q in range(4):
                    e = 4 * i + q
                    b = q % 2
                    if not last:
                        pool.wait_ge(xg_turned, e + 1)
                        index(idx_g[q], tab_g[:, bass.ds(e + 4, 1)], gather_idx, e + 1)
                        gather_rows(q)
                    pool.wait_ge(y_ready, e + 1)
                    index(idx_s[b], tab_s[:, bass.ds(e, 1)], scatter_idx, e + 1)
                    scatter_rows(b)

            with pool.Fori(0, EXPERTS // 4 - 1) as i:
                four(i, False)
            four(EXPERTS // 4 - 1, True)
            for b in range(2):
                pool.wait_ge(sem(f"y_stored{b}"), 16 * EXPERTS // 2)

            n = pool.value_load(over_n, min_val=0, max_val=OVER)
            with pool.If(n > 0):
                with pool.Fori(1, OVER + 1) as k:
                    index(idx_g[0], tab_g[:, bass.ds(k + (EXPERTS - 1), 1)], sem("ov_gather_idx"), k)
                    gather_rows(0, "ov_xg_loaded")
                    pool.wait_ge(y_ready, k + EXPERTS)
                    index(idx_s[0], tab_s[:, bass.ds(k + (EXPERTS - 1), 1)], sem("ov_scatter_idx"), k)
                    pool.indirect_dma_start(y_dram, bass.IndirectOffsetOnAxis(ap=idx_s[0].bitcast(U32), axis=0),
                                            y_sb[0], None, bounds_check=4 * SEQ - 1, oob_is_err=False)\
                        .then_inc(sem("ov_stored"), 16)
                    pool.wait_ge(sem("ov_stored"), 16 * k)
            pool.wait_ge(sem("pe_left_experts"), 1)
            for t in range(NT):
                for c in range(2):
                    for hf in range(2):
                        r = 1024 * hf + 512 * c + P * t
                        dst = y_back[t][:, c, 512 * hf:512 * hf + 512]
                        pool.dma_start(dst, y_dram[r:r + P, :]).then_inc(sem(f"y_back{t}"), 16)
            pool.dma_start(g_fin, a["norm_final_g"].partition_broadcast(P)).then_inc(sem("g_fin_loaded"), 16)
            low_parts(first_chunks, len(chunk_list))

        @block.tensor
        def _(pe):
            done = [0]

            def fill(us, *what):
                u = us[what]
                base = 0 if us is U else n1
                assert u.filled == base + done[0] + 1, what
                done[0] += 1
                if u.after:
                    pe.wait_ge(emptied[u.after[0]], u.after[1])
                return bank[u.bank]

            def gemm(o, lhs, rhs, n=KD):
                for k in range(n):
                    last = pe.matmul(o, lhs(k), rhs(k), start=(k == 0), stop=(k == n - 1))
                return last.then_inc(bank_filled, 1)

            def passes(o, lhs, rhs, k, first, last):
                (a_hi, a_lo), (b_hi, b_lo) = lhs(k), rhs(k)
                pe.matmul(o, r32(a_hi), r32(b_hi), start=first, stop=False)
                pe.matmul(o, r32(a_hi), r32(b_lo), start=False, stop=False)
                return pe.matmul(o, r32(a_lo), r32(b_hi), start=False, stop=last)

            def split_gemm(o, lhs, rhs):
                for k in range(KD):
                    last = passes(o, lhs, rhs, k, k == 0, k == KD - 1)
                return last.then_inc(bank_filled, 1)

            def weights(c):
                def part(k, c0=0, c1=512):
                    g = 2 * c + k // 4
                    return quarter(g, True)[:, k % 4, c0:c1], quarter(g, False)[:, k % 4, c0:c1]
                return part

            def chunk(name):
                c = chunk_no[name]
                pe.wait_ge(w_split, 2 * c + 2)
                return weights(c)

            def gemm_by_half(name, us, fills, n, lhs, rhs):
                c = chunk_no[name]
                part = weights(c)
                outs = [fill(us, *f)[:, 0:n] for f in fills]
                for h in range(2):
                    pe.wait_ge(w_split, 2 * c + h + 1)
                    for m, o in enumerate(outs):
                        for k in range(4 * h, 4 * h + 4):
                            last = passes(o, lambda k: lhs(m, part, k), lambda k: rhs(m, part, k), k, k == 0, k == KD - 1)
                        if h == 1:
                            last.then_inc(bank_filled, 1)
                    if h == 0:
                        last.then_inc(first_half_read, 1)

            def to_rows(name, us, fills, hi, lo):
                gemm_by_half(name, us, fills, 512, lambda m, part, k: (hi[:, k, P * m:P * m + P], lo[:, k, P * m:P * m + P]),
                             lambda m, part, k: part(k))

            def to_cols(name, us, fills, hi, lo, n=SEQ):
                gemm_by_half(name, us, fills, n, lambda m, part, k: part(k, P * m, P * m + P),
                             lambda m, part, k: (hi[:, k, :], lo[:, k, :]))

            def cols(k, c0=0, c1=SEQ):
                return hT[:, k, c0:c1], lowT[:, k, c0:c1]

            def turn(us, name, src, ready, base, n=NT):
                for k in range(KD):
                    o = fill(us, name, k)
                    for t in range(n):
                        if k == 0:
                            pe.wait_ge(ready, base + t + 1)
                        last = pe.transpose(o[:, P * t:P * t + P], src[:, t, k:D:KD], ident)
                    last.then_inc(bank_filled, 1)

            pe.wait_ge(sem("consts_loaded"), 80)
            turn(U, "x_t", xn, sem("x0n_ready"), 0)
            wait_emptied(pe, U["x_t", 7])
            pe.wait_ge(sem("w_gates_ready"), 1)
            split_gemm(fill(U, "gate")[0:GATE_M, :], lambda k: (w_gates_split[0][:, k, :], w_gates_split[1][:, k, :]), cols)

            def rotate(j):
                o = fill(U, "qk_rot", j)
                wait_emptied(pe, U["qk", j])
                pe.matmul(o[:, :], const("rot"), qkT[:, j, :], start=True, stop=True).then_inc(bank_filled, 1)

            for j in range(2 * HEADS):
                w = chunk("dq" if j < HEADS else "dk")
                m = j % HEADS
                split_gemm(fill(U, "qk", j)[:, :], lambda k: w(k, P * m, P * m + P), cols)
                if j >= 1:
                    rotate(j - 1)
            w = chunk("dv")
            for t in range(NT):
                split_gemm(fill(U, "dv", t)[:, :], lambda k: cols(k, P * t, P * t + P), w)
                if t == 0:
                    rotate(2 * HEADS - 1)

            for i in range(16 + 2):
                if i < 16:
                    h, qb = divmod(i, NT)
                    n = P * (qb + 1)
                    for m in range(2):
                        o = fill(U, "ds", i, m)
                        pe.wait_ge(sem("qk_rotated"), 5 + h)
                        r = slice(64 * m, 64 * m + 64)
                        pe.matmul(o[:, 0:n], qkT[r, h, P * qb:P * qb + P], qkT[r, HEADS + h, 0:n],
                                  start=True, stop=True).then_inc(bank_filled, 1)
                    w = chunk(("mq", "mk", "mv", "mo")[i // 4])
                    m = i % 4
                    o = fill(U, "proj", i)
                    if 8 <= i < 12:
                        split_gemm(o[:, :], lambda k: cols(k, P * m, P * m + P), w)
                    else:
                        split_gemm(o[:, :], lambda k: w(k, P * m, P * m + P), cols)
                if 1 <= i <= 16:
                    j = i - 1
                    o = fill(U, "da_t", j)
                    pe.wait_ge(sem("da_ready"), j + 1)
                    for kb in range(j % NT + 1):
                        last = pe.transpose(o[:, P * kb:P * kb + P], e_buf[:, j % 2, 0, P * kb:P * kb + P], ident)
                    last.then_inc(bank_filled, 1)
                if i >= 2:
                    j = i - 2
                    h, qb = divmod(j, NT)
                    o = fill(U, "do", j)
                    wait_emptied(pe, U["da_t", j])
                    wait_emptied(pe, U["dv", NT - 1])
                    gemm(o[:, 0:P], lambda k: daT[:, j % 2, k, :], lambda k: dv_rows[:, k, P * h:P * h + P], qb + 1)

            o = fill(U, "gates_t")
            pe.wait_ge(sem("gates_ready"), 1)
            for v, src in enumerate((g_bb, g_ex)):
                for t in range(NT):
                    last = pe.transpose(o[:, 16 * v + 4 * t:16 * v + 4 * t + 4], src[:, P * t:P * t + P],
                                        ident[0:HEADS, 0:HEADS])
            last.then_inc(bank_filled, 1)
            for h in range(HEADS):
                pe.wait_ge(sem("more_loaded2"), 16 * N_MORE)
                pe.matmul(fill(U, "m_row", h)[:, :], pick[:, P * h:P * h + P], g_M, start=True, stop=True)\
                  .then_inc(bank_filled, 1)
                pe.wait_ge(sem("silu_ready"), 8)
                for kb in range(NT):
                    o = fill(U, "ms", h, kb)
                    pe.matmul(o[:, P * kb:SEQ], mqkT[:, HEADS + h, P * kb:P * kb + P], mqkT[:, h, P * kb:SEQ],
                              start=True, stop=True).then_inc(bank_filled, 1)
                wait_emptied(pe, U["proj", 11])
                pe.wait_ge(sem("pads_zero"), 2)
                for qb in range(NT):
                    o = fill(U, "mh", h, qb)
                    wait_emptied(pe, U["ms", h, qb])
                    gemm(o[:, 0:P + 1], lambda k: sdT[:, h % 2, k, P * qb:P * qb + P],
                         lambda k: mv_rows[:, k, h, :], qb + 1)
            for m in range(8):
                o = fill(U, "y_t", m)
                pe.wait_ge(sem("y_rows_ready"), m + 1)
                for t in range(NT):
                    src = o_rows[:, t, m, :] if m < 4 else hm_rows[:, t, m - 4, :]
                    last = pe.transpose(o[:, P * t:P * t + P], src, ident)
                last.then_inc(bank_filled, 1)
            pe.wait_ge(sem("y_low_ready"), 8)
            for n in range(2):
                to_rows(f"wo{n}", U, [("wo", n, t) for t in range(NT)], yT, lowT)

            for k in range(KD // 2):
                o = fill(U, "mem_t", k)
                pe.wait_ge(sem("memn_ready"), MT)
                for kk in range(2):
                    for t in range(MT):
                        last = pe.transpose(o[:, MEM * kk + P * t:MEM * kk + P * t + P],
                                            mem_rows[:, t, 2 * k + kk:D:KD], ident)
                last.then_inc(bank_filled, 1)
            wait_emptied(pe, U["mem_t", KD // 2 - 1])
            for n in range(2):
                to_cols(f"xk{n}", U, [("xk", 4 * n + m) for m in range(4)], memT, mem_lo, MEM)
            for n in range(2):
                to_rows(f"xv{n}", U, [("xv", n, t) for t in range(MT)], memT, mem_lo)
            turn(U, "x1_t", xn, sem("x1n_ready"), 0)
            wait_emptied(pe, U["x1_t", 7])
            for n in range(2):
                to_cols(f"xq{n}", U, [("xq", 4 * n + m) for m in range(4)], hT, lowT)
            wait_emptied(pe, U["xv", 1, MT - 1])
            for i in range(16 + 2):
                if i < 16:
                    h, t = divmod(i, NT)
                    o = fill(U, "xs", i)
                    wait_emptied(pe, U["xq", 2 * h + 1])
                    gemm(o[:, 0:MEM], lambda k: xqT[:, 2 * h + k, P * t:P * t + P], lambda k: xkT[:, 2 * h + k, :], 2)
                if i >= 2:
                    j = i - 2
                    h, t = divmod(j, NT)
                    o = fill(U, "xp", j)
                    pe.wait_ge(sem("xp_ready"), j + 1)
                    for kt in range(MT):
                        last = pe.transpose(o[:, P * kt:P * kt + P], xe[:, j % 4, P * kt:P * kt + P], ident)
                    last.then_inc(bank_filled, 1)
                    if t == NT - 1:
                        wait_emptied(pe, U["xp", j])
                        for d in range(2):
                            c0 = MEM * h + P * d
                            gemm(fill(U, "xo", h, d)[:, :], lambda k: xv_rows[:, k, c0:c0 + P],
                                 lambda k: pT[:, h % 2, k, :], MT)
            wait_emptied(pe, U["xo", HEADS - 1, 1])
            for n in range(2):
                to_rows(f"xw{n}", U, [("xw", n, t) for t in range(NT)], yT, lowT)

            turn(U, "x2_t", xn, sem("x2n_ready"), 0)
            wait_emptied(pe, U["x2_t", 6])
            wait_emptied(pe, U["x2_t", 7])
            pe.wait_ge(sem("router_loaded"), 32)
            for t in range(NT):
                gemm(fill(U, "route", t)[:, 0:GROUPS + EXPERTS], lambda k: hT[:, k, P * t:P * t + P],
                     lambda k: router_w[:, k, :])
            pe.wait_ge(sem("chosen_ready"), NT)
            for t in range(NT):
                o = fill(U, "rank", t)
                for s in range(t + 1):
                    last = pe.matmul(o[:, 0:EXPERTS], const("ones") if s < t else const("before"), selb[:, s, :],
                                     start=(s == 0), stop=(s == t))
                last.then_inc(bank_filled, 1)
            gemm(fill(U, "count")[:, 0:EXPERTS], lambda k: const("ones"), lambda k: selb[:, k, :], NT)
            o = fill(U, "table")
            for s in range(2 * NT):
                pe.wait_ge(sem("onehots_ready"), s + 1)
                last = pe.matmul(o[:, 0:3 * ITEMS], oh_slot[s % 2], oh_item[s % 2], start=(s == 0),
                                 stop=(s == 2 * NT - 1))
                if s == 2 * NT - 1:
                    last.then_inc(bank_filled, 1)
                else:
                    last.then_inc(sem("onehots_used"), 1)
            pe.wait_ge(emptied["act"], act1)
            pe.wait_ge(emptied["dve"], dve1)

            h_done, y_done, xg_turned, g_turned = sem("h_done"), sem("y_done"), sem("xg_turned"), sem("g_turned")

            def turn_rows(q):
                for k in range(4):
                    last = pe.transpose(bank[q % 2][:, P * k:P * k + P], xg[q][:, k:512:4], ident)
                return last

            def hidden(b, slot):
                for n, (hf, k) in enumerate((hf, k) for hf in range(2) for k in range(4)):
                    for j in range(2):
                        w = as_expert(slot[j], j)[:, hf, 512 * k:512 * k + 512]
                        last = pe.matmul(bank[2 + b][64 * j:64 * j + 64, :], xgT[b][:, k, hf, :], w,
                                         start=(n == 0), stop=(n == 7), skip_group_check=True)
                return last

            def turn_gated(b):
                for k in range(4):
                    last = pe.transpose(bank[4 + b][:, SLOTS * k:SLOTS * k + SLOTS], gg[b][0:SLOTS, k:512:4],
                                        ident[0:SLOTS, 0:SLOTS])
                return last

            def down(b, slot):
                w = as_expert(slot[2], 2).rearrange("p (k n) -> p k n", k=4)
                for k in range(4):
                    for hf in range(2):
                        last = pe.matmul(bank[6 + b][64 * hf:64 * hf + 64, :], gT[b][:, k, :],
                                         w[:, k, 512 * hf:512 * hf + 512], start=(k == 0), stop=(k == 3),
                                         skip_group_check=True)
                return last

            def step_turn(i, q):
                pe.wait_ge(sem(f"xg_loaded{q}"), 16 * i + 16)
                turn_rows(q).then_inc(xg_turned, 1)

            def step_hidden(i, b):
                e = 2 * i + b
                pe.wait_ge(sem("xgT_ready"), e + 1)
                for j in range(2):
                    pe.wait_ge(we_loaded[b][j], 16 * i + 16)
                hidden(b, w_slot[b]).then_inc(h_done, 1)

            def step_down(i, b, first=False):
                e = 2 * i + b
                pe.wait_ge(sem("gT_ready"), e + 1)
                pe.wait_ge(we_loaded[b][2], 16 * i + 16)
                if not first:
                    pe.wait_ge(sem("y_ready"), e - 1)
                down(b, w_slot[b]).then_inc(y_done, 1)

            def step_gated(i, b):
                pe.wait_ge(sem("consts_loaded"), 80)
                pe.wait_ge(sem("g_ready"), 2 * i + b + 1)
                turn_gated(b).then_inc(g_turned, 1)

            def pair(j, half, first=False, last=False, second=False):
                i = 2 * j + half
                step_hidden(i, 0)
                step_turn(j, 2 * half + 1)
                if not first:
                    step_down(i - 1, 1, first=second)
                step_gated(i, 0)
                step_hidden(i, 1)
                if not last:
                    step_turn(j + half, 2 - 2 * half)
                step_down(i, 0, first=first)
                step_gated(i, 1)

            step_turn(0, 0)
            pair(0, 0, first=True)
            pair(0, 1, second=True)
            with pe.Fori(1, EXPERTS // 4 - 1) as j:
                pair(j, 0)
                pair(j, 1)
            pair(EXPERTS // 4 - 1, 0)
            pair(EXPERTS // 4 - 1, 1, last=True)
            step_down(EXPERTS // 2 - 1, 1)
            pe.wait_ge(sem("y_ready"), EXPERTS)

            wait_emptied(pe, U["table",])
            n = pe.value_load(over_n, min_val=0, max_val=OVER)
            with pe.If(n > 0):
                with pe.Fori(0, OVER) as k:
                    pe.wait_ge(sem("ov_xg_loaded0"), 16 * k + 16)
                    turn_rows(0).then_inc(sem("ov_xg_turned"), 1)
                    pe.wait_ge(sem("ov_xgT_ready"), k + 1)
                    pe.wait_ge(sem("ov_w_loaded"), 48 * k + 48)
                    hidden(0, over_slot).then_inc(sem("ov_h_done"), 1)
                    pe.wait_ge(sem("consts_loaded"), 80)
                    pe.wait_ge(sem("ov_g_ready"), k + 1)
                    turn_gated(0).then_inc(sem("ov_g_turned"), 1)
                    pe.wait_ge(sem("ov_gT_ready"), k + 1)
                    down(0, over_slot).then_inc(sem("ov_y_done"), 1)
                    pe.wait_ge(sem("ov_stored"), 16 * k + 16)
            pe.nop().then_inc(sem("pe_left_experts"), 1)

            done[0] = 0

            turn(V, "x4_t", xn, sem("x4n_ready"), 0)
            wait_emptied(pe, V["x4_t", 7])
            for n in range(2):
                for name in "cuzb":
                    to_cols(f"{name}{n}", V, [(name, 4 * n + m) for m in range(4)], hT, lowT)
            pe.wait_ge(sem("y2_low_ready"), 8)
            for n in range(2):
                to_rows(f"wa{n}", V, [("wa", n, t) for t in range(NT)], yT, y2_lo)
            turn(V, "x5_t", xn, sem("x5n_ready"), 0)
            wait_emptied(pe, V["x5_t", KD - 1])
            to_rows("kv", V, [("kv", t) for t in range(NT)], hkvT, hkv_lo)
            for n in range(2):
                to_rows(f"q{n}", V, [("q", n, t) for t in range(NT)], hT, lowT)
            for n in range(2):
                to_cols(f"zz{n}", V, [("zz", 4 * n + m) for m in range(4)], hT, lowT)
            pe.wait_ge(sem("k2_ready"), 1)
            for g in range(WKV):
                o = fill(V, "k_t", g)
                for t in range(NT):
                    last = pe.transpose(o[:, P * t:P * t + P], k_dup[:, t, P * g:P * g + P], ident)
                last.then_inc(bank_filled, 1)
            pe.wait_ge(sem("q2_ready"), 1)
            for p in range(8):
                o = fill(V, "q_t", p)
                for t in range(NT):
                    last = pe.transpose(o[:, P * t:P * t + P], q_rows[:, t, P * p:P * p + P], ident)
                last.then_inc(bank_filled, 1)
            wait_emptied(pe, V["k_t", WKV - 1])
            wait_emptied(pe, V["q_t", 7])
            for i in range(16 + 2):
                if i < 16:
                    nb, g = divmod(i, WKV)
                    k0, n = (P * (nb - 1), 2 * P) if nb else (0, P)
                    for hh in range(2):
                        o = fill(V, "ws", i, hh)
                        r = slice(64 * hh, 64 * hh + 64)
                        for pr in range(2):
                            last = pe.matmul(o[:, 256 * pr:256 * pr + n], q2T[r, 2 * g + pr, P * nb:P * nb + P],
                                             k2T[r, g, k0:k0 + n], start=True, stop=True)
                        last.then_inc(bank_filled, 1)
                if i >= 2:
                    j = i - 2
                    nb, g = divmod(j, WKV)
                    pe.wait_ge(sem("wp_ready"), j + 1)
                    for kt in window_tiles(j):
                        o = fill(V, "wp", j, kt)
                        for q in range(4):
                            c0 = P * (kt - (nb == 0))
                            last = pe.transpose(o[:, P * q:P * q + P], wS[:, j % 3, q, c0:c0 + P], ident)
                        last.then_inc(bank_filled, 1)
                    o = fill(V, "wv", j)
                    kts = window_tiles(j)
                    wait_emptied(pe, V["wp", j, 1])
                    for n, kt in enumerate(kts):
                        for hh in range(2):
                            last = pe.matmul(o[64 * hh:64 * hh + 64, 0:256],
                                             v_rows2[:, nb - 1 + kt, WD * g:WD * g + WD],
                                             wpT[:, j % 2, kt, 256 * hh:256 * hh + 256], start=(n == 0),
                                             stop=(n == len(kts) - 1), skip_group_check=True)
                    last.then_inc(bank_filled, 1)
            pe.wait_ge(sem("y3_low_ready"), 16)
            for n in range(2):
                to_rows(f"wb{n}", V, [("wb", n, t) for t in range(NT)], yT2, lowT)


        @block.scalar
        def _(act):
            done = emptied["act"]

            def filled(u):
                act.wait_ge(bank_filled, u.filled)
                return bank[u.bank]

            summed = [0]

            def sums(src, t, c, out_=None):
                n = summed[0]
                summed[0] += 1
                if out_ is None:
                    act.wait_ge(sem("ss_ready"), n - 1)
                    out_ = E[:, D * (n % 2):D * (n % 2) + D]
                act.activation(out_, src[:, t, :], ACT.Square, accum_out=ss[:, c:c + 1]).then_inc(sem("ss_ready"), 1)

            def roots(n, c0, c1):
                act.wait_ge(sem("ms_ready"), n)
                act.activation(root[:, c0:c1], ms[:, c0:c1], ACT.Sqrt).then_inc(sem("root_ready"), 1)

            def high_parts(*names):
                for name in names:
                    for g in (2 * chunk_no[name], 2 * chunk_no[name] + 1):
                        act.wait_ge(w_loaded[g % 4], 16 * (g // 4 + 1))
                        if g >= 4:
                            wait_half_read(act, g - 4)
                        act.activation(r32(quarter(g, True)), quarter(g, False), ACT.Copy).then_inc(w_high_ready, 1)

            def high_cols(us, name, dst, gain, n=SEQ, high=None):
                for k in range(KD):
                    o = filled(us[name, k])
                    act.activation(r32(dst[:, k, :]), o[:, 0:n], ACT.Copy, scale=gain[:, k:k + 1])\
                       .then_inc(sem("high_ready"), 1)

            for t in range(NT):
                act.wait_ge(sem(f"x_loaded{t}"), 16)
                sums(x_rows, t, t, xn[:, t, :])
            roots(1, 0, NT)
            act.wait_ge(sem("consts_loaded"), 80)
            high_cols(U, "x_t", hT, g_mix)
            high_parts("dq")

            act.wait_ge(sem("gate_abs_ready"), 1)
            act.activation(g_ex, g_l, ACT.Exp).then_inc(act_step, 1)
            act.wait_ge(act_step, 1)
            act.activation(g_l, g_ex, ACT.Ln, bias=1.0).then_inc(sem("gate_log_ready"), 1)
            act.wait_ge(sem("lam_sum_ready"), 1)
            act.activation(lam_s[:, 2:4], lam_s[:, 0:2], ACT.Exp).then_inc(sem("lam_exp_ready"), 1)

            high_parts("dk")
            for j in range(2 * HEADS):
                if j == 4:
                    high_parts("dv")
                o = filled(U["qk", j])
                act.activation(qkT[:, j, :], o[:, :], ACT.Copy).then_inc(done, 1)
            high_parts("mq")
            for t in range(NT):
                o = filled(U["dv", t])
                act.activation(dv_rows[:, t, :], o[:, :], ACT.Copy).then_inc(done, 1)
            act.wait_ge(sem("qk_rotated"), 2 * HEADS)
            for i in range(16 + 2):
                if i < 16 and i % 4 == 0:
                    high_parts(("mk", "mv", "mo", "wo0")[i // 4])
                if i < 16:
                    h, qb = divmod(i, NT)
                    n = P * (qb + 1)
                    act.wait_ge(sem("da_max_ready"), i + 1)
                    if i >= 2:
                        act.wait_ge(bank_filled, U["da_t", i - 2].filled)
                    for m in range(2):
                        c = 2 * (i % 2) + m
                        o = filled(U["ds", i, m])
                        act.activation(e_buf[:, i % 2, m, 0:n], o[:, 0:n], ACT.Exp, bias=neg[:, c:c + 1],
                                       scale=DA_DIM ** -0.5, accum_out=zsum[:, c:c + 1]).then_inc(done, 1)
                    if i < 8:
                        o = filled(U["proj", i])
                        act.activation(mqkT[:, i, :], o[:, :], ACT.Copy).then_inc(done, 1)
                    elif i >= 12:
                        o = filled(U["proj", i])
                        act.activation(moT[:, i - 12, :], o[:, :], ACT.Copy).then_inc(done, 1)
                if i >= 2:
                    j = i - 2
                    h, qb = divmod(j, NT)
                    o = filled(U["do", j])
                    act.activation(o_rows[:, qb, h, :], o[:, 0:P], ACT.Copy).then_inc(act_step, 1)
                    act.wait_ge(act_step, 2 + j)
                    act.activation(o[:, 0:P], o[:, 0:P], ACT.Square, accum_out=ss[:, 32 + j:33 + j]).then_inc(done, 1)
                if i == 11:
                    act.wait_ge(sem("conv_done"), 8)
                    for m in range(8):
                        act.activation(mqkT[:, m, :], mqkT[:, m, :], ACT.Silu).then_inc(sem("silu_ready"), 1)

            high_parts("wo1")
            wait_emptied(act, U["gates_t",])
            act.activation(em, mT, ACT.Exp, scale=-1.0).then_inc(sem("em_ready"), 1)
            for h in range(HEADS):
                o = filled(U["m_row", h])
                act.wait_ge(sem("diag_ready"), h + 1)
                for kb in range(NT):
                    n = NT * h + kb
                    if n >= 2:
                        wait_emptied(act, U[("ms",) + divmod(n - 2, NT)])
                    bias = bT[:, 4 * kb + h:4 * kb + h + 1]
                    if kb < NT - 1:
                        rest = act.activation(d_buf[:, n % 2, P:SEQ - P * kb], o[:, P * kb + P:SEQ], ACT.Exp, bias=bias)
                        if kb == NT - 2:
                            rest.then_inc(done, 1)
                    act.activation(d_buf[:, n % 2, 0:P], arg_diag[:, h % 2, P * kb:P * kb + P], ACT.Exp,
                                   bias=bias).then_inc(sem("d_ready"), 1)
            wait_emptied(act, U["proj", 15])
            for m in range(HEADS):
                act.activation(moT[:, m, :], moT[:, m, :], ACT.Sigmoid).then_inc(sem("sig_ready"), 1)
            roots(2, 32, 64)

            act.wait_ge(sem("mem_loaded"), 16)
            for t in range(MT):
                sums(mem_rows, t, NT + t)
            for m in range(8):
                if m < 4:
                    o = filled(U["y_t", m])
                    act.activation(r32(yT[:, m, :]), o[:, :], ACT.Copy, scale=g_sub_s)\
                       .then_inc(sem("high_ready"), 1)
                else:
                    wait_emptied(act, U["y_t", m])
                    act.activation(r32(yT[:, m, :]), lowT[:, m, :], ACT.Copy).then_inc(sem("high_ready"), 1)
            roots(3, NT, NT + MT)
            high_parts("xk0")
            for t in range(NT):
                wait_emptied(act, U["wo", 1, t])
                sums(x_rows, t, 8 + t)
            act.wait_ge(sem("more_loaded"), 16 * 8)
            for k in range(KD // 2):
                o = filled(U["mem_t", k])
                for kk in range(2):
                    last = act.activation(r32(memT[:, 2 * k + kk, :]), o[:, MEM * kk:MEM * kk + MEM], ACT.Copy,
                                          scale=g_mem[:, 2 * k + kk:2 * k + kk + 1])
                last.then_inc(sem("high_ready"), 1)
            roots(4, 8, 8 + NT)
            high_parts("xk1")
            for m in range(8):
                if m == 4:
                    high_parts("xv0")
                o = filled(U["xk", m])
                act.activation(xkT[:, m, :], o[:, 0:MEM], ACT.Copy).then_inc(done, 1)
            for n in range(2):
                high_parts(("xv1", "xq0")[n])
                for t in range(MT):
                    o = filled(U["xv", n, t])
                    act.activation(xv_rows[:, t, 512 * n:512 * n + 512], o[:, :], ACT.Copy).then_inc(done, 1)
            high_parts("xq1")
            high_cols(U, "x1_t", hT, g_x)
            for m in range(8):
                if m == 4:
                    high_parts("xw0")
                o = filled(U["xq", m])
                act.activation(xqT[:, m, :], o[:, :], ACT.Copy).then_inc(done, 1)
            high_parts("xw1")
            for i in range(16 + 2):
                if i < 16:
                    o = filled(U["xs", i])
                    act.wait_ge(sem("xmax_ready"), i + 1)
                    if i >= 4:
                        act.wait_ge(bank_filled, U["xp", i - 4].filled)
                    c = i % 8
                    act.activation(xe[:, i % 4, :], o[:, 0:MEM], ACT.Exp, bias=neg[:, c:c + 1], scale=1.0 / 16,
                                   accum_out=zsum[:, c:c + 1]).then_inc(done, 1)
                if i >= 2 and (i - 2) % NT == NT - 1:
                    for d in range(2):
                        o = filled(U["xo", (i - 2) // NT, d])
                        act.activation(r32(yT[:, 2 * ((i - 2) // NT) + d, :]), o[:, :], ACT.Copy)\
                           .then_inc(sem("high_ready"), 1)
            for t in range(NT):
                wait_emptied(act, U["xw", 1, t])
                sums(x_rows, t, 12 + t)
            roots(5, 12, 12 + NT)
            for k in range(0, KD, 2):
                o = filled(U["x2_t", k])
                act.activation(hT[:, k, :], o[:, :], ACT.Copy, scale=g_ffn[:, k:k + 1]).then_inc(done, 1)
            act.wait_ge(sem("dif_ready"), 1)
            act.activation(pexp, dif, ACT.Exp).then_inc(sem("pexp_ready"), 1)

            h_done, g_turned = sem("h_done"), sem("g_turned")

            def silu(b):
                return act.activation(sil[b][SLOTS:P, :], bank[2 + b][0:SLOTS, :], ACT.Silu)

            def gated_cols(b):
                return act.activation(gT[b], bank[4 + b][:, 0:4 * SLOTS].rearrange("p (k s) -> p k s", k=4), ACT.Copy)

            def pair(i, first=False):
                for b in range(2):
                    e = 2 * i + b
                    act.wait_ge(h_done, e + 1)
                    if not first:
                        act.wait_ge(sem("g_ready"), e - 1)
                    silu(b).then_inc(sem("silu_e_ready"), 1)
                    act.wait_ge(g_turned, e + 1)
                    if not first:
                        act.wait_ge(sem("y_done"), e - 1)
                    gated_cols(b).then_inc(sem("gT_ready"), 1)

            pair(0, True)
            with act.Fori(1, EXPERTS // 2) as i:
                pair(i)
            act.wait_ge(sem("y_done"), EXPERTS)
            wait_emptied(act, U["table",])
            n = act.value_load(over_n, min_val=0, max_val=OVER)
            with act.If(n > 0):
                with act.Fori(0, OVER) as k:
                    act.wait_ge(sem("ov_h_done"), k + 1)
                    silu(0).then_inc(sem("ov_silu_ready"), 1)
                    act.wait_ge(sem("ov_g_turned"), k + 1)
                    gated_cols(0).then_inc(sem("ov_gT_ready"), 1)
                    act.wait_ge(sem("ov_stored"), 16 * k + 16)

            high_parts("c0", "u0")
            for t in range(NT):
                act.wait_ge(sem("x3_ready"), t + 1)
                sums(x_rows, t, 16 + t)
            roots(6, 16, 16 + NT)
            for t in range(NT):
                act.wait_ge(sem("x4_ready"), t + 1)
                sums(x_rows, t, 20 + t)
            roots(7, 20, 20 + NT)
            high_cols(V, "x4_t", hT, g_a)
            for n in range(2):
                js = range(4 * n, 4 * n + 4)
                for j in js:
                    o = filled(V["c", j])
                    if n:
                        wait_emptied(act, V["u", j - 4])
                    act.activation(cbuf[:, j % 4, :], o[:, :], ACT.Copy).then_inc(done, 1)
                high_parts(f"z{n}", f"b{n}")
                for j in js:
                    o = filled(V["z", j])
                    if n:
                        wait_emptied(act, V["b", j - 4])
                    act.activation(zbuf[:, j % 4, :], o[:, :], ACT.Silu).then_inc(done, 1)
                high_parts(("c1", "wa0")[n])
                for j in js:
                    wait_emptied(act, V["b", j])
                    act.activation(r32(yT[:, j, :]), y2_lo[:, j, :], ACT.Copy).then_inc(sem("high_ready"), 1)
                high_parts(("u1", "wa1")[n])
            high_parts("kv")
            for t in range(NT):
                wait_emptied(act, V["wa", 1, t])
                sums(x_rows, t, 24 + t)
            roots(8, 24, 24 + NT)
            high_parts("q0")
            for k in range(KD):
                o = filled(V["x5_t", k])
                for dst, g in ((hkvT, g_kv), (hT, g_b)):
                    last = act.activation(r32(dst[:, k, :]), o[:, :], ACT.Copy, scale=g[:, k:k + 1])
                last.then_inc(sem("high_ready"), 1)
            for t in range(NT):
                o = filled(V["kv", t])
                act.activation(k_rows[:, WKV * t:WKV * t + WKV, :], o[:, 0:256].rearrange("p (g d) -> p g d", g=WKV),
                               ACT.Copy)
                act.activation(v_rows2[:, t, :], o[:, 256:512], ACT.Copy)
                act.activation(sq_buf[:, t, 0:256], o[:, 0:256], ACT.Square).then_inc(done, 1)
            for n in range(2):
                high_parts(("q1", "zz0")[n])
                for t in range(NT):
                    o = filled(V["q", n, t])
                    act.wait_ge(sem("sq_used"), NT * n + t + 1)
                    act.activation(q_rows[:, t, 512 * n:512 * n + 512], o[:, :], ACT.Copy)
                    act.activation(sq_buf[:, t, :], o[:, :], ACT.Square).then_inc(done, 1)
            high_parts("zz1")
            roots(9, 0, 80)
            for m in range(8):
                if m == 4:
                    high_parts("wb0")
                o = filled(V["zz", m])
                act.activation(zT[:, m, :], o[:, :], ACT.Silu).then_inc(done, 1)
            high_parts("wb1")
            for p in range(8):
                o = filled(V["q_t", p])
                act.activation(q2T[:, p, :], o[:, :], ACT.Copy).then_inc(done, 1)
            def high_of(j):
                nb, g = divmod(j, WKV)
                wait_emptied(act, V["wv", j])
                v = lambda t: t[:, 2 * g:2 * g + 2, P * nb:P * nb + P]
                act.activation(r32(v(yT2)), v(lowT), ACT.Copy).then_inc(sem("high_ready"), 1)

            for i in range(16 + 2):
                if i < 16:
                    n = 2 * P if i // WKV else P
                    act.wait_ge(sem("w_max_ready"), i + 1)
                    for q in range(4):
                        c = 8 * (i % 2) + q
                        act.activation(wS[:, i % 3, q, 0:n], wS[:, i % 3, q, 0:n], ACT.Exp, bias=neg[:, c:c + 1],
                                       accum_out=zsum[:, c:c + 1])
                    c = 4 * (i % 2)
                    act.activation(stat[:, 16 + c:20 + c], stat[:, c:c + 4], ACT.Exp).then_inc(sem("w_exp_ready"), 1)
                if i >= 2:
                    j = i - 2
                    if j >= 2:
                        act.wait_ge(bank_filled, V["wv", j - 2].filled)
                    for kt in window_tiles(j):
                        o = filled(V["wp", j, kt])
                        act.activation(wpT[:, j % 2, kt, :], o[:, :], ACT.Copy).then_inc(done, 1)
                if i >= 3:
                    high_of(i - 3)
            high_of(15)

        @block.vector
        def _(dve):
            done = emptied["dve"]

            def filled(u):
                dve.wait_ge(bank_filled, u.filled)
                return bank[u.bank]

            def own(ins):
                then_own(dve, ins, dve_step, dve_n)

            ss_total, ms_total = [0], [0]

            def rstds(n_sums, spans):
                ss_total[0] += n_sums
                ms_total[0] += 1
                if n_sums:
                    dve.wait_ge(sem("ss_ready"), ss_total[0])
                for c0, c1, width in spans:
                    last = dve.tensor_scalar(ms[:, c0:c1], ss[:, c0:c1], 1.0 / width, EPS, ALU.mult, ALU.add)
                last.then_inc(sem("ms_ready"), 1)
                dve.wait_ge(sem("root_ready"), ms_total[0])
                own(dve.reciprocal(rstd[:, spans[0][0]:spans[-1][1]], root[:, spans[0][0]:spans[-1][1]]))

            def normalise(c0, ready):
                for t in range(NT):
                    dve.tensor_scalar(xn[:, t, :], x_rows[:, t, :], rstd[:, c0 + t:c0 + t + 1], None, ALU.mult)\
                       .then_inc(ready, 1)

            highs = [0]

            def wait_high():
                highs[0] += 1
                dve.wait_ge(sem("high_ready"), highs[0])

            def low_cols(us, name, gain):
                for k in range(KD):
                    o = filled(us[name, k])
                    wait_high()
                    dve.scalar_tensor_tensor(r32(lowT[:, k, :]), o[:, :], gain[:, k:k + 1], r32_read(hT[:, k, :]),
                                             ALU.mult, ALU.subtract).then_inc(done, 1)

            rstds(NT, [(0, NT, D)])
            normalise(0, sem("x0n_ready"))
            dve.wait_ge(sem("consts_loaded"), 80)
            for s in range(2):
                own(dve.tensor_scalar(r32(w_gates_split[s]), ident[:, 0:GATE_M].unsqueeze(1).to_broadcast([P, KD, GATE_M]),
                                      0.0, None, ALU.mult))
            for g in range(2):
                src, at = w_gates[:, :, 4 * g:4 * g + 4], slice(32 * g, 32 * g + 4)
                own(dve.tensor_copy(r32(w_gates_split[0][:, :, at]), src))
                last = dve.tensor_tensor(r32(w_gates_split[1][:, :, at]), src, r32_read(w_gates_split[0][:, :, at]), ALU.subtract)
            last.then_inc(sem("w_gates_ready"), 1)
            low_cols(U, "x_t", g_mix)

            o = filled(U["gate",])
            for g, dst in enumerate((g_i, g_f)):
                rows = slice(32 * g, 32 * g + HEADS)
                last = dve.tensor_scalar(dst, o[rows, :], gate_b[rows, g:g + 1], None, ALU.add)
            last.then_inc(done, 1)
            wait_emptied(dve, U["gate",])
            dve.tensor_scalar(g_min, g_f, 0.0, None, ALU.min)
            dve.scalar_tensor_tensor(g_l, g_f, -1.0, g_f, ALU.mult, ALU.min).then_inc(sem("gate_abs_ready"), 1)
            dve.wait_ge(sem("more_loaded2"), 16 * N_MORE)
            for m in range(2):
                last = dve.tensor_tensor_reduce(rw[:, 64 * m:64 * m + 64], lam_in[:, P * m:P * m + DA_DIM],
                                                lam_in[:, P * m + DA_DIM:P * m + P], 1.0, 0.0, ALU.mult, ALU.add,
                                                lam_s[:, m:m + 1])
            last.then_inc(sem("lam_sum_ready"), 1)
            dve.tensor_scalar(g_sub_s, g_sub, 1.0 - LAM_INIT, None, ALU.mult)
            dve.wait_ge(sem("gate_log_ready"), 1)
            own(dve.tensor_tensor(g_f, g_min, g_l, ALU.subtract))
            own(dve.memset(g_min, 0.0))
            own(dve.tensor_tensor_scan(g_a_sum, g_f, g_min, 0.0, ALU.add, ALU.add))
            own(dve.tensor_tensor(g_bb, g_i, g_a_sum, ALU.subtract))
            own(dve.tensor_tensor_scan(g_M, g_min, g_bb, 0.0, ALU.add, ALU.max))
            dve.tensor_tensor(g_ex, g_M, g_a_sum, ALU.add).then_inc(sem("gates_ready"), 1)
            dve.wait_ge(sem("lam_exp_ready"), 1)
            own(dve.tensor_tensor(neg_lam, lam_s[:, 3:4], lam_s[:, 2:3], ALU.subtract))
            own(dve.tensor_scalar(neg_lam, neg_lam, -LAM_INIT, None, ALU.add))

            for j in range(2 * HEADS):
                o = filled(U["qk_rot", j])
                dve.tensor_tensor(rope_tmp, o[:, :], sinT, ALU.mult).then_inc(done, 1)
                own(dve.tensor_tensor(qkT[:, j, :], qkT[:, j, :], cosT, ALU.mult))
                dve.tensor_tensor(qkT[:, j, :], qkT[:, j, :], rope_tmp, ALU.add).then_inc(sem("qk_rotated"), 1)
                dve.wait_ge(sem("qk_rotated"), j + 1)

            def conv(j):
                wait_emptied(dve, U["proj", j])
                w = lambda tap: conv_w[:, KD * tap + j:KD * tap + j + 1]
                acc = conv_tmp[:, j % 2, :]
                own(dve.tensor_scalar(acc, convT[:, j, 0:SEQ], w(0), conv_b[:, j:j + 1], ALU.mult, ALU.add))
                for tap in range(1, CONV1 - 1):
                    own(dve.scalar_tensor_tensor(acc, convT[:, j, tap:tap + SEQ], w(tap), acc, ALU.mult, ALU.add))
                dve.scalar_tensor_tensor(mqkT[:, j, :], mqkT[:, j, :], w(CONV1 - 1), acc, ALU.mult, ALU.add)\
                   .then_inc(sem("conv_done"), 1)

            dve.wait_ge(sem("pads_zero"), 2)
            for i in range(16 + 2):
                if i < 16:
                    h, qb = divmod(i, NT)
                    n = P * (qb + 1)
                    c = 2 * (i % 2)
                    for m in range(2):
                        o = filled(U["ds", i, m])
                        last = dve.tensor_tensor(o[:, n - P:n], o[:, n - P:n], const("mask_qk"), ALU.add)
                    own(last)
                    for m in range(2):
                        last = dve.tensor_reduce(mx[:, c + m:c + m + 1], bank[U["ds", i, m].bank][:, 0:n], AX.X, ALU.max)
                    own(last)
                    dve.tensor_scalar(neg[:, c:c + 2], mx[:, c:c + 2], -(DA_DIM ** -0.5), None, ALU.mult)\
                       .then_inc(sem("da_max_ready"), 1)
                    if 8 <= i < 12:
                        o = filled(U["proj", i])
                        dve.tensor_copy(mv_rows[:, i - 8, :, 0:P], o[:, :].rearrange("p (h d) -> p h d", h=HEADS))\
                           .then_inc(done, 1)
                if 1 <= i <= 16:
                    j = i - 1
                    h, qb = divmod(j, NT)
                    n, c = P * (qb + 1), 2 * (j % 2)
                    wait_emptied(dve, U["ds", j, 1])
                    own(dve.reciprocal(rz[:, c:c + 2], zsum[:, c:c + 2]))
                    own(dve.tensor_tensor(rz[:, c + 1:c + 2], rz[:, c + 1:c + 2], neg_lam, ALU.mult))
                    e0, e1 = e_buf[:, j % 2, 0, 0:n], e_buf[:, j % 2, 1, 0:n]
                    own(dve.tensor_scalar(e0, e0, rz[:, c:c + 1], None, ALU.mult))
                    dve.scalar_tensor_tensor(e0, e1, rz[:, c + 1:c + 2], e0, ALU.mult, ALU.add)\
                       .then_inc(sem("da_ready"), 1)
                    if j < 8:
                        conv(j)
                    o = filled(U["da_t", j])
                    if j >= 2:
                        dve.wait_ge(bank_filled, U["do", j - 2].filled)
                    dve.tensor_copy(daT[:, j % 2, 0:qb + 1, :], o[:, 0:n].rearrange("p (k q) -> p k q", q=P))\
                       .then_inc(done, 1)

            o = filled(U["gates_t",])
            dve.tensor_copy(bmT, o[:, 0:32]).then_inc(done, 1)
            dve.wait_ge(sem("em_ready"), 1)
            bn, mv, t2 = stat[:, 32:38], stat[:, 0:32], stat[:, 40:44]
            for h in range(HEADS):
                o = filled(U["m_row", h])
                dve.tensor_tensor(arg_diag[:, h % 2, :].rearrange("p (k q) -> p k q", k=NT),
                                  o[:, :].rearrange("p (k q) -> p k q", k=NT),
                                  const("mask_kq").unsqueeze(1).to_broadcast([P, NT, P]), ALU.add)\
                   .then_inc(sem("diag_ready"), 1)
                for kb in range(NT):
                    o = filled(U["ms", h, kb])
                    dve.wait_ge(sem("d_ready"), NT * h + kb + 1)
                    n = SEQ - P * kb
                    dve.scalar_tensor_tensor(sdT[:, h % 2, kb, P * kb:SEQ], o[:, P * kb:SEQ], float(P) ** -0.5,
                                             d_buf[:, (NT * h + kb) % 2, 0:n], ALU.mult, ALU.mult).then_inc(done, 1)
                for qb in range(NT):
                    o = filled(U["mh", h, qb])
                    c = NT * h + qb
                    own(dve.tensor_copy(t2[:, 3:4], o[:, P:P + 1]))
                    own(dve.scalar_tensor_tensor(t2[:, 0:1], t2[:, 3:4], -1.0, t2[:, 3:4], ALU.mult, ALU.max))
                    own(dve.tensor_scalar(t2[:, 1:2], t2[:, 0:1], em[:, 4 * qb + h:4 * qb + h + 1], None, ALU.max))
                    own(dve.reciprocal(t2[:, 2:3], t2[:, 1:2]))
                    dve.tensor_scalar(hm_rows[:, qb, h, :], o[:, 0:P], t2[:, 2:3], None, ALU.mult).then_inc(done, 1)
                    wait_emptied(dve, U["mh", h, qb])
                    own(dve.bn_stats(bn, hm_rows[:, qb, h, :]))
                    own(dve.bn_aggr(mv[:, 2 * c:2 * c + 2], bn))

            wait_emptied(dve, U["do", 15])
            own(dve.tensor_scalar(ss[:, 48:64], mv[:, 1:32:2], float(P), None, ALU.mult))
            rstds(0, [(32, 64, P)])
            for m in range(4):
                v = o_rows[:, :, m, :]
                r = rstd[:, 32 + 4 * m:36 + 4 * m].unsqueeze(2).to_broadcast([P, NT, P])
                dve.tensor_tensor(v, v, r, ALU.mult).then_inc(sem("y_rows_ready"), 1)
            for h in range(HEADS):
                for t in range(NT):
                    c = NT * h + t
                    last = dve.tensor_scalar(hm_rows[:, t, h, :], hm_rows[:, t, h, :], mv[:, 2 * c:2 * c + 1],
                                             rstd[:, 48 + c:49 + c], ALU.subtract, ALU.mult)
                last.then_inc(sem("y_rows_ready"), 1)
            for m in range(8):
                o = filled(U["y_t", m])
                if m < 4:
                    wait_high()
                    own(dve.scalar_tensor_tensor(r32(lowT[:, m, :]), o[:, :], g_sub_s, r32_read(yT[:, m, :]), ALU.mult,
                                                 ALU.subtract))
                    dve.nop().then_inc(done, 1)
                    dve.nop().then_inc(sem("y_low_ready"), 1)
                else:
                    dve.wait_ge(sem("sig_ready"), m - 3)
                    dve.scalar_tensor_tensor(lowT[:, m, :], o[:, :], g_ml[:, m - 4:m - 3], moT[:, m - 4, :],
                                             ALU.mult, ALU.mult).then_inc(done, 1)
            for m in range(4, 8):
                wait_high()
                dve.tensor_tensor(r32(lowT[:, m, :]), lowT[:, m, :], r32_read(yT[:, m, :]), ALU.subtract)\
                   .then_inc(sem("y_low_ready"), 1)

            rstds(MT, [(NT, NT + MT, D)])
            for t in range(MT):
                dve.tensor_scalar(mem_rows[:, t, :], mem_rows[:, t, :], rstd[:, NT + t:NT + t + 1], None, ALU.mult)\
                   .then_inc(sem("memn_ready"), 1)

            def add_rows(us, name):
                for n in range(2):
                    for t in range(NT):
                        o = filled(us[name, n, t])
                        v = x_rows[:, t, 512 * n:512 * n + 512]
                        dve.tensor_tensor(v, o[:, :], v, ALU.add).then_inc(done, 1)

            dve.wait_ge(sem("x_again"), 16 * NT)
            add_rows(U, "wo")
            dve.wait_ge(sem("more_loaded"), 16 * 8)
            for k in range(KD // 2):
                o = filled(U["mem_t", k])
                wait_high()
                for kk in range(2):
                    j = 2 * k + kk
                    last = dve.scalar_tensor_tensor(r32(mem_lo[:, j, :]), o[:, MEM * kk:MEM * kk + MEM], g_mem[:, j:j + 1],
                                                    r32_read(memT[:, j, :]), ALU.mult, ALU.subtract)
                last.then_inc(done, 1)
            rstds(NT, [(8, 8 + NT, D)])
            normalise(8, sem("x1n_ready"))
            low_cols(U, "x1_t", g_x)

            for i in range(16 + 2):
                if i < 16:
                    o = filled(U["xs", i])
                    c = i % 8
                    own(dve.tensor_reduce(mx[:, c:c + 1], o[:, 0:MEM], AX.X, ALU.max))
                    dve.tensor_scalar(neg[:, c:c + 1], mx[:, c:c + 1], -1.0 / 16, None, ALU.mult)\
                       .then_inc(sem("xmax_ready"), 1)
                if 1 <= i <= 16:
                    j = i - 1
                    c = j % 8
                    wait_emptied(dve, U["xs", j])
                    own(dve.reciprocal(rz[:, c:c + 1], zsum[:, c:c + 1]))
                    dve.tensor_scalar(xe[:, j % 4, :], xe[:, j % 4, :], rz[:, c:c + 1], None, ALU.mult)\
                       .then_inc(sem("xp_ready"), 1)
                if i >= 2:
                    j = i - 2
                    h, t = divmod(j, NT)
                    o = filled(U["xp", j])
                    if h >= 2 and t == 0:
                        dve.wait_ge(bank_filled, U["xo", h - 2, 1].filled)
                    dve.tensor_copy(pT[:, h % 2, :, P * t:P * t + P], o[:, 0:MEM].rearrange("p (k q) -> p k q", q=P))\
                       .then_inc(done, 1)
                    if t == NT - 1:
                        for d in range(2):
                            o = filled(U["xo", h, d])
                            wait_high()
                            dve.tensor_tensor(r32(lowT[:, 2 * h + d, :]), o[:, :], r32_read(yT[:, 2 * h + d, :]),
                                              ALU.subtract)\
                               .then_inc(done, 1)
            add_rows(U, "xw")
            rstds(NT, [(12, 12 + NT, D)])
            normalise(12, sem("x2n_ready"))
            for k in range(1, KD, 2):
                o = filled(U["x2_t", k])
                dve.tensor_scalar(hT[:, k, :], o[:, :], g_ffn[:, k:k + 1], None, ALU.mult).then_inc(done, 1)

            for t in range(NT):
                own(dve.memset(lg[:, t, GROUPS:8], NEG))
            for t in range(NT):
                o = filled(U["route", t])
                own(dve.tensor_tensor(lg[:, t, 0:GROUPS], o[:, 0:GROUPS], router_b[:, 0:GROUPS], ALU.add))
                dve.tensor_tensor(lg[:, t, 8:40], o[:, GROUPS:GROUPS + EXPERTS], router_b[:, GROUPS:], ALU.add)\
                   .then_inc(done, 1)
                wait_emptied(dve, U["route", t])
                own(dve.max(top[:, t, 0:8], lg[:, t, 0:8]))
                own(dve.max_index(top_i[:, 16 * t:16 * t + 8], top[:, t, 0:8], lg[:, t, 0:8]))
                own(dve.tensor_copy(gf[:, t:t + 1], top_i[:, 16 * t:16 * t + 1]))
                own(dve.tensor_scalar(ohg, const("item_row")[:, 0:GROUPS], gf[:, t:t + 1], None, ALU.is_equal))
                own(dve.tensor_scalar(el[:, t, :], lg[:, t, 8:16], ohg[:, 0:1], None, ALU.mult))
                for g in range(1, GROUPS):
                    own(dve.scalar_tensor_tensor(el[:, t, :], lg[:, t, 8 + 8 * g:16 + 8 * g], ohg[:, g:g + 1],
                                                 el[:, t, :], ALU.mult, ALU.add))
                own(dve.max(top[:, t, 8:16], el[:, t, :]))
                own(dve.max_index(top_i[:, 16 * t + 8:16 * t + 16], top[:, t, 8:16], el[:, t, :]))
                own(dve.tensor_copy(ea[:, t:8:NT], top_i[:, 16 * t + 8:16 * t + 10]))
                own(dve.scalar_tensor_tensor(ea[:, t:8:NT], gf[:, t:t + 1].to_broadcast([P, 2]), float(PER_GROUP),
                                             ea[:, t:8:NT], ALU.mult, ALU.add))
                for c in range(2):
                    last = dve.tensor_scalar(sel1h[:, c, t, :], const("item_row")[:, 0:EXPERTS],
                                             ea[:, NT * c + t:NT * c + t + 1], None, ALU.is_equal)
                own(last)
                dve.tensor_tensor(selb[:, t, :], sel1h[:, 0, t, :], sel1h[:, 1, t, :], ALU.add)\
                   .then_inc(sem("chosen_ready"), 1)
                for c in range(2):
                    last = dve.tensor_scalar(dif[:, t, 8 * c:8 * c + 8], top[:, t, 8 * c:8 * c + 8],
                                             top[:, t, 8 * c:8 * c + 1], None, ALU.subtract)
            last.then_inc(sem("dif_ready"), 1)
            dve.wait_ge(sem("pexp_ready"), 1)
            own(dve.tensor_reduce(zg, pexp[:, :, 0:8], AX.X, ALU.add))
            own(dve.tensor_tensor(r4a, pexp[:, :, 8], pexp[:, :, 9], ALU.add))
            own(dve.tensor_tensor(r4b, r4a, zg, ALU.mult))
            own(dve.reciprocal(r4c, r4b))
            for c in range(2):
                last = dve.tensor_tensor(comb[:, NT * c:NT * c + NT], pexp[:, :, 8 + c], r4c, ALU.mult)
            own(last)
            for c in range(2):
                last = dve.tensor_scalar(toks[:, NT * c:NT * c + NT], const("tok_col"), SEQ * c - NOWHERE, None, ALU.add)
            own(last)
            for c in range(2):
                last = dve.tensor_scalar(tokg[:, NT * c:NT * c + NT], const("tok_col"), -NOWHERE, None, ALU.add)
            own(last)
            own(dve.tensor_scalar(half5[:, 0:1], const("half_col"), 0.5, None, ALU.mult))
            for t in range(NT):
                o = filled(U["rank", t])
                for c in range(2):
                    last = dve.tensor_tensor_reduce(junk32, o[:, 0:EXPERTS], sel1h[:, c, t, :], 1.0, 0.0, ALU.mult, ALU.add,
                                                    rk[:, NT * c + t:NT * c + t + 1])
                    if c == 0:
                        own(last)
                last.then_inc(done, 1)
                wait_emptied(dve, U["rank", t])
            o = filled(U["count",])
            dve.tensor_copy(cnt, o[:, 0:EXPERTS]).then_inc(done, 1)
            wait_emptied(dve, U["count",])
            own(dve.memset(zero32, 0.0))
            own(dve.tensor_scalar(nov, cnt, float(SLOTS), None, ALU.is_gt))
            for j in range(2, TILES):
                own(dve.scalar_tensor_tensor(nov, cnt, float(SLOTS * j), nov, ALU.is_gt, ALU.add))
            own(dve.tensor_tensor_scan(ovend, nov, zero32, 0.0, ALU.add, ALU.add))
            own(dve.tensor_tensor(ovbase, ovend, nov, ALU.subtract))
            own(dve.tensor_copy(over_n, ovend[0:1, EXPERTS - 1:EXPERTS]))
            own(dve.tensor_tensor(over_cmp.rearrange("p (k e) -> p k e", e=EXPERTS),
                                  const("item_row", 1)[:, 0:OVER + 1].unsqueeze(2).to_broadcast([1, OVER + 1, EXPERTS]),
                                  ovend[0:1, :].unsqueeze(1).to_broadcast([1, OVER + 1, EXPERTS]), ALU.is_ge))
            own(dve.tensor_reduce(over_row, over_cmp.rearrange("p (k e) -> p k e", e=EXPERTS), AX.X, ALU.add))
            own(dve.tensor_scalar(over_e[:, :], over_row, EXPERTS - 1.0, None, ALU.min))
            for c in range(2 * NT):
                own(dve.tensor_tensor_reduce(junk32, ovbase, sel1h[:, c // NT, c % NT, :], 1.0, 0.0, ALU.mult, ALU.add,
                                             ovb[:, c:c + 1]))
            jt = slot
            own(dve.tensor_scalar(jt, rk, float(SLOTS), None, ALU.is_ge))
            for j in range(2, TILES):
                own(dve.scalar_tensor_tensor(jt, rk, float(SLOTS * j), jt, ALU.is_ge, ALU.add))
            own(dve.tensor_tensor(item, jt, ovb, ALU.add))
            own(dve.scalar_tensor_tensor(item, item, EXPERTS - 1.0, ea, ALU.add, ALU.subtract))
            own(dve.tensor_scalar(ovb, jt, 1.0, None, ALU.min))
            own(dve.tensor_tensor(item, item, ovb, ALU.mult))
            own(dve.tensor_tensor(item, item, ea, ALU.add))
            own(dve.scalar_tensor_tensor(slot, jt, -float(SLOTS), rk, ALU.mult, ALU.add))
            for s in range(2 * NT):
                if s >= 2:
                    dve.wait_ge(sem("onehots_used"), s - 1)
                dve.tensor_scalar(oh_slot[s % 2], const("slot_row"), slot[:, s:s + 1], None, ALU.is_equal)
                for n, v in enumerate((tokg, toks, comb)):
                    last = dve.tensor_scalar(oh_item[s % 2][:, ITEMS * n:ITEMS * (n + 1)], const("item_row"),
                                             item[:, s:s + 1], v[:, s:s + 1], ALU.is_equal, ALU.mult)
                last.then_inc(sem("onehots_ready"), 1)
            o = filled(U["table",])
            dve.tensor_scalar(tab_g, o[:, 0:ITEMS], half5[:, 0:1], NOWHERE, ALU.add, ALU.add)
            dve.tensor_scalar(tab_s, o[:, ITEMS:2 * ITEMS], const("half_col"), NOWHERE, ALU.add, ALU.add)
            dve.tensor_copy(tab_w, o[:, 2 * ITEMS:3 * ITEMS]).then_inc(done, 1)
            wait_emptied(dve, U["table",])

            def rows_cols(b):
                g = g_xh.rearrange("p (h k) -> p k h", h=2).unsqueeze(3).to_broadcast([P, 4, 2, SLOTS])
                return dve.tensor_tensor(xgT[b], bank[b][:, :].rearrange("p (k h s) -> p k h s", k=4, h=2), g, ALU.mult)

            def gate_up(b):
                return dve.tensor_tensor(gg[b][0:SLOTS, :], sil[b][SLOTS:P, :], bank[2 + b][SLOTS:P, :], ALU.mult)

            def weigh(b, e):
                return dve.tensor_scalar(y_sb[b], bank[6 + b][:, :], tab_w[:, bass.ds(e, 1)], None, ALU.mult)

            def step_cols(i, b, first=False):
                e = 2 * i + b
                dve.wait_ge(sem("xg_turned"), e + 1)
                if not first:
                    dve.wait_ge(sem("h_done"), e - 1)
                rows_cols(b).then_inc(sem("xgT_ready"), 1)

            def step_gate(i, b, first=False):
                e = 2 * i + b
                dve.wait_ge(sem("silu_e_ready"), e + 1)
                if not first:
                    dve.wait_ge(sem("g_turned"), e - 1)
                gate_up(b).then_inc(sem("g_ready"), 1)

            def step_weigh(i, b, first=False):
                e = 2 * i + b
                dve.wait_ge(sem("y_done"), e + 1)
                if not first:
                    dve.wait_ge(sem(f"y_stored{b}"), 16 * i)
                weigh(b, e).then_inc(sem("y_ready"), 1)

            def pair(i, first, last, second=False):
                step_cols(i, 1, first)
                step_gate(i, 0, first)
                if not first:
                    step_weigh(i - 1, 1, second)
                if not last:
                    step_cols(i + 1, 0)
                step_gate(i, 1, first)
                step_weigh(i, 0, first)

            step_cols(0, 0, True)
            pair(0, True, False)
            pair(1, False, False, True)
            with dve.Fori(2, EXPERTS // 2 - 1) as i:
                pair(i, False, False)
            pair(EXPERTS // 2 - 1, False, True)
            step_weigh(EXPERTS // 2 - 1, 1)
            n = dve.value_load(over_n, min_val=0, max_val=OVER)
            with dve.If(n > 0):
                with dve.Fori(0, OVER) as k:
                    dve.wait_ge(sem("ov_xg_turned"), k + 1)
                    rows_cols(0).then_inc(sem("ov_xgT_ready"), 1)
                    dve.wait_ge(sem("ov_silu_ready"), k + 1)
                    gate_up(0).then_inc(sem("ov_g_ready"), 1)
                    dve.wait_ge(sem("ov_y_done"), k + 1)
                    weigh(0, k + EXPERTS).then_inc(sem("y_ready"), 1)
                    dve.wait_ge(sem("ov_stored"), 16 * k + 16)

            dve.wait_ge(sem("g_fin_loaded"), 16)
            for t in range(NT):
                dve.wait_ge(sem(f"y_back{t}"), 64)
                own(dve.tensor_tensor(x_rows[:, t, :], x_rows[:, t, :], y_back[t][:, 0, :], ALU.add))
                dve.tensor_tensor(x_rows[:, t, :], x_rows[:, t, :], y_back[t][:, 1, :], ALU.add)\
                   .then_inc(sem("x3_ready"), 1)
            rstds(NT, [(16, 16 + NT, D)])
            for t in range(NT):
                dve.scalar_tensor_tensor(x_rows[:, t, :], x_rows[:, t, :], rstd[:, 16 + t:17 + t], g_fin, ALU.mult,
                                         ALU.mult).then_inc(sem("x4_ready"), 1)
            rstds(NT, [(20, 20 + NT, D)])
            normalise(20, sem("x4n_ready"))
            own(dve.memset(vbuf[:, :, 0:CONV2 - 1], 0.0))
            low_cols(V, "x4_t", g_a)
            for n in range(2):
                js = range(4 * n, 4 * n + 4)
                for j in js:
                    v, acc = vbuf[:, j % 4, :], cacc[:, j % 4, :]
                    w = lambda tap: conv_w2[:, KD * tap + j:KD * tap + j + 1]
                    o = filled(V["u", j])
                    wait_emptied(dve, V["c", j])
                    dve.tensor_tensor(v[:, CONV2 - 1:], o[:, :], cbuf[:, j % 4, :], ALU.mult).then_inc(done, 1)
                    wait_emptied(dve, V["u", j])
                    own(dve.tensor_scalar(acc, v[:, 0:SEQ], w(0), None, ALU.mult))
                    for tap in range(1, CONV2):
                        own(dve.scalar_tensor_tensor(acc, v[:, tap:tap + SEQ], w(tap), acc, ALU.mult, ALU.add))
                for j in js:
                    wait_emptied(dve, V["z", j])
                    own(dve.tensor_tensor(cacc[:, j % 4, :], cacc[:, j % 4, :], zbuf[:, j % 4, :], ALU.mult))
                for j in js:
                    o = filled(V["b", j])
                    dve.tensor_tensor(y2_lo[:, j, :], o[:, :], cacc[:, j % 4, :], ALU.mult).then_inc(done, 1)
                for j in js:
                    wait_high()
                    dve.tensor_tensor(r32(y2_lo[:, j, :]), y2_lo[:, j, :], r32_read(yT[:, j, :]), ALU.subtract)\
                       .then_inc(sem("y2_low_ready"), 1)
            add_rows(V, "wa")
            rstds(NT, [(24, 24 + NT, D)])
            normalise(24, sem("x5n_ready"))
            for k in range(KD):
                o = filled(V["x5_t", k])
                wait_high()
                for hi, lo, g in ((hkvT, hkv_lo, g_kv), (hT, lowT, g_b)):
                    last = dve.scalar_tensor_tensor(r32(lo[:, k, :]), o[:, :], g[:, k:k + 1], r32_read(hi[:, k, :]),
                                                    ALU.mult, ALU.subtract)
                last.then_inc(done, 1)
            for t in range(NT):
                wait_emptied(dve, V["kv", t])
                dve.tensor_reduce(ss[:, WKV * t:WKV * t + WKV], sq_buf[:, t, 0:256].rearrange("p (g d) -> p g d", d=WD),
                                  AX.X, ALU.add).then_inc(sem("sq_used"), 1)
            for n in range(2):
                for t in range(NT):
                    wait_emptied(dve, V["q", n, t])
                    c = 16 + WH * t + 8 * n
                    dve.tensor_reduce(ss[:, c:c + 8], sq_buf[:, t, :].rearrange("p (h d) -> p h d", d=WD), AX.X, ALU.add)\
                       .then_inc(sem("sq_used"), 1)
            dve.wait_ge(sem("sq_used"), 3 * NT)
            rstds(0, [(0, 80, WD)])

            def unit(v, c0, gain, n):
                own(dve.tensor_tensor(v, v, rstd[:, c0:c0 + n].unsqueeze(2).to_broadcast([P, n, WD]), ALU.mult))
                own(dve.tensor_tensor(v, v, gain.unsqueeze(1).to_broadcast([P, n, WD]), ALU.mult))

            def rope(v, n):
                for t in range(NT):
                    hd = v[:, n * t:n * t + n, :]
                    r1, r2 = hd[:, :, 0:ROT // 2], hd[:, :, ROT // 2:ROT]
                    cs = [const(x)[:, 8 * t:8 * t + 8].unsqueeze(1).to_broadcast([P, n, ROT // 2]) for x in ("cos2", "sin2")]
                    tmp = [f3(E, (n, ROT // 2), SEQ * s + 128 * (t % 4)) for s in range(4)]
                    dve.tensor_tensor(tmp[0], r1, cs[0], ALU.mult)
                    dve.tensor_tensor(tmp[1], r2, cs[1], ALU.mult)
                    dve.tensor_tensor(tmp[2], r2, cs[0], ALU.mult)
                    own(dve.tensor_tensor(tmp[3], r1, cs[1], ALU.mult))
                    dve.tensor_tensor(r1, tmp[0], tmp[1], ALU.subtract)
                    own(dve.tensor_tensor(r2, tmp[2], tmp[3], ALU.add))

            unit(k_rows, 0, k_gain, NT * WKV)
            rope(k_rows, WKV)
            dup = f3(B2, (NT * WKV, 2, WD))
            for c in range(2):
                last = dve.tensor_copy(dup[:, :, c, :], k_rows)
            last.then_inc(sem("k2_ready"), 1)
            qh = f3(XN, (NT * WH, WD))
            for t in range(NT):
                unit(qh[:, WH * t:WH * t + WH, :], 16 + WH * t, q_gain, WH)
            rope(qh, WH)
            dve.nop().then_inc(sem("q2_ready"), 1)
            for g in range(WKV):
                o = filled(V["k_t", g])
                dve.tensor_copy(k2T[:, g, :], o[:, :]).then_inc(done, 1)

            def low_of(j):
                nb, g = divmod(j, WKV)
                wait_high()
                v = lambda t: t[:, 2 * g:2 * g + 2, P * nb:P * nb + P]
                dve.tensor_tensor(r32(v(lowT)), v(lowT), r32_read(v(yT2)), ALU.subtract).then_inc(sem("y3_low_ready"), 1)

            for i in range(16 + 3):
                if i < 16:
                    nb, g = divmod(i, WKV)
                    n = 2 * P if nb else P
                    S = wS[:, i % 3, :, 0:n]
                    band = const("band")[:, 2 * P - n:].unsqueeze(1).to_broadcast([P, 2, n])
                    if i >= 3:
                        dve.wait_ge(bank_filled, V["wp", i - 3, 1].filled)
                    for hh in range(2):
                        o = filled(V["ws", i, hh])
                        dve.scalar_tensor_tensor(S[:, 2 * hh:2 * hh + 2, :],
                                                 o[:, :].rearrange("p (r k) -> p r k", r=2)[:, :, 0:n], WD ** -0.5, band,
                                                 ALU.mult, ALU.add).then_inc(done, 1)
                    wait_emptied(dve, V["ws", i, 1])
                    c = 8 * (i % 2)
                    m4, n4 = mx[:, c:c + 4], neg[:, c:c + 4]
                    own(dve.tensor_reduce(m4, S, AX.X, ALU.max))
                    sk = sink[:, 4 * g:4 * g + 4].rearrange("p (r h) -> p h r", h=2)
                    own(dve.tensor_tensor(m4.rearrange("p (h r) -> p h r", h=2), m4.rearrange("p (h r) -> p h r", h=2), sk,
                                          ALU.max))
                    own(dve.tensor_scalar(n4, m4, -1.0, None, ALU.mult))
                    s4 = stat[:, 4 * (i % 2):4 * (i % 2) + 4]
                    dve.tensor_tensor(s4.rearrange("p (h r) -> p h r", h=2), n4.rearrange("p (h r) -> p h r", h=2), sk,
                                      ALU.add).then_inc(sem("w_max_ready"), 1)
                if 1 <= i <= 16:
                    j = i - 1
                    n = 2 * P if j // WKV else P
                    c = 8 * (j % 2)
                    dve.wait_ge(sem("w_exp_ready"), j + 1)
                    own(dve.tensor_tensor(rz[:, c:c + 4], zsum[:, c:c + 4], stat[:, 16 + 4 * (j % 2):20 + 4 * (j % 2)],
                                          ALU.add))
                    own(dve.reciprocal(rz[:, c + 4:c + 8], rz[:, c:c + 4]))
                    S = wS[:, j % 3, :, 0:n]
                    dve.tensor_tensor(S, S, rz[:, c + 4:c + 8].unsqueeze(2).to_broadcast([P, 4, n]), ALU.mult)\
                       .then_inc(sem("wp_ready"), 1)
                if 2 <= i <= 17:
                    j = i - 2
                    nb, g = divmod(j, WKV)
                    o = filled(V["wv", j])
                    wait_emptied(dve, V["zz", 7])
                    dve.tensor_tensor(lowT[:, 2 * g:2 * g + 2, P * nb:P * nb + P],
                                      o[:, 0:256].rearrange("p (r q) -> p r q", r=2),
                                      zT[:, 2 * g:2 * g + 2, P * nb:P * nb + P], ALU.mult).then_inc(done, 1)
                if i >= 3:
                    low_of(i - 3)
            add_rows(V, "wb")


def kernel(**inputs):
    import concourse.bacc as bacc
    from concourse.bass_utils import run_bass_kernel_spmd

    nc = bacc.Bacc("TRN2", target_bir_lowering=False, num_devices=1)
    arrays, a = {}, {}
    given = {name: np.ascontiguousarray(inputs[name]) for name in INS}
    given.update(shape_constants())
    for name, v in given.items():
        arrays[f"in_{name}"] = v
        a[name] = nc.dram_tensor(f"in_{name}", v.shape, mybir.dt.from_np(v.dtype), kind="ExternalInput").ap()
    out = nc.dram_tensor("out_0", (1, SEQ, D), F32, kind="ExternalOutput").ap()
    build(nc, a, out)
    r = run_bass_kernel_spmd(nc, [arrays], core_ids=[0])
    return r.results[0]["out_0"]
```

```python
import math
from contextlib import ExitStack

import numpy as np

import concourse.bass as bass
from concourse import mybir

F32 = mybir.dt.float32
F32R = mybir.dt.float32r
I32 = mybir.dt.int32
U32 = mybir.dt.uint32
ALU = mybir.AluOpType
ACT = mybir.ActivationFunctionType
AX = mybir.AxisListType

P = 128
D = 1024
SEQ = 512
NT = SEQ // P
KD = D // P
MEM = 256
MT = MEM // P
HEADS = 4
DA_DIM = 64
LAM_INIT = 0.8 - 0.6 * math.exp(-0.0)
EPS = 1e-6
NEG = -1e30
CONV1 = 4
CONV2 = 3
GROUPS = 4
EXPERTS = 32
PER_GROUP = EXPERTS // GROUPS
SLOTS = 64
TILES = SEQ // SLOTS
OVER = 2 * SEQ // SLOTS - 1
ITEMS = EXPERTS + OVER
NOWHERE = 4096.0
WH = 16
WKV = 4
WD = 64
ROT = 16
CHUNK = 4096
HALF = CHUNK // 2
GATE_M = 36

CONST_COLS = [("ident", P), ("mask_qk", P), ("mask_kq", P), ("rot", P), ("before", P), ("ones", P),
              ("slot_row", P), ("item_row", ITEMS), ("tok_col", NT), ("band", 2 * P),
              ("cos2", NT * ROT // 2), ("sin2", NT * ROT // 2), ("half_col", 1)]
CONST_AT = {}
_n = 0
for _name, _c in CONST_COLS:
    CONST_AT[_name] = (_n, _c)
    _n += _c
CONST_N = _n


def shape_constants():
    c = np.zeros((P, CONST_N), np.float32)

    def put(name, a):
        at, n = CONST_AT[name]
        c[:, at:at + n] = np.asarray(a, np.float32).reshape(P, n)

    i = np.arange(P)
    put("ident", np.eye(P))
    put("mask_qk", np.where(i[None, :] <= i[:, None], 0.0, NEG))
    put("mask_kq", np.where(i[:, None] <= i[None, :], 0.0, NEG))
    rot = np.zeros((P, P))
    for base in (0, DA_DIM):
        for j in range(DA_DIM // 2):
            rot[base + DA_DIM // 2 + j, base + j] = -1.0
            rot[base + j, base + DA_DIM // 2 + j] = 1.0
    put("rot", rot)
    put("before", i[:, None] < i[None, :])
    put("ones", np.ones((P, P)))
    put("slot_row", np.broadcast_to(i % SLOTS, (P, P)))
    put("item_row", np.broadcast_to(np.arange(ITEMS), (P, ITEMS)))
    put("tok_col", i[:, None] + P * np.arange(NT)[None, :])
    q, k = i[:, None], np.arange(2 * P)[None, :]
    put("band", np.where((k <= q + P) & (k > q), 0.0, NEG))
    pos = np.arange(SEQ, dtype=np.float32)
    inv = np.float32(500000.0) ** (-np.arange(0, ROT, 2, dtype=np.float32) / np.float32(ROT))
    ang = (pos[:, None] * inv[None, :]).astype(np.float32)
    rows = lambda a: a.reshape(NT, P, ROT // 2).transpose(1, 0, 2).reshape(P, -1)
    put("cos2", rows(np.cos(ang)))
    put("sin2", rows(np.sin(ang)))
    put("half_col", (i >= SLOTS) * 2.0 * SEQ)
    inv = np.float32(10000.0) ** (-np.arange(0, DA_DIM, 2, dtype=np.float32) / np.float32(DA_DIM))
    ang = (pos[:, None] * inv[None, :]).astype(np.float32).T
    rope = np.concatenate([np.tile(np.cos(ang), (4, 1)), np.tile(np.sin(ang), (4, 1))], axis=1)
    pick = np.zeros((HEADS, HEADS, P), np.float32)
    for h in range(HEADS):
        pick[h, h, :] = -1.0
    return {"consts": c, "rope": rope.astype(np.float32), "pick": pick.reshape(HEADS, HEADS * P)}


def first_plan():
    plan = [(("x_t", k), "dve") for k in range(KD)]
    plan += [(("gate",), "dve")]
    for j in range(2 * HEADS):
        plan.append((("qk", j), "act"))
        if j >= 1:
            plan.append((("qk_rot", j - 1), "dve"))
    plan.append((("dv", 0), "act"))
    plan.append((("qk_rot", 2 * HEADS - 1), "dve"))
    plan += [(("dv", t), "act") for t in range(1, NT)]
    for i in range(16 + 2):
        if i < 16:
            plan += [(("ds", i, 0), "act"), (("ds", i, 1), "act")]
            plan.append((("proj", i), "dve" if 8 <= i < 12 else "act"))
        if 1 <= i <= 16:
            plan.append((("da_t", i - 1), "dve"))
        if i >= 2:
            plan.append((("do", i - 2), "act"))
    plan.append((("gates_t",), "dve"))
    for h in range(HEADS + 1):
        if h < HEADS:
            plan.append((("m_row", h), "act"))
            plan += [(("ms", h, kb), "dve") for kb in range(NT)]
        if h >= 1:
            plan += [(("mh", h - 1, qb), "dve") for qb in range(NT)]
    plan += [(("y_t", m), "dve") for m in range(8)]
    plan += [(("wo", n, t), "dve") for n in range(2) for t in range(NT)]
    plan += [(("mem_t", k), "dve") for k in range(KD // 2)]
    plan += [(("xk", m), "act") for m in range(8)]
    plan += [(("x1_t", k), "dve") for k in range(KD)]
    plan += [(("xv", n, t), "act") for n in range(2) for t in range(MT)]
    plan += [(("xq", m), "act") for m in range(8)]
    for i in range(16 + 2):
        if i < 16:
            plan.append((("xs", i), "act"))
        if i >= 2:
            plan.append((("xp", i - 2), "dve"))
            if (i - 2) % NT == NT - 1:
                plan += [(("xo", (i - 2) // NT, d), "dve") for d in range(2)]
    plan += [(("xw", n, t), "dve") for n in range(2) for t in range(NT)]
    plan += [(("x2_t", k), "act" if k % 2 == 0 else "dve") for k in range(KD)]
    plan += [(("route", t), "dve") for t in range(NT)]
    plan += [(("rank", t), "dve") for t in range(NT)] + [(("count",), "dve")]
    plan += [(("table",), "dve")]
    return plan


def second_plan():
    plan = [(("x4_t", k), "dve") for k in range(KD)]
    for half in range(2):
        for name, by in (("c", "act"), ("u", "dve"), ("z", "act"), ("b", "dve")):
            plan += [((name, j), by) for j in range(4 * half, 4 * half + 4)]
    plan += [(("wa", n, t), "dve") for n in range(2) for t in range(NT)]
    plan += [(("x5_t", k), "dve") for k in range(KD)]
    plan += [(("kv", t), "act") for t in range(NT)]
    plan += [(("q", n, t), "act") for n in range(2) for t in range(NT)]
    plan += [(("zz", m), "act") for m in range(8)]
    plan += [(("k_t", g), "dve") for g in range(WKV)]
    plan += [(("q_t", p), "act") for p in range(8)]
    for i in range(16 + 3):
        if i < 16:
            plan += [(("ws", i, 0), "dve"), (("ws", i, 1), "dve")]
        if 2 <= i < 18:
            plan += [(("wp", i - 2, kt), "act") for kt in window_tiles(i - 2)]
        if i >= 3:
            plan.append((("wv", i - 3), "dve"))
    plan += [(("wb", n, t), "dve") for n in range(2) for t in range(NT)]
    return plan


def window_tiles(i):
    return [0, 1] if i // WKV > 0 else [1]


class Use:

    def __init__(self, n, what, by, filled, after, of_engine):
        self.what, self.bank, self.by = what, n % 8, by
        self.filled = filled
        self.after = after
        self.emptied = of_engine


def number(plan, base, act0, dve0):
    uses, order, count = {}, [], {"act": act0, "dve": dve0}
    for n, (what, by) in enumerate(plan):
        count[by] += 1
        after = (order[n - 8].by, order[n - 8].emptied) if n >= 8 else None
        u = Use(n, what, by, base + n + 1, after, count[by])
        order.append(u)
        uses[what] = u
    return uses, count["act"], count["dve"]


N_MORE = 3 + 2 + CONV1 + 1 + CONV2 + 5

INS = ["x", "mem", "norm_mix_g", "w_in", "w_out", "da_lambda", "da_subln_g", "ml_conv_w", "ml_conv_b",
       "ml_gate_b", "ml_norm_g", "norm_x_g", "norm_mem_g", "w_xq", "w_xk", "w_xv", "w_xo", "norm_ffn_g",
       "w_router_group", "b_router_group", "w_router_expert", "b_router_expert", "w1", "w3", "w2",
       "norm_final_g", "ln_a_2", "w_in_a_2", "conv_a_2", "w_out_a_2", "ln_kv_2", "w_kv_2", "k_norm_2",
       "ln_b_2", "w_in_b_2", "q_norm_2", "sinks_2", "w_out_b_2"]


def build(nc, a, out):
    U, act1, dve1 = number(first_plan(), 0, 0, 0)
    n1 = len(first_plan())
    V, _, _ = number(second_plan(), n1, act1, dve1)

    ctx = ExitStack()
    with ctx:
        def sb(name, cols, dt=F32, parts=P):
            return ctx.enter_context(nc.sbuf_tensor(name, [parts, cols], dt))

        sems = {}

        def sem(name):
            if name not in sems:
                sems[name] = ctx.enter_context(nc.semaphore(name))
            return sems[name]

        rounded = {}

        def region(name, cols):
            with ExitStack() as place:
                plain = place.enter_context(nc.sbuf_tensor(name, [P, cols], F32))
            rounded[name] = ctx.enter_context(nc.sbuf_tensor(f"{name}_rounded", [P, cols], F32R))
            return plain

        ring = [region(f"ring{i}", CHUNK) for i in range(5)]
        X = sb("X", NT * D)
        XN = region("XN", NT * D)
        HT = region("HT", KD * SEQ)
        A0 = region("A0", KD * SEQ)
        A1 = region("A1", KD * (SEQ + CONV1 - 1))
        B0 = sb("B0", NT * SEQ)
        B1 = sb("B1", NT * HEADS * (P + 1))
        B2 = sb("B2", NT * SEQ)
        E = region("E", NT * SEQ)
        cst = sb("cst", CONST_N)
        pick = sb("pick", HEADS * P, parts=HEADS)
        small = sb("small", 1472)
        ints = sb("ints", 2 * ITEMS + 8, dt=I32)

        bank = [ctx.enter_context(nc.psum_tensor(f"bank{i}", [P, 512], F32)) for i in range(8)]

        xn_dram = nc.dram_tensor("xn_dram", (2 * SEQ, 512), F32).ap()
        y_dram = nc.dram_tensor("y_dram", (4 * SEQ, 512), F32).ap()

        def const(name, rows=P):
            at, n = CONST_AT[name]
            return cst[0:rows, at:at + n]

        ident = const("ident")
        taken = [0]

        def col(n):
            at = taken[0]
            taken[0] += n
            assert taken[0] <= 1472
            return small[:, at:at + n]

        g_mix, g_x, g_mem, g_ffn, g_a, g_kv, g_b = (col(KD) for _ in range(7))
        g_xh = col(KD)
        g_sub, g_ml, conv_w, conv_b = col(1), col(HEADS), col(KD * CONV1), col(KD)
        gate_b = col(2)
        conv_w2 = col(KD * CONV2)
        lam_in, lam_c = col(4 * DA_DIM), col(8)
        router_b = col(GROUPS + EXPERTS)
        k_gain, q_gain, sink = col(WD), col(WD), col(WH)
        ss, ms, root, rstd = col(80), col(80), col(80), col(80)
        stat = col(96)
        mx, neg, zsum, rz = (col(16) for _ in range(4))
        bmT, em = col(32), col(16)
        bT, mT = bmT[:, 0:16], bmT[:, 16:32]
        lam_s, neg_lam, g_sub_s = lam_c[:, 0:4], lam_c[:, 4:5], lam_c[:, 5:6]

        def f3(t, shape, at=0):
            n = int(np.prod(shape))
            v = t[:, at:at + n]
            if len(shape) == 2:
                return v.rearrange("p (a b) -> p a b", a=shape[0])
            return v.rearrange("p (a b c) -> p a b c", a=shape[0], b=shape[1])

        x_rows, xn, hT = f3(X, (NT, D)), f3(XN, (NT, D)), f3(HT, (KD, SEQ))
        w_gates = E[:, 1024:1024 + 8 * KD].rearrange("p (k n) -> p k n", k=KD)
        w_gates_split = [f3(E, (KD, GATE_M), 1152 + KD * GATE_M * s) for s in range(2)]
        cosT, sinT = E[:, 0:SEQ], E[:, SEQ:2 * SEQ]
        qkT = f3(A0, (KD, SEQ))
        convT = f3(A1, (KD, SEQ + CONV1 - 1))
        mqkT = convT[:, :, CONV1 - 1:]
        dv_rows = f3(B0, (NT, SEQ))
        mv_rows = f3(B1, (NT, HEADS, P + 1))
        moT = f3(B2, (HEADS, SEQ))
        e_buf = f3(E, (2, 2, SEQ))
        yT = f3(XN, (KD, SEQ))
        rope_tmp = X[:, 0:SEQ]
        conv_tmp = f3(X, (2, SEQ), 0)
        daT = f3(X, (2, NT, P), 2 * SEQ)
        o_rows = f3(X, (NT, HEADS, P), 4 * SEQ)
        gw = [f3(XN, (1, SEQ), SEQ * i)[0:HEADS, 0, :] for i in range(8)]
        g_i, g_f, g_min, g_l, g_a_sum, g_bb, g_M, g_ex = gw
        d_buf = f3(A0, (2, SEQ), 0)
        arg_diag = f3(A0, (2, SEQ), 2 * SEQ)
        hm_rows = f3(A0, (NT, HEADS, P), 4 * SEQ)
        sdT = f3(HT, (2, NT, SEQ))
        mem_rows = f3(A1, (MT, D))
        memT, mem_lo = f3(A0, (KD, MEM)), f3(A0, (KD, MEM), KD * MEM)
        lowT = f3(ring[4], (KD, SEQ))
        hkv_lo, y2_lo = f3(A1, (KD, SEQ)), f3(A0, (KD, SEQ))
        xqT, xkT, xv_rows = f3(A0, (KD, SEQ)), f3(B2, (KD, MEM)), f3(B0, (MT, D))
        xe = f3(E, (4, MEM))
        pT = f3(B1, (2, MT, SEQ))
        w_slot = [[ring[1], ring[3], A1], [ring[0], ring[2], ring[4]], [A0, HT, XN]]
        over_slot = w_slot[2]
        xg = [E[:, 0:512], E[:, 512:1024], B0[:, 1536:2048], B2[:, 1024:1536]]
        y_sb = [E[:, 1024:1536], E[:, 1536:2048]]
        xgT = [f3(B0, (4, 2, SLOTS), 512 * b) for b in range(2)]
        gT = [f3(B0, (4, SLOTS), 1024 + 256 * b) for b in range(2)]
        sil = [B1[:, 0:512], B1[:, 512:1024]]
        gg = [B1[:, 1024:1536], B1[:, 1536:2048]]
        tab_w = B2[:, 2 * ITEMS:3 * ITEMS]
        router_w = f3(B2, (KD, GROUPS + EXPERTS), 256)
        sel1h = f3(B2, (2, NT, EXPERTS), 600)
        selb = f3(B2, (NT, EXPERTS), 860)
        rw = B2[:, 1000:2048]
        tab_g, tab_s = ints[:, 0:ITEMS], ints[:, ITEMS:2 * ITEMS]
        idx_g = [ints[:, 2 * ITEMS + q:2 * ITEMS + q + 1] for q in range(4)]
        idx_s = [ints[:, 2 * ITEMS + 4 + b:2 * ITEMS + 5 + b] for b in range(2)]
        over_n = ints[0:1, 2 * ITEMS + 6:2 * ITEMS + 7]
        over_e = sb("over_e", OVER + 1, dt=I32, parts=1)

        dve_n, pool_n = [0], [0]
        act_step, dve_step, pool_step = sem("act_step"), sem("dve_step"), sem("pool_step")
        bank_filled = sem("bank_filled")
        emptied = {"act": sem("emptied_by_act"), "dve": sem("emptied_by_dve")}

        def wait_emptied(eng, use):
            eng.wait_ge(emptied[use.by], use.emptied)

        def then_own(eng, ins, step, n):
            n[0] += 1
            ins.then_inc(step, 1)
            eng.wait_ge(step, n[0])

        def w_cols(w, c0, n=512):
            return w.rearrange("(p k) n -> p k n", k=KD)[:, :, c0:c0 + n]

        def w_nat(w, c0, n=512):
            return w.rearrange("(k p) n -> p k n", p=P)[:, :, c0:c0 + n]

        lg = f3(rw, (NT, GROUPS + EXPERTS), 0)
        el = f3(rw, (NT, PER_GROUP), 224)
        dif, pexp = f3(rw, (NT, 8), 256), f3(rw, (NT, 8), 320)
        tmp_g, tmp_e = f3(rw, (NT, GROUPS), 288), f3(rw, (NT, PER_GROUP), 352)
        most_g, most_1, most_2, chosen_g = (rw[:, 160 + NT * n:160 + NT * (n + 1)] for n in range(4))
        sel8 = f3(B2, (2 * NT, EXPERTS), 600)
        of_group = f3(E, (NT, GROUPS, PER_GROUP), 1280)
        of_choice, of_choice8 = f3(E, (2, NT, EXPERTS), 1280), f3(E, (2 * NT, EXPERTS), 1280)
        rk, ovb, ea, slot, item, comb, tokg, toks = (rw[:, 384 + 8 * n:392 + 8 * n] for n in range(8))
        r4b, zg, half5 = (rw[:, 448 + 4 * n:452 + 4 * n] for n in range(3))
        oh_slot, oh_item = f3(B1, (2 * NT, P)), f3(B0, (2 * NT, 3, ITEMS))
        is_item = f3(rw, (2 * NT, ITEMS), 480)
        cnt, nov, ovend, ovbase, zero32 = (E[:, 1024 + EXPERTS * n:1024 + EXPERTS * (n + 1)] for n in range(5))
        over_cmp = E[0:1, 1280:1280 + (OVER + 1) * EXPERTS]
        over_row = E[0:1, 1900:1900 + OVER + 1]
        y_back = [f3(XN if t < 2 else A0, (2, D), 2048 * (t % 2)) for t in range(NT)]
        g_fin = B0[:, 0:D]

        cbuf, zbuf = f3(B2, (4, SEQ)), f3(B0, (4, SEQ))
        vbuf = f3(B1, (4, SEQ + CONV2 - 1))
        cacc = f3(E, (4, SEQ))
        hkvT = f3(A0, (KD, SEQ))
        k_rows, v_rows2 = f3(B0, (NT * WKV, WD)), f3(B0, (NT, WKV * WD), NT * WKV * WD)
        q_rows = f3(XN, (NT, D))
        sq_buf = f3(E, (4, SEQ))
        k_dup, k2T = f3(B2, (NT, 2 * WKV * WD)), f3(B1, (WKV, SEQ))
        q2T, zT = f3(A0, (KD, SEQ)), f3(A1, (KD, SEQ))
        wS = f3(HT, (3, 4, 2 * P))
        wpT = f3(E, (2, 2, 4 * P))
        yT2 = f3(XN, (KD, SEQ))

        w_in = a["w_in"][0]
        w_a, w_b = a["w_in_a_2"][0], a["w_in_b_2"][0]
        chunk_list, chunk_no = [], {}

        def add_chunk(name, src, us, last, by_half=True):
            chunk_no[name] = len(chunk_list)
            chunk_list.append((src, us[last].filled, by_half))

        add_chunk("dq", w_cols(w_in, 0), U, ("qk", 3), False)
        add_chunk("dk", w_cols(w_in, 512), U, ("qk", 7), False)
        add_chunk("dv", w_cols(w_in, 1024), U, ("dv", 3), False)
        for n, name in enumerate(("mq", "mk", "mv", "mo")):
            add_chunk(name, w_cols(w_in, 1536 + 512 * n), U, ("proj", 4 * n + 3), False)
        for n in range(2):
            add_chunk(f"wo{n}", w_nat(a["w_out"][0], 512 * n), U, ("wo", n, 3))
        for n in range(2):
            add_chunk(f"xk{n}", w_cols(a["w_xk"][0], 512 * n), U, ("xk", 4 * n + 3))
        for n in range(2):
            add_chunk(f"xv{n}", w_cols(a["w_xv"][0], 512 * n), U, ("xv", n, MT - 1))
        for n in range(2):
            add_chunk(f"xq{n}", w_cols(a["w_xq"][0], 512 * n), U, ("xq", 4 * n + 3))
        for n in range(2):
            add_chunk(f"xw{n}", w_nat(a["w_xo"][0], 512 * n), U, ("xw", n, 3))
        first_chunks = len(chunk_list)
        for n in range(2):
            for f, name in ((1, "c"), (2, "u"), (3, "z"), (0, "b")):
                add_chunk(f"{name}{n}", w_cols(w_a, D * f + 512 * n), V, (name, 4 * n + 3))
        for n in range(2):
            add_chunk(f"wa{n}", w_nat(a["w_out_a_2"][0], 512 * n), V, ("wa", n, 3))
        add_chunk("kv", w_cols(a["w_kv_2"], 0), V, ("kv", 3))
        for n in range(2):
            add_chunk(f"q{n}", w_cols(w_b, 512 * n), V, ("q", n, 3))
        for n in range(2):
            add_chunk(f"zz{n}", w_cols(w_b, D + 512 * n), V, ("zz", 4 * n + 3))
        for n in range(2):
            add_chunk(f"wb{n}", w_nat(a["w_out_b_2"][0], 512 * n), V, ("wb", n, 3))

        w_loaded = [sem(f"w_loaded{q}") for q in range(4)]
        w_high_ready, w_split = sem("w_high_ready"), sem("w_split")
        first_half_read = sem("first_half_read")

        def quarter(g, high):
            at = HALF * (g % 2)
            return f3(ring[(2 if high else 0) + g // 2 % 2], (4, 512), at)

        def wait_half_read(eng, g):
            _, filled, by_half = chunk_list[g // 2]
            if g % 2 == 0 and by_half:
                eng.wait_ge(first_half_read, sum(c[2] for c in chunk_list[:g // 2 + 1]))
            else:
                eng.wait_ge(bank_filled, filled)

        def r32(v):
            return bass.AP(tensor=rounded[v.tensor.name], offset=v.offset, ap=v.ap)

        def r32_read(v):
            return r32(v).bitcast(F32)

        we_loaded = [[sem(f"we_loaded{b}{j}") for j in range(3)] for b in range(3)]

        def expert_weights(e):
            one = lambda w: w[0, bass.ds(e, 1)]
            return [one(a["w1"]).rearrange("o (h p k) n -> p (o h) (k n)", h=2, p=P),
                    one(a["w3"]).rearrange("o (h p k) n -> p (o h) (k n)", h=2, p=P),
                    one(a["w2"]).rearrange("o (p k) n -> p (o k n)", p=P)]

        def as_expert(t, j):
            return f3(t, (2, 2048)) if j < 2 else t[:, 0:CHUNK]

        def w_slot_as(b, j):
            return as_expert(w_slot[b][j], j)

        block = ctx.enter_context(nc.Block())

        @block.sync
        def _(sp):
            consts_loaded = sem("consts_loaded")
            for t in range(NT):
                sp.dma_start(x_rows[:, t, :], a["x"][0, P * t:P * t + P, :]).then_inc(sem(f"x_loaded{t}"), 16)
            sp.dma_start(cst[:, :], a["consts"]).then_inc(consts_loaded, 16)
            sp.dma_start(g_mix, a["norm_mix_g"][0].rearrange("(p k) -> p k", k=KD)).then_inc(consts_loaded, 16)
            sp.dma_start(w_gates, w_cols(w_in, 3584, 8)).then_inc(consts_loaded, 16)
            for g in range(2):
                sp.dma_start(gate_b[32 * g:32 * g + HEADS, g:g + 1], a["ml_gate_b"][0, g].rearrange("(h o) -> h o", o=1),
                             allow_slow_non_contiguous=True).then_inc(consts_loaded, 16)

            def load_half(g):
                c, h = g // 2, g % 2
                sp.dma_start(quarter(g, False), chunk_list[c][0][:, 4 * h:4 * h + 4, :]).then_inc(w_loaded[g % 4], 16)

            for c in range(first_chunks):
                for g in (2 * c, 2 * c + 1):
                    if g >= 4:
                        wait_half_read(sp, g - 4)
                    load_half(g)
                if c == 1:
                    for dst, name, k in ((g_x, "norm_x_g", KD), (g_mem, "norm_mem_g", KD), (g_ffn, "norm_ffn_g", KD),
                                         (g_a, "ln_a_2", KD), (g_b, "ln_b_2", KD)):
                        sp.dma_start(dst, a[name][0].rearrange("(p k) -> p k", k=k)).then_inc(sem("more_loaded"), 16)
                    sp.dma_start(g_kv, a["ln_kv_2"].rearrange("(p k) -> p k", k=KD)).then_inc(sem("more_loaded"), 16)
                    for hf in range(2):
                        sp.dma_start(g_xh[:, 4 * hf:4 * hf + 4],
                                     a["norm_ffn_g"][0, 512 * hf:512 * hf + 512].rearrange("(p k) -> p k", k=4))\
                          .then_inc(sem("more_loaded"), 16)

            for b in range(2):
                for j, src in enumerate(expert_weights(b)):
                    if b == 0 and j == 2:
                        sp.wait_ge(bank_filled, U["mem_t", KD // 2 - 1].filled)
                    elif b == 0:
                        wait_half_read(sp, 2 * chunk_no["xw0"] + 1)
                    else:
                        wait_half_read(sp, 2 * chunk_no["xw1"] + 1)
                    sp.dma_start(w_slot_as(b, j), src).then_inc(we_loaded[b][j], 16)
            h_done, y_done = sem("h_done"), sem("y_done")
            for j, src in enumerate(expert_weights(2)):
                if j < 2:
                    sp.wait_ge(bank_filled, U[(("xs", 15), ("route", NT - 1))[j]].filled)
                else:
                    sp.wait_ge(sem("xn_stored"), 16 * 2 * NT)
                sp.dma_start(w_slot_as(2, j), src).then_inc(we_loaded[2][j], 16)

            def load_expert(e, slot, before):
                for j, src in enumerate(expert_weights(e)):
                    sp.wait_ge(h_done if j < 2 else y_done, before)
                    sp.wait_ge(we_loaded[1][2], 16)
                    sp.dma_start(w_slot_as(slot, j), src).then_inc(we_loaded[slot][j], 16)

            load_expert(3, 0, 1)
            load_expert(4, 1, 2)
            load_expert(5, 0, 4)
            with sp.Fori(3, EXPERTS // 2) as i:
                for b in range(2):
                    load_expert(2 * i + b, 1 - b, 2 * i + b - 1)

            for n, c in enumerate(("u0", "c0")):
                sp.wait_ge(h_done, EXPERTS - 1 + n)
                for h in range(2):
                    load_half(2 * chunk_no[c] + h)

            wait_emptied(sp, U["table",])
            n = sp.value_load(over_n, min_val=0, max_val=OVER)
            with sp.If(n > 0):
                with sp.Fori(0, OVER) as k:
                    sp.wait_ge(sem("y_ready"), k + EXPERTS)
                    e = sp.value_load(over_e[0:1, bass.ds(k, 1)], min_val=0, max_val=EXPERTS - 1)
                    for j, src in enumerate(expert_weights(e)):
                        sp.dma_start(as_expert(over_slot[j], j), src).then_inc(sem("ov_w_loaded"), 16)

            sp.wait_ge(sem("rows_stored"), 1)
            sp.wait_ge(sem("pe_left_experts"), 1)
            for t in range(NT):
                for c in range(2):
                    src = y_dram.rearrange("(h r) n -> r h n", h=2)[512 * c + P * t:512 * c + P * t + P]
                    sp.dma_start(y_back[t][:, c, :].rearrange("p (h n) -> p h n", h=2), src)\
                      .then_inc(sem(f"y_back{t}"), 16)
                if t == 0:
                    sp.dma_start(g_fin, a["norm_final_g"].partition_broadcast(P)).then_inc(sem("g_fin_loaded"), 16)

            for c in range(chunk_no["z0"], len(chunk_list)):
                for g in (2 * c, 2 * c + 1):
                    wait_half_read(sp, g - 4)
                    load_half(g)
            for n in range(2):
                for t in range(NT):
                    wait_emptied(sp, V["wb", n, t])
                    sp.dma_start(out[0, P * t:P * t + P, 512 * n:512 * n + 512],
                                 x_rows[:, t, 512 * n:512 * n + 512]).then_inc(sem("out_stored"), 16)
            sp.wait_ge(sem("out_stored"), 16 * 2 * NT)

        @block.gpsimd
        def _(pool):
            more = sem("more_loaded2")
            pool.memset(convT[:, :, 0:CONV1 - 1], 0.0).then_inc(sem("pads_zero"), 1)
            pool.memset(mv_rows[:, :, :, P:P + 1], 1.0).then_inc(sem("pads_zero"), 1)
            loads = [(E[:, 0:2 * SEQ], a["rope"])]
            loads += [(pick[:, :], a["pick"])]
            loads += [(lam_in, a["da_lambda"][0].rearrange("f n -> (f n)").partition_broadcast(P))]
            loads += [(g_sub, a["da_subln_g"][0].rearrange("(p k) -> p k", k=1))]
            loads += [(g_ml, a["ml_norm_g"][0].rearrange("(h p) -> p h", p=P))]
            loads += [(conv_w.rearrange("p (t m) -> p t m", m=KD)[:, t, :],
                       a["ml_conv_w"][0, t, 0].rearrange("(m p) -> p m", p=P)) for t in range(CONV1)]
            loads += [(conv_b, a["ml_conv_b"][0].rearrange("(m p) -> p m", p=P))]
            loads += [(conv_w2.rearrange("p (t m) -> p t m", m=KD)[:, t, :],
                       a["conv_a_2"][0, t, 0].rearrange("(m p) -> p m", p=P)) for t in range(CONV2)]
            loads += [(router_b[:, 0:GROUPS], a["b_router_group"][0].partition_broadcast(P)),
                      (router_b[:, GROUPS:], a["b_router_expert"][0].partition_broadcast(P)),
                      (k_gain, a["k_norm_2"].partition_broadcast(P)), (q_gain, a["q_norm_2"][0].partition_broadcast(P)),
                      (sink, a["sinks_2"][0].partition_broadcast(P))]
            for dst, src in loads:
                pool.dma_start(dst, src, allow_slow_non_contiguous=True).then_inc(more, 16)
            assert len(loads) == N_MORE

            def low_parts(c0, c1):
                for c in range(c0, c1):
                    for g in (2 * c, 2 * c + 1):
                        pool.wait_ge(w_high_ready, g + 1)
                        lo = quarter(g, False)
                        pool.tensor_tensor(r32(lo), lo, r32_read(quarter(g, True)), ALU.subtract).then_inc(w_split, 1)

            low_parts(0, chunk_no["xk0"])
            pool.wait_ge(bank_filled, U["ms", HEADS - 1, NT - 1].filled)
            pool.dma_start(mem_rows, a["mem"][0].rearrange("(t p) d -> p t d", p=P)).then_inc(sem("mem_loaded"), 16)
            pool.wait_ge(bank_filled, U["y_t", 3].filled)
            for t in range(NT):
                pool.dma_start(x_rows[:, t, :], a["x"][0, P * t:P * t + P, :]).then_inc(sem("x_again"), 16)
            low_parts(chunk_no["xk0"], first_chunks)
            pool.wait_ge(bank_filled, U["xs", 15].filled)
            rg = a["w_router_group"][0].rearrange("(p k) n -> p k n", k=KD)
            re = a["w_router_expert"][0].rearrange("(p k) n -> p k n", k=KD)
            pool.dma_start(router_w[:, :, 0:GROUPS], rg).then_inc(sem("router_loaded"), 16)
            pool.dma_start(router_w[:, :, GROUPS:], re).then_inc(sem("router_loaded"), 16)
            for t in range(NT):
                pool.wait_ge(sem("x2n_ready"), t + 1)
                for hf in range(2):
                    pool.dma_start(xn_dram[512 * hf + P * t:512 * hf + P * t + P, :],
                                   xn[:, t, 512 * hf:512 * hf + 512]).then_inc(sem("xn_stored"), 16)
            pool.wait_ge(bank_filled, U["xo", HEADS - 1, 1].filled)
            for b in range(3):
                then_own(pool, pool.memset(xg[b], 0.0), pool_step, pool_n)
            pool.wait_ge(sem("xn_stored"), 16 * 2 * NT)
            wait_emptied(pool, U["table",])
            then_own(pool, pool.memset(xg[3], 0.0), pool_step, pool_n)

            xg_turned, y_ready = sem("xg_turned"), sem("y_ready")
            first_idx, gather_idx, scatter_idx = sem("first_idx"), sem("gather_idx"), sem("scatter_idx")

            def index(dst, src, written, value):
                pool.tensor_copy(dst, src).then_inc(written, 1)
                pool.wait_ge(sem("xn_stored"), 16 * 2 * NT)
                pool.wait_ge(written, value)

            def gather_rows(q, s="xg_loaded"):
                pool.indirect_dma_start(xg[q], None, xn_dram,
                                        bass.IndirectOffsetOnAxis(ap=idx_g[q].bitcast(U32), axis=0),
                                        bounds_check=2 * SEQ - 1, oob_is_err=False).then_inc(sem(f"{s}{q}"), 16)

            def scatter_rows(b):
                pool.indirect_dma_start(y_dram, bass.IndirectOffsetOnAxis(ap=idx_s[b].bitcast(U32), axis=0),
                                        y_sb[b], None, bounds_check=4 * SEQ - 1, oob_is_err=False)\
                    .then_inc(sem(f"y_stored{b}"), 16)

            for q in range(4):
                index(idx_g[q], tab_g[:, q:q + 1], first_idx, q + 1)
                gather_rows(q)

            def four(i, last):
                for q in range(4):
                    e = 4 * i + q
                    b = q % 2
                    if not last:
                        pool.wait_ge(xg_turned, e + 1)
                        index(idx_g[q], tab_g[:, bass.ds(e + 4, 1)], gather_idx, e + 1)
                        gather_rows(q)
                    pool.wait_ge(y_ready, e + 1)
                    index(idx_s[b], tab_s[:, bass.ds(e, 1)], scatter_idx, e + 1)
                    scatter_rows(b)

            with pool.Fori(0, EXPERTS // 4 - 1) as i:
                four(i, False)
            four(EXPERTS // 4 - 1, True)
            for b in range(2):
                pool.wait_ge(sem(f"y_stored{b}"), 16 * EXPERTS // 2)

            n = pool.value_load(over_n, min_val=0, max_val=OVER)
            with pool.If(n > 0):
                with pool.Fori(1, OVER + 1) as k:
                    index(idx_g[0], tab_g[:, bass.ds(k + (EXPERTS - 1), 1)], sem("ov_gather_idx"), k)
                    gather_rows(0, "ov_xg_loaded")
                    pool.wait_ge(y_ready, k + EXPERTS)
                    index(idx_s[0], tab_s[:, bass.ds(k + (EXPERTS - 1), 1)], sem("ov_scatter_idx"), k)
                    pool.indirect_dma_start(y_dram, bass.IndirectOffsetOnAxis(ap=idx_s[0].bitcast(U32), axis=0),
                                            y_sb[0], None, bounds_check=4 * SEQ - 1, oob_is_err=False)\
                        .then_inc(sem("ov_stored"), 16)
                    pool.wait_ge(sem("ov_stored"), 16 * k)
            pool.nop().then_inc(sem("rows_stored"), 1)
            low_parts(first_chunks, len(chunk_list))

        @block.tensor
        def _(pe):
            done = [0]

            def fill(us, *what):
                u = us[what]
                base = 0 if us is U else n1
                assert u.filled == base + done[0] + 1, what
                done[0] += 1
                if u.after:
                    pe.wait_ge(emptied[u.after[0]], u.after[1])
                return bank[u.bank]

            def gemm(o, lhs, rhs, n=KD):
                for k in range(n):
                    last = pe.matmul(o, lhs(k), rhs(k), start=(k == 0), stop=(k == n - 1))
                return last.then_inc(bank_filled, 1)

            def passes(o, lhs, rhs, k, first, last):
                (a_hi, a_lo), (b_hi, b_lo) = lhs(k), rhs(k)
                pe.matmul(o, r32(a_hi), r32(b_hi), start=first, stop=False)
                pe.matmul(o, r32(a_hi), r32(b_lo), start=False, stop=False)
                return pe.matmul(o, r32(a_lo), r32(b_hi), start=False, stop=last)

            def split_gemm(o, lhs, rhs):
                for k in range(KD):
                    last = passes(o, lhs, rhs, k, k == 0, k == KD - 1)
                return last.then_inc(bank_filled, 1)

            def weights(c):
                def part(k, c0=0, c1=512):
                    g = 2 * c + k // 4
                    return quarter(g, True)[:, k % 4, c0:c1], quarter(g, False)[:, k % 4, c0:c1]
                return part

            def chunk(name):
                c = chunk_no[name]
                pe.wait_ge(w_split, 2 * c + 2)
                return weights(c)

            def gemm_by_half(name, us, fills, n, lhs, rhs):
                c = chunk_no[name]
                part = weights(c)
                outs = [fill(us, *f)[:, 0:n] for f in fills]
                for h in range(2):
                    pe.wait_ge(w_split, 2 * c + h + 1)
                    for m, o in enumerate(outs):
                        for k in range(4 * h, 4 * h + 4):
                            last = passes(o, lambda k: lhs(m, part, k), lambda k: rhs(m, part, k), k, k == 0, k == KD - 1)
                        if h == 1:
                            last.then_inc(bank_filled, 1)
                    if h == 0:
                        last.then_inc(first_half_read, 1)

            def to_rows(name, us, fills, hi, lo):
                gemm_by_half(name, us, fills, 512, lambda m, part, k: (hi[:, k, P * m:P * m + P], lo[:, k, P * m:P * m + P]),
                             lambda m, part, k: part(k))

            def to_cols(name, us, fills, hi, lo, n=SEQ):
                gemm_by_half(name, us, fills, n, lambda m, part, k: part(k, P * m, P * m + P),
                             lambda m, part, k: (hi[:, k, :], lo[:, k, :]))

            def cols(k, c0=0, c1=SEQ):
                return hT[:, k, c0:c1], lowT[:, k, c0:c1]

            def turn(us, name, src, ready):
                for k in range(KD):
                    o = fill(us, name, k)
                    for t in range(NT):
                        if k == 0:
                            pe.wait_ge(ready, t + 1)
                        last = pe.transpose(o[:, P * t:P * t + P], src[:, t, k:D:KD], ident)
                    last.then_inc(bank_filled, 1)

            pe.wait_ge(sem("consts_loaded"), 80)
            turn(U, "x_t", xn, sem("x0n_ready"))
            wait_emptied(pe, U["x_t", 7])
            pe.wait_ge(sem("w_gates_ready"), 1)
            split_gemm(fill(U, "gate")[0:GATE_M, :], lambda k: (w_gates_split[0][:, k, :], w_gates_split[1][:, k, :]), cols)

            def rotate(j):
                o = fill(U, "qk_rot", j)
                wait_emptied(pe, U["qk", j])
                pe.matmul(o[:, :], const("rot"), qkT[:, j, :], start=True, stop=True).then_inc(bank_filled, 1)

            for j in range(2 * HEADS):
                w = chunk("dq" if j < HEADS else "dk")
                m = j % HEADS
                split_gemm(fill(U, "qk", j)[:, :], lambda k: w(k, P * m, P * m + P), cols)
                if j >= 1:
                    rotate(j - 1)
            w = chunk("dv")
            for t in range(NT):
                split_gemm(fill(U, "dv", t)[:, :], lambda k: cols(k, P * t, P * t + P), w)
                if t == 0:
                    rotate(2 * HEADS - 1)

            for i in range(16 + 2):
                if i < 16:
                    h, qb = divmod(i, NT)
                    n = P * (qb + 1)
                    for m in range(2):
                        o = fill(U, "ds", i, m)
                        pe.wait_ge(sem("qk_rotated"), 5 + h)
                        r = slice(64 * m, 64 * m + 64)
                        pe.matmul(o[:, 0:n], qkT[r, h, P * qb:P * qb + P], qkT[r, HEADS + h, 0:n],
                                  start=True, stop=True).then_inc(bank_filled, 1)
                    w = chunk(("mq", "mk", "mv", "mo")[i // 4])
                    m = i % 4
                    o = fill(U, "proj", i)
                    if 8 <= i < 12:
                        split_gemm(o[:, :], lambda k: cols(k, P * m, P * m + P), w)
                    else:
                        split_gemm(o[:, :], lambda k: w(k, P * m, P * m + P), cols)
                if 1 <= i <= 16:
                    j = i - 1
                    o = fill(U, "da_t", j)
                    pe.wait_ge(sem("da_ready"), j + 1)
                    for kb in range(j % NT + 1):
                        last = pe.transpose(o[:, P * kb:P * kb + P], e_buf[:, j % 2, 0, P * kb:P * kb + P], ident)
                    last.then_inc(bank_filled, 1)
                if i >= 2:
                    j = i - 2
                    h, qb = divmod(j, NT)
                    o = fill(U, "do", j)
                    wait_emptied(pe, U["da_t", j])
                    wait_emptied(pe, U["dv", NT - 1])
                    gemm(o[:, 0:P], lambda k: daT[:, j % 2, k, :], lambda k: dv_rows[:, k, P * h:P * h + P], qb + 1)

            o = fill(U, "gates_t")
            pe.wait_ge(sem("gates_ready"), 1)
            for v, src in enumerate((g_bb, g_ex)):
                for t in range(NT):
                    last = pe.transpose(o[:, 16 * v + 4 * t:16 * v + 4 * t + 4], src[:, P * t:P * t + P],
                                        ident[0:HEADS, 0:HEADS])
            last.then_inc(bank_filled, 1)
            pe.wait_ge(sem("more_loaded2"), 16 * N_MORE)
            pe.wait_ge(sem("silu_ready"), 8)
            wait_emptied(pe, U["proj", 11])
            pe.wait_ge(sem("pads_zero"), 2)
            for h in range(HEADS + 1):
                if h < HEADS:
                    pe.matmul(fill(U, "m_row", h)[:, :], pick[:, P * h:P * h + P], g_M, start=True, stop=True)\
                      .then_inc(bank_filled, 1)
                    for kb in range(NT):
                        o = fill(U, "ms", h, kb)
                        pe.matmul(o[:, P * kb:SEQ], mqkT[:, HEADS + h, P * kb:P * kb + P], mqkT[:, h, P * kb:SEQ],
                                  start=True, stop=True).then_inc(bank_filled, 1)
                if h >= 1:
                    for qb in range(NT):
                        o = fill(U, "mh", h - 1, qb)
                        wait_emptied(pe, U["ms", h - 1, qb])
                        gemm(o[:, 0:P + 1], lambda k: sdT[:, (h - 1) % 2, k, P * qb:P * qb + P],
                             lambda k: mv_rows[:, k, h - 1, :], qb + 1)
            for m in range(8):
                o = fill(U, "y_t", m)
                pe.wait_ge(sem("y_rows_ready"), m + 1)
                for t in range(NT):
                    src = o_rows[:, t, m, :] if m < 4 else hm_rows[:, t, m - 4, :]
                    last = pe.transpose(o[:, P * t:P * t + P], src, ident)
                last.then_inc(bank_filled, 1)
            pe.wait_ge(sem("y_low_ready"), 8)
            for n in range(2):
                to_rows(f"wo{n}", U, [("wo", n, t) for t in range(NT)], yT, lowT)

            for k in range(KD // 2):
                o = fill(U, "mem_t", k)
                pe.wait_ge(sem("memn_ready"), MT)
                for kk in range(2):
                    for t in range(MT):
                        last = pe.transpose(o[:, MEM * kk + P * t:MEM * kk + P * t + P],
                                            mem_rows[:, t, 2 * k + kk:D:KD], ident)
                last.then_inc(bank_filled, 1)
            wait_emptied(pe, U["mem_t", KD // 2 - 1])
            for n in range(2):
                to_cols(f"xk{n}", U, [("xk", 4 * n + m) for m in range(4)], memT, mem_lo, MEM)
            turn(U, "x1_t", xn, sem("x1n_ready"))
            for n in range(2):
                to_rows(f"xv{n}", U, [("xv", n, t) for t in range(MT)], memT, mem_lo)
            wait_emptied(pe, U["x1_t", 7])
            for n in range(2):
                to_cols(f"xq{n}", U, [("xq", 4 * n + m) for m in range(4)], hT, lowT)
            wait_emptied(pe, U["xv", 1, MT - 1])
            for i in range(16 + 2):
                if i < 16:
                    h, t = divmod(i, NT)
                    o = fill(U, "xs", i)
                    wait_emptied(pe, U["xq", 2 * h + 1])
                    gemm(o[:, 0:MEM], lambda k: xqT[:, 2 * h + k, P * t:P * t + P], lambda k: xkT[:, 2 * h + k, :], 2)
                if i >= 2:
                    j = i - 2
                    h, t = divmod(j, NT)
                    o = fill(U, "xp", j)
                    pe.wait_ge(sem("xp_ready"), j + 1)
                    for kt in range(MT):
                        last = pe.transpose(o[:, P * kt:P * kt + P], xe[:, j % 4, P * kt:P * kt + P], ident)
                    last.then_inc(bank_filled, 1)
                    if t == NT - 1:
                        wait_emptied(pe, U["xp", j])
                        for d in range(2):
                            c0 = MEM * h + P * d
                            gemm(fill(U, "xo", h, d)[:, :], lambda k: xv_rows[:, k, c0:c0 + P],
                                 lambda k: pT[:, h % 2, k, :], MT)
            wait_emptied(pe, U["xo", HEADS - 1, 1])
            for n in range(2):
                to_rows(f"xw{n}", U, [("xw", n, t) for t in range(NT)], yT, lowT)

            turn(U, "x2_t", xn, sem("x2n_ready"))
            wait_emptied(pe, U["x2_t", 6])
            wait_emptied(pe, U["x2_t", 7])
            pe.wait_ge(sem("router_loaded"), 32)
            for t in range(NT):
                gemm(fill(U, "route", t)[:, 0:GROUPS + EXPERTS], lambda k: hT[:, k, P * t:P * t + P],
                     lambda k: router_w[:, k, :])
            pe.wait_ge(sem("chosen_ready"), 1)
            for t in range(NT):
                o = fill(U, "rank", t)
                for s in range(t + 1):
                    last = pe.matmul(o[:, 0:EXPERTS], const("ones") if s < t else const("before"), selb[:, s, :],
                                     start=(s == 0), stop=(s == t))
                last.then_inc(bank_filled, 1)
            gemm(fill(U, "count")[:, 0:EXPERTS], lambda k: const("ones"), lambda k: selb[:, k, :], NT)
            o = fill(U, "table")
            pe.wait_ge(sem("onehots_ready"), 1)
            gemm(o[:, 0:3 * ITEMS], lambda s: oh_slot[:, s, :], lambda s: oh_item[:, s].rearrange("p v i -> p (v i)"), 2 * NT)
            pe.wait_ge(emptied["act"], act1)
            pe.wait_ge(emptied["dve"], dve1)

            h_done, y_done, xg_turned, g_turned = sem("h_done"), sem("y_done"), sem("xg_turned"), sem("g_turned")

            def turn_rows(q):
                for k in range(4):
                    last = pe.transpose(bank[q % 2][:, P * k:P * k + P], xg[q][:, k:512:4], ident)
                return last

            def hidden(b, slot):
                for n, (hf, k) in enumerate((hf, k) for hf in range(2) for k in range(4)):
                    for j in range(2):
                        w = as_expert(slot[j], j)[:, hf, 512 * k:512 * k + 512]
                        last = pe.matmul(bank[2 + b][64 * j:64 * j + 64, :], xgT[b][:, k, hf, :], w,
                                         start=(n == 0), stop=(n == 7), skip_group_check=True)
                return last

            def turn_gated(b):
                for k in range(4):
                    last = pe.transpose(bank[4 + b][:, SLOTS * k:SLOTS * k + SLOTS], gg[b][0:SLOTS, k:512:4],
                                        ident[0:SLOTS, 0:SLOTS])
                return last

            def down(b, slot):
                w = as_expert(slot[2], 2).rearrange("p (k n) -> p k n", k=4)
                for k in range(4):
                    for hf in range(2):
                        last = pe.matmul(bank[6 + b][64 * hf:64 * hf + 64, :], gT[b][:, k, :],
                                         w[:, k, 512 * hf:512 * hf + 512], start=(k == 0), stop=(k == 3),
                                         skip_group_check=True)
                return last

            def step_turn(i, q):
                pe.wait_ge(sem(f"xg_loaded{q}"), 16 * i + 16)
                turn_rows(q).then_inc(xg_turned, 1)

            def slot_of(i, b):
                if isinstance(i, int) and i < 2:
                    return ((0, 1), (1, 1), (2, 1), (0, 2))[2 * i + b]
                return 1 - b, i + b

            def step_hidden(i, b):
                slot, held = slot_of(i, b)
                pe.wait_ge(sem("xgT_ready"), 2 * i + b + 1)
                for j in range(2):
                    pe.wait_ge(we_loaded[slot][j], 16 * held)
                hidden(b, w_slot[slot]).then_inc(h_done, 1)

            def step_down(i, b, first=False):
                e = 2 * i + b
                slot, held = slot_of(i, b)
                pe.wait_ge(sem("gT_ready"), e + 1)
                pe.wait_ge(we_loaded[slot][2], 16 * held)
                if not first:
                    pe.wait_ge(sem("y_ready"), e - 1)
                down(b, w_slot[slot]).then_inc(y_done, 1)

            def step_gated(i, b):
                pe.wait_ge(sem("consts_loaded"), 80)
                pe.wait_ge(sem("g_ready"), 2 * i + b + 1)
                turn_gated(b).then_inc(g_turned, 1)

            def pair(j, half, first=False, last=False, second=False):
                i = 2 * j + half
                step_hidden(i, 0)
                step_turn(j, 2 * half + 1)
                if not first:
                    step_down(i - 1, 1, first=second)
                step_gated(i, 0)
                step_hidden(i, 1)
                if not last:
                    step_turn(j + half, 2 - 2 * half)
                step_down(i, 0, first=first)
                step_gated(i, 1)

            step_turn(0, 0)
            pair(0, 0, first=True)
            pair(0, 1, second=True)
            with pe.Fori(1, EXPERTS // 4 - 1) as j:
                pair(j, 0)
                pair(j, 1)
            pair(EXPERTS // 4 - 1, 0)
            pair(EXPERTS // 4 - 1, 1, last=True)
            step_down(EXPERTS // 2 - 1, 1)
            pe.wait_ge(sem("y_ready"), EXPERTS)

            wait_emptied(pe, U["table",])
            n = pe.value_load(over_n, min_val=0, max_val=OVER)
            with pe.If(n > 0):
                with pe.Fori(0, OVER) as k:
                    pe.wait_ge(sem("ov_xg_loaded0"), 16 * k + 16)
                    turn_rows(0).then_inc(sem("ov_xg_turned"), 1)
                    pe.wait_ge(sem("ov_xgT_ready"), k + 1)
                    pe.wait_ge(sem("ov_w_loaded"), 48 * k + 48)
                    hidden(0, over_slot).then_inc(sem("ov_h_done"), 1)
                    pe.wait_ge(sem("consts_loaded"), 80)
                    pe.wait_ge(sem("ov_g_ready"), k + 1)
                    turn_gated(0).then_inc(sem("ov_g_turned"), 1)
                    pe.wait_ge(sem("ov_gT_ready"), k + 1)
                    down(0, over_slot).then_inc(sem("ov_y_done"), 1)
                    pe.wait_ge(sem("ov_stored"), 16 * k + 16)
            pe.nop().then_inc(sem("pe_left_experts"), 1)

            done[0] = 0

            turn(V, "x4_t", xn, sem("x4n_ready"))
            wait_emptied(pe, V["x4_t", 7])
            for n in range(2):
                for name in "cuzb":
                    to_cols(f"{name}{n}", V, [(name, 4 * n + m) for m in range(4)], hT, lowT)
            pe.wait_ge(sem("y2_low_ready"), 8)
            for n in range(2):
                to_rows(f"wa{n}", V, [("wa", n, t) for t in range(NT)], yT, y2_lo)
            turn(V, "x5_t", xn, sem("x5n_ready"))
            wait_emptied(pe, V["x5_t", KD - 1])
            to_rows("kv", V, [("kv", t) for t in range(NT)], hkvT, hkv_lo)
            for n in range(2):
                to_rows(f"q{n}", V, [("q", n, t) for t in range(NT)], hT, lowT)
            for n in range(2):
                to_cols(f"zz{n}", V, [("zz", 4 * n + m) for m in range(4)], hT, lowT)
            pe.wait_ge(sem("k2_ready"), 1)
            for g in range(WKV):
                o = fill(V, "k_t", g)
                for t in range(NT):
                    last = pe.transpose(o[:, P * t:P * t + P], k_dup[:, t, P * g:P * g + P], ident)
                last.then_inc(bank_filled, 1)
            pe.wait_ge(sem("q2_ready"), 1)
            for p in range(8):
                o = fill(V, "q_t", p)
                for t in range(NT):
                    last = pe.transpose(o[:, P * t:P * t + P], q_rows[:, t, P * p:P * p + P], ident)
                last.then_inc(bank_filled, 1)
            wait_emptied(pe, V["k_t", WKV - 1])
            wait_emptied(pe, V["q_t", 7])
            for i in range(16 + 3):
                if i < 16:
                    nb, g = divmod(i, WKV)
                    k0, n = (P * (nb - 1), 2 * P) if nb else (0, P)
                    for hh in range(2):
                        o = fill(V, "ws", i, hh)
                        r = slice(64 * hh, 64 * hh + 64)
                        for pr in range(2):
                            last = pe.matmul(o[:, 256 * pr:256 * pr + n], q2T[r, 2 * g + pr, P * nb:P * nb + P],
                                             k2T[r, g, k0:k0 + n], start=True, stop=True)
                        last.then_inc(bank_filled, 1)
                if 2 <= i < 18:
                    j = i - 2
                    nb, g = divmod(j, WKV)
                    pe.wait_ge(sem("wp_ready"), j + 1)
                    for kt in window_tiles(j):
                        o = fill(V, "wp", j, kt)
                        for q in range(4):
                            c0 = P * (kt - (nb == 0))
                            last = pe.transpose(o[:, P * q:P * q + P], wS[:, j % 3, q, c0:c0 + P], ident)
                        last.then_inc(bank_filled, 1)
                if i >= 3:
                    j = i - 3
                    nb, g = divmod(j, WKV)
                    o = fill(V, "wv", j)
                    kts = window_tiles(j)
                    wait_emptied(pe, V["wp", j, 1])
                    for n, kt in enumerate(kts):
                        for hh in range(2):
                            last = pe.matmul(o[64 * hh:64 * hh + 64, 0:256],
                                             v_rows2[:, nb - 1 + kt, WD * g:WD * g + WD],
                                             wpT[:, j % 2, kt, 256 * hh:256 * hh + 256], start=(n == 0),
                                             stop=(n == len(kts) - 1), skip_group_check=True)
                    last.then_inc(bank_filled, 1)
            pe.wait_ge(sem("y3_low_ready"), 16)
            for n in range(2):
                to_rows(f"wb{n}", V, [("wb", n, t) for t in range(NT)], yT2, lowT)


        @block.scalar
        def _(act):
            done = emptied["act"]

            def filled(u):
                act.wait_ge(bank_filled, u.filled)
                return bank[u.bank]

            summed = [0]

            def sums(src, t, c, out_=None):
                n = summed[0]
                summed[0] += 1
                if out_ is None:
                    act.wait_ge(sem("ss_ready"), n - 1)
                    out_ = E[:, D * (n % 2):D * (n % 2) + D]
                act.activation(out_, src[:, t, :], ACT.Square, accum_out=ss[:, c:c + 1]).then_inc(sem("ss_ready"), 1)

            def roots(n, c0, c1):
                act.wait_ge(sem("ms_ready"), n)
                act.activation(root[:, c0:c1], ms[:, c0:c1], ACT.Sqrt).then_inc(sem("root_ready"), 1)

            def high_parts(*names):
                for name in names:
                    for g in (2 * chunk_no[name], 2 * chunk_no[name] + 1):
                        act.wait_ge(w_loaded[g % 4], 16 * (g // 4 + 1))
                        if g >= 4:
                            wait_half_read(act, g - 4)
                        act.activation(r32(quarter(g, True)), quarter(g, False), ACT.Copy).then_inc(w_high_ready, 1)

            def high_cols(us, name, gain):
                for k in range(KD):
                    o = filled(us[name, k])
                    act.activation(r32(hT[:, k, :]), o[:, :], ACT.Copy, scale=gain[:, k:k + 1])\
                       .then_inc(sem("high_ready"), 1)

            for t in range(NT):
                act.wait_ge(sem(f"x_loaded{t}"), 16)
                sums(x_rows, t, t, xn[:, t, :])
            roots(1, 0, NT)
            act.wait_ge(sem("consts_loaded"), 80)
            high_cols(U, "x_t", g_mix)
            high_parts("dq")

            act.wait_ge(sem("gate_abs_ready"), 1)
            act.activation(g_ex, g_l, ACT.Exp).then_inc(act_step, 1)
            act.wait_ge(act_step, 1)
            act.activation(g_l, g_ex, ACT.Ln, bias=1.0).then_inc(sem("gate_log_ready"), 1)
            act.wait_ge(sem("lam_sum_ready"), 1)
            act.activation(lam_s[:, 2:4], lam_s[:, 0:2], ACT.Exp).then_inc(sem("lam_exp_ready"), 1)

            high_parts("dk")
            for j in range(2 * HEADS):
                if j == 4:
                    high_parts("dv")
                o = filled(U["qk", j])
                act.activation(qkT[:, j, :], o[:, :], ACT.Copy).then_inc(done, 1)
            high_parts("mq")
            for t in range(NT):
                o = filled(U["dv", t])
                act.activation(dv_rows[:, t, :], o[:, :], ACT.Copy).then_inc(done, 1)
            act.wait_ge(sem("qk_rotated"), 2 * HEADS)
            for i in range(16 + 2):
                if i < 16 and i % 4 == 0:
                    high_parts(("mk", "mv", "mo", "wo0")[i // 4])
                if i < 16:
                    h, qb = divmod(i, NT)
                    n = P * (qb + 1)
                    act.wait_ge(sem("da_max_ready"), i + 1)
                    if i >= 2:
                        act.wait_ge(bank_filled, U["da_t", i - 2].filled)
                    for m in range(2):
                        c = 2 * (i % 2) + m
                        o = filled(U["ds", i, m])
                        act.activation(e_buf[:, i % 2, m, 0:n], o[:, 0:n], ACT.Exp, bias=neg[:, c:c + 1],
                                       scale=DA_DIM ** -0.5, accum_out=zsum[:, c:c + 1]).then_inc(done, 1)
                    if i < 8:
                        o = filled(U["proj", i])
                        act.activation(mqkT[:, i, :], o[:, :], ACT.Copy).then_inc(done, 1)
                    elif i >= 12:
                        o = filled(U["proj", i])
                        act.activation(moT[:, i - 12, :], o[:, :], ACT.Copy).then_inc(done, 1)
                if i >= 2:
                    j = i - 2
                    h, qb = divmod(j, NT)
                    o = filled(U["do", j])
                    act.activation(o_rows[:, qb, h, :], o[:, 0:P], ACT.Copy).then_inc(act_step, 1)
                    act.wait_ge(act_step, 2 + j)
                    act.activation(o[:, 0:P], o[:, 0:P], ACT.Square, accum_out=ss[:, 32 + j:33 + j]).then_inc(done, 1)
                if i == 11:
                    act.wait_ge(sem("conv_done"), 8)
                    for m in range(8):
                        act.activation(mqkT[:, m, :], mqkT[:, m, :], ACT.Silu).then_inc(sem("silu_ready"), 1)

            high_parts("wo1")
            roots(2, 32, 48)
            wait_emptied(act, U["gates_t",])
            act.activation(em, mT, ACT.Exp, scale=-1.0).then_inc(sem("em_ready"), 1)
            for h in range(HEADS):
                o = filled(U["m_row", h])
                act.wait_ge(sem("diag_ready"), h + 1)
                for kb in range(NT):
                    n = NT * h + kb
                    if n >= 2:
                        wait_emptied(act, U[("ms",) + divmod(n - 2, NT)])
                    bias = bT[:, 4 * kb + h:4 * kb + h + 1]
                    if kb < NT - 1:
                        rest = act.activation(d_buf[:, n % 2, P:SEQ - P * kb], o[:, P * kb + P:SEQ], ACT.Exp, bias=bias)
                        if kb == NT - 2:
                            rest.then_inc(done, 1)
                    act.activation(d_buf[:, n % 2, 0:P], arg_diag[:, h % 2, P * kb:P * kb + P], ACT.Exp,
                                   bias=bias).then_inc(sem("d_ready"), 1)
            wait_emptied(act, U["proj", 15])
            for m in range(HEADS):
                act.activation(moT[:, m, :], moT[:, m, :], ACT.Sigmoid).then_inc(sem("sig_ready"), 1)
            roots(3, 48, 64)

            act.wait_ge(sem("mem_loaded"), 16)
            for t in range(MT):
                sums(mem_rows, t, NT + t)
            for m in range(8):
                if m < 4:
                    o = filled(U["y_t", m])
                    act.activation(r32(yT[:, m, :]), o[:, :], ACT.Copy, scale=g_sub_s)\
                       .then_inc(sem("high_ready"), 1)
                else:
                    wait_emptied(act, U["y_t", m])
                    act.activation(r32(yT[:, m, :]), lowT[:, m, :], ACT.Copy).then_inc(sem("high_ready"), 1)
            roots(4, NT, NT + MT)
            high_parts("xk0")
            for t in range(NT):
                wait_emptied(act, U["wo", 1, t])
                sums(x_rows, t, 8 + t)
            act.wait_ge(sem("more_loaded"), 16 * 8)
            for k in range(KD // 2):
                o = filled(U["mem_t", k])
                for kk in range(2):
                    last = act.activation(r32(memT[:, 2 * k + kk, :]), o[:, MEM * kk:MEM * kk + MEM], ACT.Copy,
                                          scale=g_mem[:, 2 * k + kk:2 * k + kk + 1])
                last.then_inc(sem("high_ready"), 1)
            roots(5, 8, 8 + NT)
            high_parts("xk1")
            for m in range(8):
                if m == 4:
                    high_parts("xv0")
                o = filled(U["xk", m])
                act.activation(xkT[:, m, :], o[:, 0:MEM], ACT.Copy).then_inc(done, 1)
            high_cols(U, "x1_t", g_x)
            high_parts("xv1")
            for n in range(2):
                if n == 1:
                    high_parts("xq0")
                for t in range(MT):
                    o = filled(U["xv", n, t])
                    act.activation(xv_rows[:, t, 512 * n:512 * n + 512], o[:, :], ACT.Copy).then_inc(done, 1)
            high_parts("xq1")
            for m in range(8):
                if m == 4:
                    high_parts("xw0")
                o = filled(U["xq", m])
                act.activation(xqT[:, m, :], o[:, :], ACT.Copy).then_inc(done, 1)
            high_parts("xw1")
            for i in range(16 + 2):
                if i < 16:
                    o = filled(U["xs", i])
                    act.wait_ge(sem("xmax_ready"), i + 1)
                    if i >= 4:
                        act.wait_ge(bank_filled, U["xp", i - 4].filled)
                    c = i % 8
                    act.activation(xe[:, i % 4, :], o[:, 0:MEM], ACT.Exp, bias=neg[:, c:c + 1], scale=1.0 / 16,
                                   accum_out=zsum[:, c:c + 1]).then_inc(done, 1)
                if i >= 2 and (i - 2) % NT == NT - 1:
                    for d in range(2):
                        o = filled(U["xo", (i - 2) // NT, d])
                        act.activation(r32(yT[:, 2 * ((i - 2) // NT) + d, :]), o[:, :], ACT.Copy)\
                           .then_inc(sem("high_ready"), 1)
            for t in range(NT):
                wait_emptied(act, U["xw", 1, t])
                sums(x_rows, t, 12 + t)
            roots(6, 12, 12 + NT)
            for k in range(0, KD, 2):
                o = filled(U["x2_t", k])
                act.activation(hT[:, k, :], o[:, :], ACT.Copy, scale=g_ffn[:, k:k + 1]).then_inc(done, 1)
            act.wait_ge(sem("dif_ready"), 1)
            act.activation(pexp[:, :, 0:GROUPS + 1], dif[:, :, 0:GROUPS + 1], ACT.Exp).then_inc(sem("pexp_ready"), 1)

            h_done, g_turned = sem("h_done"), sem("g_turned")

            def silu(b):
                return act.activation(sil[b][SLOTS:P, :], bank[2 + b][0:SLOTS, :], ACT.Silu)

            def gated_cols(b):
                return act.activation(gT[b], bank[4 + b][:, 0:4 * SLOTS].rearrange("p (k s) -> p k s", k=4), ACT.Copy)

            def pair(i, first=False):
                for b in range(2):
                    e = 2 * i + b
                    act.wait_ge(h_done, e + 1)
                    if not first:
                        act.wait_ge(sem("g_ready"), e - 1)
                    silu(b).then_inc(sem("silu_e_ready"), 1)
                    act.wait_ge(g_turned, e + 1)
                    if not first:
                        act.wait_ge(sem("y_done"), e - 1)
                    gated_cols(b).then_inc(sem("gT_ready"), 1)

            pair(0, True)
            with act.Fori(1, EXPERTS // 2) as i:
                pair(i)
            act.wait_ge(sem("y_done"), EXPERTS)
            wait_emptied(act, U["table",])
            n = act.value_load(over_n, min_val=0, max_val=OVER)
            with act.If(n > 0):
                with act.Fori(0, OVER) as k:
                    act.wait_ge(sem("ov_h_done"), k + 1)
                    silu(0).then_inc(sem("ov_silu_ready"), 1)
                    act.wait_ge(sem("ov_g_turned"), k + 1)
                    gated_cols(0).then_inc(sem("ov_gT_ready"), 1)
                    act.wait_ge(sem("ov_stored"), 16 * k + 16)

            high_parts("c0", "u0")
            for t in range(NT + 1):
                if t < NT:
                    act.wait_ge(sem("x3_ready"), t + 1)
                    sums(x_rows, t, 16 + t)
                if t >= 1:
                    act.wait_ge(sem("x3g_ready"), t)
                    sums(x_rows, t - 1, 20 + t - 1)
            roots(7, 16, 16 + 2 * NT)
            for t in range(NT):
                act.wait_ge(sem("x4n_ready"), t + 1)
                act.activation(x_rows[:, t, :], x_rows[:, t, :], ACT.Copy, scale=rstd[:, 16 + t:17 + t])\
                   .then_inc(sem("x4_ready"), 1)
            high_cols(V, "x4_t", g_a)
            for n in range(2):
                js = range(4 * n, 4 * n + 4)
                for j in js:
                    o = filled(V["c", j])
                    if n:
                        wait_emptied(act, V["u", j - 4])
                    act.activation(cbuf[:, j % 4, :], o[:, :], ACT.Copy).then_inc(done, 1)
                high_parts(f"z{n}", f"b{n}")
                for j in js:
                    o = filled(V["z", j])
                    if n:
                        wait_emptied(act, V["b", j - 4])
                    act.activation(zbuf[:, j % 4, :], o[:, :], ACT.Silu).then_inc(done, 1)
                high_parts(("c1", "wa0")[n])
                for j in js:
                    wait_emptied(act, V["b", j])
                    act.activation(r32(yT[:, j, :]), y2_lo[:, j, :], ACT.Copy).then_inc(sem("high_ready"), 1)
                high_parts(("u1", "wa1")[n])
            high_parts("kv")
            for t in range(NT):
                wait_emptied(act, V["wa", 1, t])
                sums(x_rows, t, 24 + t)
            roots(8, 24, 24 + NT)
            high_parts("q0")
            for k in range(KD):
                o = filled(V["x5_t", k])
                for dst, g in ((hkvT, g_kv), (hT, g_b)):
                    last = act.activation(r32(dst[:, k, :]), o[:, :], ACT.Copy, scale=g[:, k:k + 1])
                last.then_inc(sem("high_ready"), 1)
            for t in range(NT):
                o = filled(V["kv", t])
                act.activation(k_rows[:, WKV * t:WKV * t + WKV, :], o[:, 0:256].rearrange("p (g d) -> p g d", g=WKV),
                               ACT.Copy)
                act.activation(v_rows2[:, t, :], o[:, 256:512], ACT.Copy)
                act.activation(sq_buf[:, t, 0:256], o[:, 0:256], ACT.Square).then_inc(done, 1)
            for n in range(2):
                high_parts(("q1", "zz0")[n])
                for t in range(NT):
                    o = filled(V["q", n, t])
                    act.wait_ge(sem("sq_used"), NT * n + t + 1)
                    act.activation(q_rows[:, t, 512 * n:512 * n + 512], o[:, :], ACT.Copy)
                    act.activation(sq_buf[:, t, :], o[:, :], ACT.Square).then_inc(done, 1)
            high_parts("zz1")
            roots(9, 0, 80)
            for m in range(8):
                if m == 4:
                    high_parts("wb0")
                o = filled(V["zz", m])
                act.activation(zT[:, m, :], o[:, :], ACT.Silu).then_inc(done, 1)
            high_parts("wb1")
            for p in range(8):
                o = filled(V["q_t", p])
                act.activation(q2T[:, p, :], o[:, :], ACT.Copy).then_inc(done, 1)
            def high_of(j):
                nb, g = divmod(j, WKV)
                wait_emptied(act, V["wv", j])
                v = lambda t: t[:, 2 * g:2 * g + 2, P * nb:P * nb + P]
                act.activation(r32(v(yT2)), v(lowT), ACT.Copy).then_inc(sem("high_ready"), 1)

            for i in range(16 + 4):
                if i < 16:
                    n = 2 * P if i // WKV else P
                    act.wait_ge(sem("w_max_ready"), i + 1)
                    for q in range(4):
                        c = 8 * (i % 2) + q
                        act.activation(wS[:, i % 3, q, 0:n], wS[:, i % 3, q, 0:n], ACT.Exp, bias=neg[:, c:c + 1],
                                       accum_out=zsum[:, c:c + 1])
                    c = 4 * (i % 2)
                    act.activation(stat[:, 16 + c:20 + c], stat[:, c:c + 4], ACT.Exp).then_inc(sem("w_exp_ready"), 1)
                if 2 <= i < 18:
                    j = i - 2
                    if j >= 2:
                        act.wait_ge(bank_filled, V["wv", j - 2].filled)
                    for kt in window_tiles(j):
                        o = filled(V["wp", j, kt])
                        act.activation(wpT[:, j % 2, kt, :], o[:, :], ACT.Copy).then_inc(done, 1)
                if i >= 4:
                    high_of(i - 4)

        @block.vector
        def _(dve):
            done = emptied["dve"]

            def filled(u):
                dve.wait_ge(bank_filled, u.filled)
                return bank[u.bank]

            def own(ins):
                then_own(dve, ins, dve_step, dve_n)

            ss_total, ms_total = [0], [0]

            def rstds(n_sums, spans):
                ss_total[0] += n_sums
                ms_total[0] += 1
                if n_sums:
                    dve.wait_ge(sem("ss_ready"), ss_total[0])
                for c0, c1, width in spans:
                    last = dve.tensor_scalar(ms[:, c0:c1], ss[:, c0:c1], 1.0 / width, EPS, ALU.mult, ALU.add)
                last.then_inc(sem("ms_ready"), 1)
                dve.wait_ge(sem("root_ready"), ms_total[0])
                own(dve.reciprocal(rstd[:, spans[0][0]:spans[-1][1]], root[:, spans[0][0]:spans[-1][1]]))

            def normalise(c0, ready):
                for t in range(NT):
                    dve.tensor_scalar(xn[:, t, :], x_rows[:, t, :], rstd[:, c0 + t:c0 + t + 1], None, ALU.mult)\
                       .then_inc(ready, 1)

            highs = [0]

            def wait_high():
                highs[0] += 1
                dve.wait_ge(sem("high_ready"), highs[0])

            def low_cols(us, name, gain):
                for k in range(KD):
                    o = filled(us[name, k])
                    wait_high()
                    dve.scalar_tensor_tensor(r32(lowT[:, k, :]), o[:, :], gain[:, k:k + 1], r32_read(hT[:, k, :]),
                                             ALU.mult, ALU.subtract).then_inc(done, 1)

            rstds(NT, [(0, NT, D)])
            normalise(0, sem("x0n_ready"))
            dve.wait_ge(sem("consts_loaded"), 80)
            for s in range(2):
                own(dve.tensor_scalar(r32(w_gates_split[s]), ident[:, 0:GATE_M].unsqueeze(1).to_broadcast([P, KD, GATE_M]),
                                      0.0, None, ALU.mult))
            for g in range(2):
                src, at = w_gates[:, :, 4 * g:4 * g + 4], slice(32 * g, 32 * g + 4)
                own(dve.tensor_copy(r32(w_gates_split[0][:, :, at]), src))
                last = dve.tensor_tensor(r32(w_gates_split[1][:, :, at]), src, r32_read(w_gates_split[0][:, :, at]), ALU.subtract)
            last.then_inc(sem("w_gates_ready"), 1)
            low_cols(U, "x_t", g_mix)

            o = filled(U["gate",])
            for g, dst in enumerate((g_i, g_f)):
                rows = slice(32 * g, 32 * g + HEADS)
                last = dve.tensor_scalar(dst, o[rows, :], gate_b[rows, g:g + 1], None, ALU.add)
            last.then_inc(done, 1)
            wait_emptied(dve, U["gate",])
            dve.tensor_scalar(g_min, g_f, 0.0, None, ALU.min)
            dve.scalar_tensor_tensor(g_l, g_f, -1.0, g_f, ALU.mult, ALU.min).then_inc(sem("gate_abs_ready"), 1)
            dve.wait_ge(sem("more_loaded2"), 16 * N_MORE)
            for m in range(2):
                last = dve.tensor_tensor_reduce(rw[:, 64 * m:64 * m + 64], lam_in[:, P * m:P * m + DA_DIM],
                                                lam_in[:, P * m + DA_DIM:P * m + P], 1.0, 0.0, ALU.mult, ALU.add,
                                                lam_s[:, m:m + 1])
            last.then_inc(sem("lam_sum_ready"), 1)
            dve.tensor_scalar(g_sub_s, g_sub, 1.0 - LAM_INIT, None, ALU.mult)
            dve.wait_ge(sem("gate_log_ready"), 1)
            own(dve.tensor_tensor(g_f, g_min, g_l, ALU.subtract))
            own(dve.memset(g_min, 0.0))
            own(dve.tensor_tensor_scan(g_a_sum, g_f, g_min, 0.0, ALU.add, ALU.add))
            own(dve.tensor_tensor(g_bb, g_i, g_a_sum, ALU.subtract))
            own(dve.tensor_tensor_scan(g_M, g_min, g_bb, 0.0, ALU.add, ALU.max))
            dve.tensor_tensor(g_ex, g_M, g_a_sum, ALU.add).then_inc(sem("gates_ready"), 1)
            dve.wait_ge(sem("lam_exp_ready"), 1)
            own(dve.tensor_tensor(neg_lam, lam_s[:, 3:4], lam_s[:, 2:3], ALU.subtract))
            own(dve.tensor_scalar(neg_lam, neg_lam, -LAM_INIT, None, ALU.add))

            for j in range(2 * HEADS):
                o = filled(U["qk_rot", j])
                dve.tensor_tensor(rope_tmp, o[:, :], sinT, ALU.mult).then_inc(done, 1)
                own(dve.tensor_tensor(qkT[:, j, :], qkT[:, j, :], cosT, ALU.mult))
                dve.tensor_tensor(qkT[:, j, :], qkT[:, j, :], rope_tmp, ALU.add).then_inc(sem("qk_rotated"), 1)
                dve.wait_ge(sem("qk_rotated"), j + 1)

            def conv(j):
                wait_emptied(dve, U["proj", j])
                w = lambda tap: conv_w[:, KD * tap + j:KD * tap + j + 1]
                acc = conv_tmp[:, j % 2, :]
                own(dve.tensor_scalar(acc, convT[:, j, 0:SEQ], w(0), conv_b[:, j:j + 1], ALU.mult, ALU.add))
                for tap in range(1, CONV1 - 1):
                    own(dve.scalar_tensor_tensor(acc, convT[:, j, tap:tap + SEQ], w(tap), acc, ALU.mult, ALU.add))
                dve.scalar_tensor_tensor(mqkT[:, j, :], mqkT[:, j, :], w(CONV1 - 1), acc, ALU.mult, ALU.add)\
                   .then_inc(sem("conv_done"), 1)

            dve.wait_ge(sem("pads_zero"), 2)
            for i in range(16 + 2):
                if i < 16:
                    h, qb = divmod(i, NT)
                    n = P * (qb + 1)
                    c = 2 * (i % 2)
                    for m in range(2):
                        o = filled(U["ds", i, m])
                        last = dve.tensor_tensor(o[:, n - P:n], o[:, n - P:n], const("mask_qk"), ALU.add)
                    own(last)
                    for m in range(2):
                        last = dve.tensor_reduce(mx[:, c + m:c + m + 1], bank[U["ds", i, m].bank][:, 0:n], AX.X, ALU.max)
                    own(last)
                    dve.tensor_scalar(neg[:, c:c + 2], mx[:, c:c + 2], -(DA_DIM ** -0.5), None, ALU.mult)\
                       .then_inc(sem("da_max_ready"), 1)
                    if 8 <= i < 12:
                        o = filled(U["proj", i])
                        dve.tensor_copy(mv_rows[:, i - 8, :, 0:P], o[:, :].rearrange("p (h d) -> p h d", h=HEADS))\
                           .then_inc(done, 1)
                if 1 <= i <= 16:
                    j = i - 1
                    h, qb = divmod(j, NT)
                    n, c = P * (qb + 1), 2 * (j % 2)
                    wait_emptied(dve, U["ds", j, 1])
                    own(dve.reciprocal(rz[:, c:c + 2], zsum[:, c:c + 2]))
                    own(dve.tensor_tensor(rz[:, c + 1:c + 2], rz[:, c + 1:c + 2], neg_lam, ALU.mult))
                    e0, e1 = e_buf[:, j % 2, 0, 0:n], e_buf[:, j % 2, 1, 0:n]
                    own(dve.tensor_scalar(e0, e0, rz[:, c:c + 1], None, ALU.mult))
                    dve.scalar_tensor_tensor(e0, e1, rz[:, c + 1:c + 2], e0, ALU.mult, ALU.add)\
                       .then_inc(sem("da_ready"), 1)
                    if j < 8:
                        conv(j)
                    o = filled(U["da_t", j])
                    if j >= 2:
                        dve.wait_ge(bank_filled, U["do", j - 2].filled)
                    dve.tensor_copy(daT[:, j % 2, 0:qb + 1, :], o[:, 0:n].rearrange("p (k q) -> p k q", q=P))\
                       .then_inc(done, 1)

            wait_emptied(dve, U["do", 15])
            rstds(0, [(32, 48, P)])
            for m in range(4):
                v = o_rows[:, :, m, :]
                r = rstd[:, 32 + 4 * m:36 + 4 * m].unsqueeze(2).to_broadcast([P, NT, P])
                dve.tensor_tensor(v, v, r, ALU.mult).then_inc(sem("y_rows_ready"), 1)

            o = filled(U["gates_t",])
            dve.tensor_copy(bmT, o[:, 0:32]).then_inc(done, 1)
            dve.wait_ge(sem("em_ready"), 1)
            mv, bn = stat[:, 0:32], stat[:, 32:56]
            den, size, recip = (stat[:, 56 + NT * n:56 + NT * (n + 1)] for n in range(3))

            def weighted_scores(h):
                o = filled(U["m_row", h])
                dve.tensor_tensor(arg_diag[:, h % 2, :].rearrange("p (k q) -> p k q", k=NT),
                                  o[:, :].rearrange("p (k q) -> p k q", k=NT),
                                  const("mask_kq").unsqueeze(1).to_broadcast([P, NT, P]), ALU.add)\
                   .then_inc(sem("diag_ready"), 1)
                for kb in range(NT):
                    o = filled(U["ms", h, kb])
                    dve.wait_ge(sem("d_ready"), NT * h + kb + 1)
                    n = SEQ - P * kb
                    dve.scalar_tensor_tensor(sdT[:, h % 2, kb, P * kb:SEQ], o[:, P * kb:SEQ], float(P) ** -0.5,
                                             d_buf[:, (NT * h + kb) % 2, 0:n], ALU.mult, ALU.mult).then_inc(done, 1)

            def head_rows(h):
                for qb in range(NT):
                    o = filled(U["mh", h, qb])
                    last = dve.tensor_copy(den[:, qb:qb + 1], o[:, P:P + 1])
                own(last)
                own(dve.scalar_tensor_tensor(size, den, -1.0, den, ALU.mult, ALU.max))
                own(dve.tensor_tensor(size, size, em[:, h:4 * NT:4], ALU.max))
                own(dve.reciprocal(recip, size))
                for qb in range(NT):
                    dve.tensor_scalar(hm_rows[:, qb, h, :], bank[U["mh", h, qb].bank][:, 0:P], recip[:, qb:qb + 1], None,
                                      ALU.mult).then_inc(done, 1)
                for qb in range(NT):
                    wait_emptied(dve, U["mh", h, qb])
                    last = dve.bn_stats(bn[:, 6 * qb:6 * qb + 6], hm_rows[:, qb, h, :])
                own(last)
                for qb in range(NT):
                    c = NT * h + qb
                    last = dve.bn_aggr(mv[:, 2 * c:2 * c + 2], bn[:, 6 * qb:6 * qb + 6])
                own(last)

            for h in range(HEADS + 1):
                if h < HEADS:
                    weighted_scores(h)
                if h >= 1:
                    head_rows(h - 1)

            own(dve.tensor_scalar(ss[:, 48:64], mv[:, 1:32:2], float(P), None, ALU.mult))
            rstds(0, [(48, 64, P)])
            for h in range(HEADS):
                for t in range(NT):
                    c = NT * h + t
                    last = dve.tensor_scalar(hm_rows[:, t, h, :], hm_rows[:, t, h, :], mv[:, 2 * c:2 * c + 1],
                                             rstd[:, 48 + c:49 + c], ALU.subtract, ALU.mult)
                last.then_inc(sem("y_rows_ready"), 1)
            for m in range(8):
                o = filled(U["y_t", m])
                if m < 4:
                    wait_high()
                    own(dve.scalar_tensor_tensor(r32(lowT[:, m, :]), o[:, :], g_sub_s, r32_read(yT[:, m, :]), ALU.mult,
                                                 ALU.subtract))
                    dve.nop().then_inc(done, 1)
                    dve.nop().then_inc(sem("y_low_ready"), 1)
                else:
                    dve.wait_ge(sem("sig_ready"), m - 3)
                    dve.scalar_tensor_tensor(lowT[:, m, :], o[:, :], g_ml[:, m - 4:m - 3], moT[:, m - 4, :],
                                             ALU.mult, ALU.mult).then_inc(done, 1)
            for m in range(4, 8):
                wait_high()
                dve.tensor_tensor(r32(lowT[:, m, :]), lowT[:, m, :], r32_read(yT[:, m, :]), ALU.subtract)\
                   .then_inc(sem("y_low_ready"), 1)

            rstds(MT, [(NT, NT + MT, D)])
            for t in range(MT):
                dve.tensor_scalar(mem_rows[:, t, :], mem_rows[:, t, :], rstd[:, NT + t:NT + t + 1], None, ALU.mult)\
                   .then_inc(sem("memn_ready"), 1)

            def add_rows(us, name):
                for n in range(2):
                    for t in range(NT):
                        o = filled(us[name, n, t])
                        v = x_rows[:, t, 512 * n:512 * n + 512]
                        dve.tensor_tensor(v, o[:, :], v, ALU.add).then_inc(done, 1)

            dve.wait_ge(sem("x_again"), 16 * NT)
            add_rows(U, "wo")
            dve.wait_ge(sem("more_loaded"), 16 * 8)
            for k in range(KD // 2):
                o = filled(U["mem_t", k])
                wait_high()
                for kk in range(2):
                    j = 2 * k + kk
                    last = dve.scalar_tensor_tensor(r32(mem_lo[:, j, :]), o[:, MEM * kk:MEM * kk + MEM], g_mem[:, j:j + 1],
                                                    r32_read(memT[:, j, :]), ALU.mult, ALU.subtract)
                last.then_inc(done, 1)
            rstds(NT, [(8, 8 + NT, D)])
            normalise(8, sem("x1n_ready"))
            low_cols(U, "x1_t", g_x)

            for i in range(16 + 2):
                if i < 16:
                    o = filled(U["xs", i])
                    c = i % 8
                    own(dve.tensor_reduce(mx[:, c:c + 1], o[:, 0:MEM], AX.X, ALU.max))
                    dve.tensor_scalar(neg[:, c:c + 1], mx[:, c:c + 1], -1.0 / 16, None, ALU.mult)\
                       .then_inc(sem("xmax_ready"), 1)
                if 1 <= i <= 16:
                    j = i - 1
                    c = j % 8
                    wait_emptied(dve, U["xs", j])
                    own(dve.reciprocal(rz[:, c:c + 1], zsum[:, c:c + 1]))
                    dve.tensor_scalar(xe[:, j % 4, :], xe[:, j % 4, :], rz[:, c:c + 1], None, ALU.mult)\
                       .then_inc(sem("xp_ready"), 1)
                if i >= 2:
                    j = i - 2
                    h, t = divmod(j, NT)
                    o = filled(U["xp", j])
                    if h >= 2 and t == 0:
                        dve.wait_ge(bank_filled, U["xo", h - 2, 1].filled)
                    dve.tensor_copy(pT[:, h % 2, :, P * t:P * t + P], o[:, 0:MEM].rearrange("p (k q) -> p k q", q=P))\
                       .then_inc(done, 1)
                    if t == NT - 1:
                        for d in range(2):
                            o = filled(U["xo", h, d])
                            wait_high()
                            dve.tensor_tensor(r32(lowT[:, 2 * h + d, :]), o[:, :], r32_read(yT[:, 2 * h + d, :]),
                                              ALU.subtract)\
                               .then_inc(done, 1)
            add_rows(U, "xw")
            rstds(NT, [(12, 12 + NT, D)])
            normalise(12, sem("x2n_ready"))
            for k in range(1, KD, 2):
                o = filled(U["x2_t", k])
                dve.tensor_scalar(hT[:, k, :], o[:, :], g_ffn[:, k:k + 1], None, ALU.mult).then_inc(done, 1)

            for t in range(NT):
                o = filled(U["route", t])
                dve.tensor_tensor(lg[:, t, :], o[:, 0:GROUPS + EXPERTS], router_b, ALU.add).then_inc(done, 1)
            wait_emptied(dve, U["route", NT - 1])

            def over(v, n):
                return v.unsqueeze(2).to_broadcast([P, NT, n])

            def columns(n):
                return const("item_row")[:, 0:n].unsqueeze(1).to_broadcast([P, NT, n])

            def first_max(vals, n, most, index, tmp):
                own(dve.tensor_reduce(most, vals, AX.X, ALU.max))
                own(dve.tensor_tensor(tmp, vals, over(most, n), ALU.is_lt))
                own(dve.scalar_tensor_tensor(tmp, tmp, float(SLOTS), columns(n), ALU.mult, ALU.add))
                own(dve.tensor_reduce(index, tmp, AX.X, ALU.min))

            groups, experts = lg[:, :, 0:GROUPS], lg[:, :, GROUPS:].rearrange("p t (g e) -> p t g e", g=GROUPS)
            first, second = ea[:, 0:NT], ea[:, NT:2 * NT]
            first_max(groups, GROUPS, most_g, chosen_g, tmp_g)
            own(dve.tensor_tensor(tmp_g, columns(GROUPS), over(chosen_g, GROUPS), ALU.is_equal))
            own(dve.tensor_tensor(of_group, experts, tmp_g.unsqueeze(3).to_broadcast([P, NT, GROUPS, PER_GROUP]), ALU.mult))
            own(dve.tensor_reduce(el, of_group.rearrange("p t g e -> p t e g"), AX.X, ALU.add))
            first_max(el, PER_GROUP, most_1, first, tmp_e)
            own(dve.tensor_tensor(tmp_e, columns(PER_GROUP), over(first, PER_GROUP), ALU.is_equal))
            own(dve.scalar_tensor_tensor(el, tmp_e, NEG, el, ALU.mult, ALU.add))
            first_max(el, PER_GROUP, most_2, second, tmp_e)
            for v in (first, second):
                last = dve.scalar_tensor_tensor(v, chosen_g, float(PER_GROUP), v, ALU.mult, ALU.add)
            own(last)
            own(dve.tensor_tensor(sel8, const("item_row")[:, 0:EXPERTS].unsqueeze(1).to_broadcast([P, 2 * NT, EXPERTS]),
                                  ea.unsqueeze(2).to_broadcast([P, 2 * NT, EXPERTS]), ALU.is_equal))
            dve.tensor_tensor(selb, sel1h[:, 0], sel1h[:, 1], ALU.add).then_inc(sem("chosen_ready"), 1)
            dve.tensor_tensor(dif[:, :, 0:GROUPS], groups, over(most_g, GROUPS), ALU.subtract)
            dve.tensor_tensor(dif[:, :, GROUPS], most_2, most_1, ALU.subtract).then_inc(sem("dif_ready"), 1)
            dve.wait_ge(sem("pexp_ready"), 1)
            own(dve.tensor_reduce(zg, pexp[:, :, 0:GROUPS], AX.X, ALU.add))
            own(dve.scalar_tensor_tensor(r4b, pexp[:, :, GROUPS], 1.0, zg, ALU.add, ALU.mult))
            own(dve.reciprocal(comb[:, 0:NT], r4b))
            own(dve.tensor_tensor(comb[:, NT:2 * NT], pexp[:, :, GROUPS], comb[:, 0:NT], ALU.mult))
            for c in range(2):
                last = dve.tensor_scalar(toks[:, NT * c:NT * c + NT], const("tok_col"), SEQ * c - NOWHERE, None, ALU.add)
            own(last)
            for c in range(2):
                last = dve.tensor_scalar(tokg[:, NT * c:NT * c + NT], const("tok_col"), -NOWHERE, None, ALU.add)
            own(last)
            own(dve.tensor_scalar(half5[:, 0:1], const("half_col"), 0.5, None, ALU.mult))
            for t in range(NT):
                o = filled(U["rank", t])
                dve.tensor_tensor(of_choice[:, :, t, :], o[:, 0:EXPERTS].unsqueeze(1).to_broadcast([P, 2, EXPERTS]),
                                  sel1h[:, :, t, :], ALU.mult).then_inc(done, 1)
            wait_emptied(dve, U["rank", NT - 1])
            own(dve.tensor_reduce(rk, of_choice8, AX.X, ALU.add))
            o = filled(U["count",])
            dve.tensor_copy(cnt, o[:, 0:EXPERTS]).then_inc(done, 1)
            wait_emptied(dve, U["count",])
            own(dve.memset(zero32, 0.0))
            own(dve.tensor_scalar(nov, cnt, float(SLOTS), None, ALU.is_gt))
            for j in range(2, TILES):
                own(dve.scalar_tensor_tensor(nov, cnt, float(SLOTS * j), nov, ALU.is_gt, ALU.add))
            own(dve.tensor_tensor_scan(ovend, nov, zero32, 0.0, ALU.add, ALU.add))
            own(dve.tensor_tensor(ovbase, ovend, nov, ALU.subtract))
            own(dve.tensor_tensor(of_choice8, ovbase.unsqueeze(1).to_broadcast([P, 2 * NT, EXPERTS]), sel8, ALU.mult))
            own(dve.tensor_reduce(ovb, of_choice8, AX.X, ALU.add))
            jt = slot
            own(dve.tensor_scalar(jt, rk, float(SLOTS), None, ALU.is_ge))
            for j in range(2, TILES):
                own(dve.scalar_tensor_tensor(jt, rk, float(SLOTS * j), jt, ALU.is_ge, ALU.add))
            own(dve.tensor_tensor(item, jt, ovb, ALU.add))
            own(dve.scalar_tensor_tensor(item, item, EXPERTS - 1.0, ea, ALU.add, ALU.subtract))
            own(dve.tensor_scalar(ovb, jt, 1.0, None, ALU.min))
            own(dve.tensor_tensor(item, item, ovb, ALU.mult))
            own(dve.tensor_tensor(item, item, ea, ALU.add))
            own(dve.scalar_tensor_tensor(slot, jt, -float(SLOTS), rk, ALU.mult, ALU.add))
            def each(v, n):
                return v.unsqueeze(2).to_broadcast([P, 2 * NT, n])

            dve.tensor_tensor(oh_slot, const("slot_row").unsqueeze(1).to_broadcast([P, 2 * NT, P]), each(slot, P),
                              ALU.is_equal)
            own(dve.tensor_tensor(is_item, const("item_row").unsqueeze(1).to_broadcast([P, 2 * NT, ITEMS]),
                                  each(item, ITEMS), ALU.is_equal))
            for n, v in enumerate((tokg, toks, comb)):
                last = dve.tensor_tensor(oh_item[:, :, n, :], is_item, each(v, ITEMS), ALU.mult)
            last.then_inc(sem("onehots_ready"), 1)
            own(dve.tensor_copy(over_n, ovend[0:1, EXPERTS - 1:EXPERTS]))
            own(dve.tensor_tensor(over_cmp.rearrange("p (k e) -> p k e", e=EXPERTS),
                                  const("item_row", 1)[:, 0:OVER + 1].unsqueeze(2).to_broadcast([1, OVER + 1, EXPERTS]),
                                  ovend[0:1, :].unsqueeze(1).to_broadcast([1, OVER + 1, EXPERTS]), ALU.is_ge))
            own(dve.tensor_reduce(over_row, over_cmp.rearrange("p (k e) -> p k e", e=EXPERTS), AX.X, ALU.add))
            own(dve.tensor_scalar(over_e[:, :], over_row, EXPERTS - 1.0, None, ALU.min))
            o = filled(U["table",])
            dve.tensor_scalar(tab_g, o[:, 0:ITEMS], half5[:, 0:1], NOWHERE, ALU.add, ALU.add)
            dve.tensor_scalar(tab_s, o[:, ITEMS:2 * ITEMS], const("half_col"), NOWHERE, ALU.add, ALU.add)
            dve.tensor_copy(tab_w, o[:, 2 * ITEMS:3 * ITEMS]).then_inc(done, 1)
            wait_emptied(dve, U["table",])

            def rows_cols(b):
                g = g_xh.rearrange("p (h k) -> p k h", h=2).unsqueeze(3).to_broadcast([P, 4, 2, SLOTS])
                return dve.tensor_tensor(xgT[b], bank[b][:, :].rearrange("p (k h s) -> p k h s", k=4, h=2), g, ALU.mult)

            def gate_up(b):
                return dve.tensor_tensor(gg[b][0:SLOTS, :], sil[b][SLOTS:P, :], bank[2 + b][SLOTS:P, :], ALU.mult)

            def weigh(b, e):
                return dve.tensor_scalar(y_sb[b], bank[6 + b][:, :], tab_w[:, bass.ds(e, 1)], None, ALU.mult)

            def step_cols(i, b, first=False):
                e = 2 * i + b
                dve.wait_ge(sem("xg_turned"), e + 1)
                if not first:
                    dve.wait_ge(sem("h_done"), e - 1)
                rows_cols(b).then_inc(sem("xgT_ready"), 1)

            def step_gate(i, b, first=False):
                e = 2 * i + b
                dve.wait_ge(sem("silu_e_ready"), e + 1)
                if not first:
                    dve.wait_ge(sem("g_turned"), e - 1)
                gate_up(b).then_inc(sem("g_ready"), 1)

            def step_weigh(i, b, first=False):
                e = 2 * i + b
                dve.wait_ge(sem("y_done"), e + 1)
                if not first:
                    dve.wait_ge(sem(f"y_stored{b}"), 16 * i)
                weigh(b, e).then_inc(sem("y_ready"), 1)

            def pair(i, first, last, second=False):
                step_cols(i, 1, first)
                step_gate(i, 0, first)
                if not first:
                    step_weigh(i - 1, 1, second)
                if not last:
                    step_cols(i + 1, 0)
                step_gate(i, 1, first)
                step_weigh(i, 0, first)

            step_cols(0, 0, True)
            pair(0, True, False)
            pair(1, False, False, True)
            with dve.Fori(2, EXPERTS // 2 - 1) as i:
                pair(i, False, False)
            pair(EXPERTS // 2 - 1, False, True)
            step_weigh(EXPERTS // 2 - 1, 1)
            n = dve.value_load(over_n, min_val=0, max_val=OVER)
            with dve.If(n > 0):
                with dve.Fori(0, OVER) as k:
                    dve.wait_ge(sem("ov_xg_turned"), k + 1)
                    rows_cols(0).then_inc(sem("ov_xgT_ready"), 1)
                    dve.wait_ge(sem("ov_silu_ready"), k + 1)
                    gate_up(0).then_inc(sem("ov_g_ready"), 1)
                    dve.wait_ge(sem("ov_y_done"), k + 1)
                    weigh(0, k + EXPERTS).then_inc(sem("y_ready"), 1)
                    dve.wait_ge(sem("ov_stored"), 16 * k + 16)

            summed = ss_total[0]
            for t in range(NT + 1):
                if t < NT:
                    dve.wait_ge(sem(f"y_back{t}"), 32)
                    own(dve.tensor_tensor(x_rows[:, t, :], x_rows[:, t, :], y_back[t][:, 0, :], ALU.add))
                    dve.tensor_tensor(x_rows[:, t, :], x_rows[:, t, :], y_back[t][:, 1, :], ALU.add)\
                       .then_inc(sem("x3_ready"), 1)
                if t >= 1:
                    dve.wait_ge(sem("g_fin_loaded"), 16)
                    dve.wait_ge(sem("ss_ready"), summed + (1 if t == 1 else 2 * t - 2))
                    dve.wait_ge(sem("x3_ready"), t)
                    dve.tensor_tensor(x_rows[:, t - 1, :], x_rows[:, t - 1, :], g_fin, ALU.mult)\
                       .then_inc(sem("x3g_ready"), 1)
            ss_total[0] += 2 * NT
            ms_total[0] += 1
            dve.wait_ge(sem("ss_ready"), ss_total[0])
            own(dve.tensor_scalar(ms[:, 16:16 + NT], ss[:, 16:16 + NT], 1.0 / D, EPS, ALU.mult, ALU.add))
            own(dve.tensor_scalar(ms[:, 20:20 + NT], ss[:, 20:20 + NT], 1.0 / D, None, ALU.mult))
            dve.scalar_tensor_tensor(ms[:, 20:20 + NT], ms[:, 16:16 + NT], EPS, ms[:, 20:20 + NT], ALU.mult, ALU.add)\
               .then_inc(sem("ms_ready"), 1)
            dve.wait_ge(sem("root_ready"), ms_total[0])
            own(dve.reciprocal(rstd[:, 16:16 + 2 * NT], root[:, 16:16 + 2 * NT]))
            normalise(20, sem("x4n_ready"))
            own(dve.memset(vbuf[:, :, 0:CONV2 - 1], 0.0))
            low_cols(V, "x4_t", g_a)
            for n in range(2):
                js = range(4 * n, 4 * n + 4)
                for j in js:
                    v, acc = vbuf[:, j % 4, :], cacc[:, j % 4, :]
                    w = lambda tap: conv_w2[:, KD * tap + j:KD * tap + j + 1]
                    o = filled(V["u", j])
                    wait_emptied(dve, V["c", j])
                    dve.tensor_tensor(v[:, CONV2 - 1:], o[:, :], cbuf[:, j % 4, :], ALU.mult).then_inc(done, 1)
                    wait_emptied(dve, V["u", j])
                    own(dve.tensor_scalar(acc, v[:, 0:SEQ], w(0), None, ALU.mult))
                    for tap in range(1, CONV2):
                        own(dve.scalar_tensor_tensor(acc, v[:, tap:tap + SEQ], w(tap), acc, ALU.mult, ALU.add))
                for j in js:
                    wait_emptied(dve, V["z", j])
                    own(dve.tensor_tensor(cacc[:, j % 4, :], cacc[:, j % 4, :], zbuf[:, j % 4, :], ALU.mult))
                for j in js:
                    o = filled(V["b", j])
                    dve.tensor_tensor(y2_lo[:, j, :], o[:, :], cacc[:, j % 4, :], ALU.mult).then_inc(done, 1)
                for j in js:
                    wait_high()
                    dve.tensor_tensor(r32(y2_lo[:, j, :]), y2_lo[:, j, :], r32_read(yT[:, j, :]), ALU.subtract)\
                       .then_inc(sem("y2_low_ready"), 1)
            dve.wait_ge(sem("x4_ready"), NT)
            add_rows(V, "wa")
            rstds(NT, [(24, 24 + NT, D)])
            normalise(24, sem("x5n_ready"))
            for k in range(KD):
                o = filled(V["x5_t", k])
                wait_high()
                for hi, lo, g in ((hkvT, hkv_lo, g_kv), (hT, lowT, g_b)):
                    last = dve.scalar_tensor_tensor(r32(lo[:, k, :]), o[:, :], g[:, k:k + 1], r32_read(hi[:, k, :]),
                                                    ALU.mult, ALU.subtract)
                last.then_inc(done, 1)
            for t in range(NT):
                wait_emptied(dve, V["kv", t])
                dve.tensor_reduce(ss[:, WKV * t:WKV * t + WKV], sq_buf[:, t, 0:256].rearrange("p (g d) -> p g d", d=WD),
                                  AX.X, ALU.add).then_inc(sem("sq_used"), 1)
            for n in range(2):
                for t in range(NT):
                    wait_emptied(dve, V["q", n, t])
                    c = 16 + WH * t + 8 * n
                    dve.tensor_reduce(ss[:, c:c + 8], sq_buf[:, t, :].rearrange("p (h d) -> p h d", d=WD), AX.X, ALU.add)\
                       .then_inc(sem("sq_used"), 1)
            dve.wait_ge(sem("sq_used"), 3 * NT)
            rstds(0, [(0, 80, WD)])

            def unit(v, c0, gain, n):
                own(dve.tensor_tensor(v, v, rstd[:, c0:c0 + n].unsqueeze(2).to_broadcast([P, n, WD]), ALU.mult))
                own(dve.tensor_tensor(v, v, gain.unsqueeze(1).to_broadcast([P, n, WD]), ALU.mult))

            def rope(v, n):
                for t in range(NT):
                    hd = v[:, n * t:n * t + n, :]
                    r1, r2 = hd[:, :, 0:ROT // 2], hd[:, :, ROT // 2:ROT]
                    cs = [const(x)[:, 8 * t:8 * t + 8].unsqueeze(1).to_broadcast([P, n, ROT // 2]) for x in ("cos2", "sin2")]
                    tmp = [f3(E, (n, ROT // 2), SEQ * s + 128 * (t % 4)) for s in range(4)]
                    dve.tensor_tensor(tmp[0], r1, cs[0], ALU.mult)
                    dve.tensor_tensor(tmp[1], r2, cs[1], ALU.mult)
                    dve.tensor_tensor(tmp[2], r2, cs[0], ALU.mult)
                    own(dve.tensor_tensor(tmp[3], r1, cs[1], ALU.mult))
                    dve.tensor_tensor(r1, tmp[0], tmp[1], ALU.subtract)
                    own(dve.tensor_tensor(r2, tmp[2], tmp[3], ALU.add))

            unit(k_rows, 0, k_gain, NT * WKV)
            rope(k_rows, WKV)
            dup = f3(B2, (NT * WKV, 2, WD))
            for c in range(2):
                last = dve.tensor_copy(dup[:, :, c, :], k_rows)
            last.then_inc(sem("k2_ready"), 1)
            qh = f3(XN, (NT * WH, WD))
            for t in range(NT):
                unit(qh[:, WH * t:WH * t + WH, :], 16 + WH * t, q_gain, WH)
            rope(qh, WH)
            dve.nop().then_inc(sem("q2_ready"), 1)
            for g in range(WKV):
                o = filled(V["k_t", g])
                dve.tensor_copy(k2T[:, g, :], o[:, :]).then_inc(done, 1)

            def low_of(j):
                nb, g = divmod(j, WKV)
                wait_high()
                v = lambda t: t[:, 2 * g:2 * g + 2, P * nb:P * nb + P]
                dve.tensor_tensor(r32(v(lowT)), v(lowT), r32_read(v(yT2)), ALU.subtract).then_inc(sem("y3_low_ready"), 1)

            for i in range(16 + 4):
                if i < 16:
                    nb, g = divmod(i, WKV)
                    n = 2 * P if nb else P
                    S = wS[:, i % 3, :, 0:n]
                    band = const("band")[:, 2 * P - n:].unsqueeze(1).to_broadcast([P, 2, n])
                    if i >= 3:
                        dve.wait_ge(bank_filled, V["wp", i - 3, 1].filled)
                    for hh in range(2):
                        o = filled(V["ws", i, hh])
                        dve.scalar_tensor_tensor(S[:, 2 * hh:2 * hh + 2, :],
                                                 o[:, :].rearrange("p (r k) -> p r k", r=2)[:, :, 0:n], WD ** -0.5, band,
                                                 ALU.mult, ALU.add).then_inc(done, 1)
                    wait_emptied(dve, V["ws", i, 1])
                    c = 8 * (i % 2)
                    m4, n4 = mx[:, c:c + 4], neg[:, c:c + 4]
                    own(dve.tensor_reduce(m4, S, AX.X, ALU.max))
                    sk = sink[:, 4 * g:4 * g + 4].rearrange("p (r h) -> p h r", h=2)
                    own(dve.tensor_tensor(m4.rearrange("p (h r) -> p h r", h=2), m4.rearrange("p (h r) -> p h r", h=2), sk,
                                          ALU.max))
                    own(dve.tensor_scalar(n4, m4, -1.0, None, ALU.mult))
                    s4 = stat[:, 4 * (i % 2):4 * (i % 2) + 4]
                    dve.tensor_tensor(s4.rearrange("p (h r) -> p h r", h=2), n4.rearrange("p (h r) -> p h r", h=2), sk,
                                      ALU.add).then_inc(sem("w_max_ready"), 1)
                if 1 <= i <= 16:
                    j = i - 1
                    n = 2 * P if j // WKV else P
                    c = 8 * (j % 2)
                    dve.wait_ge(sem("w_exp_ready"), j + 1)
                    own(dve.tensor_tensor(rz[:, c:c + 4], zsum[:, c:c + 4], stat[:, 16 + 4 * (j % 2):20 + 4 * (j % 2)],
                                          ALU.add))
                    own(dve.reciprocal(rz[:, c + 4:c + 8], rz[:, c:c + 4]))
                    S = wS[:, j % 3, :, 0:n]
                    dve.tensor_tensor(S, S, rz[:, c + 4:c + 8].unsqueeze(2).to_broadcast([P, 4, n]), ALU.mult)\
                       .then_inc(sem("wp_ready"), 1)
                if 3 <= i <= 18:
                    j = i - 3
                    nb, g = divmod(j, WKV)
                    o = filled(V["wv", j])
                    wait_emptied(dve, V["zz", 7])
                    dve.tensor_tensor(lowT[:, 2 * g:2 * g + 2, P * nb:P * nb + P],
                                      o[:, 0:256].rearrange("p (r q) -> p r q", r=2),
                                      zT[:, 2 * g:2 * g + 2, P * nb:P * nb + P], ALU.mult).then_inc(done, 1)
                if i >= 4:
                    low_of(i - 4)
            add_rows(V, "wb")


def kernel(**inputs):
    import concourse.bacc as bacc
    from concourse.bass_utils import run_bass_kernel_spmd

    nc = bacc.Bacc("TRN2", target_bir_lowering=False, num_devices=1)
    arrays, a = {}, {}
    given = {name: np.ascontiguousarray(inputs[name]) for name in INS}
    given.update(shape_constants())
    for name, v in given.items():
        arrays[f"in_{name}"] = v
        a[name] = nc.dram_tensor(f"in_{name}", v.shape, mybir.dt.from_np(v.dtype), kind="ExternalInput").ap()
    out = nc.dram_tensor("out_0", (1, SEQ, D), F32, kind="ExternalOutput").ap()
    build(nc, a, out)
    r = run_bass_kernel_spmd(nc, [arrays], core_ids=[0])
    return r.results[0]["out_0"]
```
